# Optimizing a Trainium2 kernel written in Bass

```python
import jax
import jax.numpy as jnp
from jax import lax
import numpy as np

D_MODEL = 1024
BATCH = 1
SEQ = 128
DEPTH = 2
DEC_BATCH = 1
DEC_SEQ = 512
PAST_LEN = 128

GRID_W = 64
N_EVEN = (DEPTH + 1) // 2
N_ODD = DEPTH // 2
EPS = 1e-6
Q_BLOCK = 128
ROPE_BASE = 10000.0

B_HEADS = 8
B_KV_HEADS = 2
B_HEAD_DIM = 64
A_HEADS = 4
A_QK_DIM = 64
A_V_DIM = 128
A_CHUNK = 64
EVEN_IN = B_HEADS * B_HEAD_DIM + 2 * B_KV_HEADS * B_HEAD_DIM + A_HEADS * (2 * A_QK_DIM + 2 * A_V_DIM) + 4 * A_HEADS
EVEN_MIX = B_HEADS * B_HEAD_DIM + A_HEADS * A_V_DIM
C_HEADS = 8
C_Q_LORA = 384
C_KV_LORA = 256
C_NOPE = 64
C_ROPE = 32
C_V = 64
D_RNN = 512
RG_BLOCKS = 8
RG_BW = D_RNN // RG_BLOCKS
RG_C = 8.0
CONV_W = 4
CONV_LEFT = 2
ODD_IN = C_Q_LORA + C_KV_LORA + C_ROPE + 2 * D_RNN
ODD_MIX = C_HEADS * C_V + D_RNN
N_EXPERTS = 16
EXPERT_FF = 512
EC_CAPACITY = 2

kernel_name = 'hybrid_diffusion_prefix_step'

def rms_norm(x, w):
    xf = x.astype(jnp.float32)
    y = xf * lax.rsqrt(jnp.mean(xf * xf, axis=-1, keepdims=True) + EPS)
    return (y * w.astype(jnp.float32)).astype(x.dtype)

def split_cols(a, sizes):
    return jnp.split(a, [int(s) for s in np.cumsum(sizes)[:-1]], axis=-1)

def grid_positions(n_tokens):
    rows = n_tokens // GRID_W
    row = jnp.repeat(jnp.arange(rows, dtype=jnp.float32), GRID_W)
    col = jnp.tile(jnp.arange(GRID_W, dtype=jnp.float32), rows)
    return row, col

def rope_axis(x, pos):
    half = x.shape[-1] // 2
    inv_freq = ROPE_BASE ** (-jnp.arange(half, dtype=jnp.float32) / half)
    ang = pos[:, None] * inv_freq[None, :]
    cos = jnp.cos(ang)[None, :, None, :]
    sin = jnp.sin(ang)[None, :, None, :]
    xf = x.astype(jnp.float32)
    x1, x2 = xf[..., :half], xf[..., half:]
    return jnp.concatenate([x1 * cos - x2 * sin, x1 * sin + x2 * cos], axis=-1).astype(x.dtype)

def rope_2d(x, row, col):
    d = x.shape[-1] // 2
    return jnp.concatenate([rope_axis(x[..., :d], row), rope_axis(x[..., d:], col)], axis=-1)

def attend(q, k, v, scale):
    s = jnp.einsum('bqhgd,bshd->bhgqs', q, k).astype(jnp.float32) * scale
    p = jax.nn.softmax(s, axis=-1).astype(v.dtype)
    return jnp.einsum('bhgqs,bshd->bqhgd', p, v)

def attend_blocked(q, k, v, scale):
    bsz, n_q = q.shape[:2]
    nb = n_q // Q_BLOCK
    qb = jnp.moveaxis(q.reshape((bsz, nb, Q_BLOCK) + q.shape[2:]), 1, 0)
    out = lax.map(lambda qi: attend(qi, k, v, scale), qb)
    return jnp.moveaxis(out, 0, 1).reshape((bsz, n_q) + out.shape[3:])

def mlstm_chunkwise(q, k, v, i_pre, log_f, c0, n0, m0):
    bsz, n_tok, n_heads, _ = q.shape
    nc = n_tok // A_CHUNK

    def to_chunks(a):
        a = a.astype(jnp.float32).reshape((bsz, nc, A_CHUNK) + a.shape[2:])
        return jnp.moveaxis(jnp.moveaxis(a, 1, 0), 3, 2)

    mask = jnp.tril(jnp.ones((A_CHUNK, A_CHUNK), dtype=bool))

    def step(carry, inp):
        cm, nv, m = carry
        qc, kc, vc, ic, fc = inp
        b = jnp.cumsum(fc, axis=-1)
        dmat = jnp.where(mask, b[..., :, None] - b[..., None, :] + ic[..., None, :], -jnp.inf)
        m_inter = b + m[..., None]
        m_t = jnp.maximum(m_inter, dmat.max(axis=-1))
        w_inter = jnp.exp(m_inter - m_t)
        s = jnp.einsum('bhtd,bhsd->bhts', qc, kc) * jnp.exp(dmat - m_t[..., None])
        num = w_inter[..., None] * jnp.einsum('bhtd,bhde->bhte', qc, cm) + jnp.einsum('bhts,bhse->bhte', s, vc)
        den = w_inter * jnp.einsum('bhtd,bhd->bht', qc, nv) + s.sum(axis=-1)
        h = num / jnp.maximum(jnp.abs(den), jnp.exp(-m_t))[..., None]
        b_last = b[..., -1]
        g = b_last[..., None] - b + ic
        m_new = jnp.maximum(b_last + m, g.max(axis=-1))
        decay = jnp.exp(b_last + m - m_new)
        wk = jnp.exp(g - m_new[..., None])
        c_new = decay[..., None, None] * cm + jnp.einsum('bhs,bhsd,bhse->bhde', wk, kc, vc)
        n_new = decay[..., None] * nv + jnp.einsum('bhs,bhsd->bhd', wk, kc)
        return (c_new, n_new, m_new), h

    init = (c0.astype(jnp.float32), n0.astype(jnp.float32), m0.astype(jnp.float32))
    (c_f, n_f, m_f), h = lax.scan(step, init, (to_chunks(q), to_chunks(k), to_chunks(v), to_chunks(i_pre), to_chunks(log_f)))
    h = jnp.moveaxis(jnp.moveaxis(h, 0, 1), 2, 3).reshape(bsz, n_tok, n_heads, -1)
    return h, c_f, n_f, m_f

def mlstm_bidir(q, k, v, gates, c0, n0, m0):
    flip = lambda a: jnp.flip(a, axis=1)
    h_f, cf, nf, mf = mlstm_chunkwise(q, k, v, gates[:, :, 0], jax.nn.log_sigmoid(gates[:, :, 1]), c0[:, 0], n0[:, 0], m0[:, 0])
    h_b, cb, nb, mb = mlstm_chunkwise(flip(q), flip(k), flip(v), flip(gates[:, :, 2]), flip(jax.nn.log_sigmoid(gates[:, :, 3])), c0[:, 1], n0[:, 1], m0[:, 1])
    h = h_f + flip(h_b)
    return h, jnp.stack([cf, cb], axis=1), jnp.stack([nf, nb], axis=1), jnp.stack([mf, mb], axis=1)

def conv_centred(x, w, b):
    y = lax.conv_general_dilated(x, w[:, None, :].astype(x.dtype), window_strides=(1,),
                                 padding=[(CONV_LEFT, CONV_W - 1 - CONV_LEFT)],
                                 dimension_numbers=('NWC', 'WIO', 'NWC'), feature_group_count=x.shape[-1])
    return y + b.astype(x.dtype)

def rglru_scan(x, wa, ba, wx, bx, lam, h0):
    bsz, n_tok, _ = x.shape
    xb = x.reshape(bsz, n_tok, RG_BLOCKS, RG_BW)
    r = jax.nn.sigmoid(jnp.einsum('btnd,nde->btne', xb, wa.astype(jnp.float32)).reshape(bsz, n_tok, D_RNN) + ba.astype(jnp.float32))
    i = jax.nn.sigmoid(jnp.einsum('btnd,nde->btne', xb, wx.astype(jnp.float32)).reshape(bsz, n_tok, D_RNN) + bx.astype(jnp.float32))
    log_a = -RG_C * r * jax.nn.softplus(-lam.astype(jnp.float32))
    a = jnp.exp(log_a)
    b = jnp.sqrt(-jnp.expm1(2.0 * log_a)) * (i * x)
    b = b.at[:, 0].add(a[:, 0] * h0.astype(jnp.float32))
    _, h = lax.associative_scan(lambda e1, e2: (e1[0] * e2[0], e2[0] * e1[1] + e2[1]), (a, b), axis=1)
    return h

def ec_moe(x, router_w, w_gate, w_up, w_down):
    bsz, n_tok, _ = x.shape
    cap = n_tok * EC_CAPACITY // N_EXPERTS
    aff = jax.nn.softmax(jnp.einsum('btd,de->bte', x, router_w).astype(jnp.float32), axis=-1)
    gate, idx = lax.top_k(jnp.swapaxes(aff, 1, 2), cap)
    bidx = jnp.arange(bsz)[:, None, None]
    xe = x[bidx, idx]
    hid = jax.nn.silu(jnp.einsum('becd,edf->becf', xe, w_gate)) * jnp.einsum('becd,edf->becf', xe, w_up)
    ye = jnp.einsum('becf,efd->becd', hid, w_down) * gate[..., None].astype(x.dtype)
    return jnp.zeros_like(x).at[bidx, idx].add(ye)

def adaln(cond, w, b):
    m = (jax.nn.silu(cond) @ w + b)[:, None, :]
    return jnp.split(m, 6, axis=-1)

def even_mixer(xm, j, P, ctx):
    bsz, n_tok, _ = xm.shape
    proj = xm @ P['ev_w_in'][j]
    qb, kb, vb, qa, ka, va, oa, ga = split_cols(proj, [B_HEADS * B_HEAD_DIM, B_KV_HEADS * B_HEAD_DIM, B_KV_HEADS * B_HEAD_DIM,
                                                      A_HEADS * A_QK_DIM, A_HEADS * A_QK_DIM, A_HEADS * A_V_DIM, A_HEADS * A_V_DIM, 4 * A_HEADS])
    qb = rms_norm(qb.reshape(bsz, n_tok, B_HEADS, B_HEAD_DIM), P['gqa_q_norm'][j])
    kb = rms_norm(kb.reshape(bsz, n_tok, B_KV_HEADS, B_HEAD_DIM), P['gqa_k_norm'][j])
    vb = vb.reshape(bsz, n_tok, B_KV_HEADS, B_HEAD_DIM)
    if ctx is None:
        k_all, v_all = kb, vb
        c0 = jnp.zeros((bsz, 2, A_HEADS, A_QK_DIM, A_V_DIM), jnp.float32)
        n0 = jnp.zeros((bsz, 2, A_HEADS, A_QK_DIM), jnp.float32)
        m0 = jnp.zeros((bsz, 2, A_HEADS), jnp.float32)
    else:
        c0, n0, m0, ctx_k, ctx_v = ctx
        row, col = grid_positions(n_tok)
        qb = rope_2d(qb, row, col)
        k_all = jnp.concatenate([ctx_k.astype(xm.dtype), rope_2d(kb, row, col)], axis=1)
        v_all = jnp.concatenate([ctx_v.astype(xm.dtype), vb], axis=1)
    ob = attend_blocked(qb.reshape(bsz, n_tok, B_KV_HEADS, B_HEADS // B_KV_HEADS, B_HEAD_DIM), k_all, v_all, B_HEAD_DIM ** -0.5)
    ob = ob.reshape(bsz, n_tok, B_HEADS * B_HEAD_DIM)
    gates = (ga + P['mlstm_gate_b'][j]).astype(jnp.float32).reshape(bsz, n_tok, 4, A_HEADS)
    qa = qa.reshape(bsz, n_tok, A_HEADS, A_QK_DIM)
    ka = ka.reshape(bsz, n_tok, A_HEADS, A_QK_DIM) * (A_QK_DIM ** -0.5)
    va = va.reshape(bsz, n_tok, A_HEADS, A_V_DIM)
    ha, c_f, n_f, m_f = mlstm_bidir(qa, ka, va, gates, c0, n0, m0)
    ha = rms_norm(ha.astype(xm.dtype), P['mlstm_norm_w'][j].reshape(A_HEADS, A_V_DIM)).reshape(bsz, n_tok, A_HEADS * A_V_DIM)
    ha = ha * jax.nn.sigmoid(oa)
    out = jnp.concatenate([ob, ha], axis=-1) @ P['ev_w_out'][j]
    st = (c_f, n_f, m_f, kb, vb) if ctx is None else None
    return out, st

def odd_mixer(xm, j, P, ctx):
    bsz, n_tok, _ = xm.shape
    proj = xm @ P['od_w_in'][j]
    cq, ckv, kr, xr, xg = split_cols(proj, [C_Q_LORA, C_KV_LORA, C_ROPE, D_RNN, D_RNN])
    cq = rms_norm(cq, P['mla_q_norm'][j])
    q = (cq @ P['mla_w_uq'][j]).reshape(bsz, n_tok, C_HEADS, C_NOPE + C_ROPE)
    q_nope, q_rope = q[..., :C_NOPE], q[..., C_NOPE:]
    ckv = rms_norm(ckv, P['mla_kv_norm'][j])
    if ctx is None:
        ckv_all, kr_all = ckv, kr
        h0 = jnp.zeros((bsz, 2, D_RNN), jnp.float32)
    else:
        ctx_ckv, ctx_kr, h0 = ctx
        row, col = grid_positions(n_tok)
        q_rope = rope_2d(q_rope, row, col)
        kr_rot = rope_2d(kr[:, :, None, :], row, col)[:, :, 0]
        ckv_all = jnp.concatenate([ctx_ckv.astype(xm.dtype), ckv], axis=1)
        kr_all = jnp.concatenate([ctx_kr.astype(xm.dtype), kr_rot], axis=1)
    n_keys = ckv_all.shape[1]
    kv = (ckv_all @ P['mla_w_ukv'][j]).reshape(bsz, n_keys, C_HEADS, C_NOPE + C_V)
    k = jnp.concatenate([kv[..., :C_NOPE], jnp.broadcast_to(kr_all[:, :, None, :], (bsz, n_keys, C_HEADS, C_ROPE))], axis=-1)
    v = kv[..., C_NOPE:]
    qf = jnp.concatenate([q_nope, q_rope], axis=-1)[:, :, :, None, :]
    oc = attend_blocked(qf, k, v, (C_NOPE + C_ROPE) ** -0.5).reshape(bsz, n_tok, C_HEADS * C_V)
    xc = conv_centred(xr, P['rg_conv_w'][j], P['rg_conv_b'][j]).astype(jnp.float32)
    hf = rglru_scan(xc, P['rg_wa'][j, 0], P['rg_ba'][j, 0], P['rg_wx'][j, 0], P['rg_bx'][j, 0], P['rg_lambda'][j, 0], h0[:, 0])
    hb = rglru_scan(jnp.flip(xc, axis=1), P['rg_wa'][j, 1], P['rg_ba'][j, 1], P['rg_wx'][j, 1], P['rg_bx'][j, 1], P['rg_lambda'][j, 1], h0[:, 1])
    rg = (hf + jnp.flip(hb, axis=1)).astype(xm.dtype) * jax.nn.gelu(xg)
    out = jnp.concatenate([oc, rg], axis=-1) @ P['od_w_out'][j]
    st = (ckv, kr, jnp.stack([hf[:, -1], hb[:, -1]], axis=1)) if ctx is None else None
    return out, st

def trunk(x, cond, P, caches):
    ev_states, od_states = [], []
    for layer in range(DEPTH):
        j = layer // 2
        sh1, sc1, g1, sh2, sc2, g2 = adaln(cond, P['ada_w'][layer], P['ada_b'][layer])
        xm = rms_norm(x, P['norm1_w'][layer]) * (1 + sc1) + sh1
        if layer % 2 == 0:
            ctx = None if caches is None else (caches['mC'][:, j], caches['mn'][:, j], caches['mm'][:, j], caches['gk'][:, j], caches['gv'][:, j])
            out, st = even_mixer(xm, j, P, ctx)
            if st is not None:
                ev_states.append(st)
        else:
            ctx = None if caches is None else (caches['ckv'][:, j], caches['kr'][:, j], caches['rh'][:, j])
            out, st = odd_mixer(xm, j, P, ctx)
            if st is not None:
                od_states.append(st)
        x = x + g1 * out
        xm = rms_norm(x, P['norm2_w'][layer]) * (1 + sc2) + sh2
        x = x + g2 * ec_moe(xm, P['router_w'][layer], P['exp_w_gate'][layer], P['exp_w_up'][layer], P['exp_w_down'][layer])
    return rms_norm(x, P['final_norm_w']), ev_states, od_states

def setup_inputs(seed: int = 0) -> dict:
    key = jax.random.key(seed)
    ks = jax.random.split(key, 40)
    f32 = jnp.float32

    def nrm(k, shape, scale=1.0):
        return jax.random.normal(k, shape, f32) * scale

    def gain(k, shape):
        return 1.0 + nrm(k, shape, 0.05)

    gate_base = jnp.repeat(jnp.array([0.0, 3.0, 0.0, 3.0], f32), A_HEADS)
    return {
        'x_prompt': nrm(ks[0], (BATCH, SEQ, D_MODEL)),
        'x_sample': nrm(ks[1], (DEC_BATCH, DEC_SEQ, D_MODEL)),
        'state_mlstm_C': nrm(ks[2], (DEC_BATCH, N_EVEN, 2, A_HEADS, A_QK_DIM, A_V_DIM), 0.1),
        'state_mlstm_n': nrm(ks[3], (DEC_BATCH, N_EVEN, 2, A_HEADS, A_QK_DIM), 0.1),
        'state_mlstm_m': nrm(ks[4], (DEC_BATCH, N_EVEN, 2, A_HEADS)),
        'cache_gqa_k': nrm(ks[5], (DEC_BATCH, N_EVEN, PAST_LEN, B_KV_HEADS, B_HEAD_DIM)),
        'cache_gqa_v': nrm(ks[6], (DEC_BATCH, N_EVEN, PAST_LEN, B_KV_HEADS, B_HEAD_DIM)),
        'cache_mla_ckv': nrm(ks[7], (DEC_BATCH, N_ODD, PAST_LEN, C_KV_LORA)),
        'cache_mla_krope': nrm(ks[8], (DEC_BATCH, N_ODD, PAST_LEN, C_ROPE)),
        'state_rglru_h': nrm(ks[9], (DEC_BATCH, N_ODD, 2, D_RNN), 0.5),
        'c': nrm(ks[10], (DEC_BATCH, D_MODEL)),
        'c_ctx': nrm(ks[11], (D_MODEL,)),
        'norm1_w': gain(ks[12], (DEPTH, D_MODEL)),
        'norm2_w': gain(ks[13], (DEPTH, D_MODEL)),
        'final_norm_w': gain(ks[14], (D_MODEL,)),
        'ada_w': nrm(ks[15], (DEPTH, D_MODEL, 6 * D_MODEL), D_MODEL ** -0.5),
        'ada_b': nrm(ks[16], (DEPTH, 6 * D_MODEL), 0.02),
        'ev_w_in': nrm(ks[17], (N_EVEN, D_MODEL, EVEN_IN), D_MODEL ** -0.5),
        'ev_w_out': nrm(ks[18], (N_EVEN, EVEN_MIX, D_MODEL), EVEN_MIX ** -0.5),
        'gqa_q_norm': gain(ks[19], (N_EVEN, B_HEAD_DIM)),
        'gqa_k_norm': gain(ks[20], (N_EVEN, B_HEAD_DIM)),
        'mlstm_gate_b': gate_base[None, :] + nrm(ks[21], (N_EVEN, 4 * A_HEADS), 0.1),
        'mlstm_norm_w': gain(ks[22], (N_EVEN, A_HEADS * A_V_DIM)),
        'od_w_in': nrm(ks[23], (N_ODD, D_MODEL, ODD_IN), D_MODEL ** -0.5),
        'od_w_out': nrm(ks[24], (N_ODD, ODD_MIX, D_MODEL), ODD_MIX ** -0.5),
        'mla_q_norm': gain(ks[25], (N_ODD, C_Q_LORA)),
        'mla_kv_norm': gain(ks[26], (N_ODD, C_KV_LORA)),
        'mla_w_uq': nrm(ks[27], (N_ODD, C_Q_LORA, C_HEADS * (C_NOPE + C_ROPE)), C_Q_LORA ** -0.5),
        'mla_w_ukv': nrm(ks[28], (N_ODD, C_KV_LORA, C_HEADS * (C_NOPE + C_V)), C_KV_LORA ** -0.5),
        'rg_conv_w': nrm(ks[29], (N_ODD, CONV_W, D_RNN), CONV_W ** -0.5),
        'rg_conv_b': nrm(ks[30], (N_ODD, D_RNN), 0.02),
        'rg_wa': nrm(ks[31], (N_ODD, 2, RG_BLOCKS, RG_BW, RG_BW), RG_BW ** -0.5),
        'rg_ba': nrm(ks[32], (N_ODD, 2, D_RNN), 0.02),
        'rg_wx': nrm(ks[33], (N_ODD, 2, RG_BLOCKS, RG_BW, RG_BW), RG_BW ** -0.5),
        'rg_bx': nrm(ks[34], (N_ODD, 2, D_RNN), 0.02),
        'rg_lambda': 4.3 + 4.7 * jax.random.uniform(ks[35], (N_ODD, 2, D_RNN), f32),
        'router_w': nrm(ks[36], (DEPTH, D_MODEL, N_EXPERTS), D_MODEL ** -0.5),
        'exp_w_gate': nrm(ks[37], (DEPTH, N_EXPERTS, D_MODEL, EXPERT_FF), D_MODEL ** -0.5),
        'exp_w_up': nrm(ks[38], (DEPTH, N_EXPERTS, D_MODEL, EXPERT_FF), D_MODEL ** -0.5),
        'exp_w_down': nrm(ks[39], (DEPTH, N_EXPERTS, EXPERT_FF, D_MODEL), EXPERT_FF ** -0.5),
    }

def reference(x_prompt, x_sample, state_mlstm_C, state_mlstm_n, state_mlstm_m, cache_gqa_k, cache_gqa_v,
              cache_mla_ckv, cache_mla_krope, state_rglru_h, c, c_ctx, norm1_w, norm2_w, final_norm_w,
              ada_w, ada_b, ev_w_in, ev_w_out, gqa_q_norm, gqa_k_norm, mlstm_gate_b, mlstm_norm_w,
              od_w_in, od_w_out, mla_q_norm, mla_kv_norm, mla_w_uq, mla_w_ukv, rg_conv_w, rg_conv_b,
              rg_wa, rg_ba, rg_wx, rg_bx, rg_lambda, router_w, exp_w_gate, exp_w_up, exp_w_down):
    P = dict(norm1_w=norm1_w, norm2_w=norm2_w, final_norm_w=final_norm_w, ada_w=ada_w, ada_b=ada_b,
             ev_w_in=ev_w_in, ev_w_out=ev_w_out, gqa_q_norm=gqa_q_norm, gqa_k_norm=gqa_k_norm,
             mlstm_gate_b=mlstm_gate_b, mlstm_norm_w=mlstm_norm_w, od_w_in=od_w_in, od_w_out=od_w_out,
             mla_q_norm=mla_q_norm, mla_kv_norm=mla_kv_norm, mla_w_uq=mla_w_uq, mla_w_ukv=mla_w_ukv,
             rg_conv_w=rg_conv_w, rg_conv_b=rg_conv_b, rg_wa=rg_wa, rg_ba=rg_ba, rg_wx=rg_wx, rg_bx=rg_bx,
             rg_lambda=rg_lambda, router_w=router_w, exp_w_gate=exp_w_gate, exp_w_up=exp_w_up, exp_w_down=exp_w_down)
    y_prompt, ev_st, od_st = trunk(x_prompt, c_ctx[None, :], P, None)
    dt = x_prompt.dtype
    new_mC = jnp.stack([s[0] for s in ev_st], axis=1).astype(dt)
    new_mn = jnp.stack([s[1] for s in ev_st], axis=1).astype(dt)
    new_mm = jnp.stack([s[2] for s in ev_st], axis=1).astype(dt)
    new_gk = jnp.stack([s[3] for s in ev_st], axis=1).astype(dt)
    new_gv = jnp.stack([s[4] for s in ev_st], axis=1).astype(dt)
    new_ckv = jnp.stack([s[0] for s in od_st], axis=1).astype(dt)
    new_kr = jnp.stack([s[1] for s in od_st], axis=1).astype(dt)
    new_rh = jnp.stack([s[2] for s in od_st], axis=1).astype(dt)
    caches = dict(mC=state_mlstm_C, mn=state_mlstm_n, mm=state_mlstm_m, gk=cache_gqa_k, gv=cache_gqa_v,
                  ckv=cache_mla_ckv, kr=cache_mla_krope, rh=state_rglru_h)
    y_sample, _, _ = trunk(x_sample, c, P, caches)
    return (y_prompt, y_sample, new_mC, new_mn, new_mm, new_gk, new_gv, new_ckv, new_kr, new_rh)


_drawn_inputs = setup_inputs


def setup_inputs(seed=0):
    import zlib

    import numpy as np

    out = dict(_drawn_inputs(seed))
    spreads = {}
    factors = {'state_mlstm_C': 3.212,
     'state_mlstm_n': 4.928,
     'state_mlstm_m': 3.813,
     'cache_gqa_k': 3.134,
     'cache_gqa_v': 2.82,
     'cache_mla_ckv': 7.575,
     'cache_mla_krope': 8.0,
     'gqa_q_norm': 4.151,
     'mla_q_norm': 8.0,
     'rg_ba': 8.0,
     'rg_bx': 5.721}
    for name, (base, spread) in spreads.items():
        noise = np.random.default_rng([zlib.crc32(name.encode()), seed]).standard_normal(out[name].shape)
        drawn = base * np.exp(spread * noise) if base else spread * noise
        out[name] = jnp.asarray(drawn.astype(out[name].dtype))
    for name, factor in factors.items():
        out[name] = (out[name] * factor).astype(out[name].dtype)
    return out
```

```python
from contextlib import ExitStack

import concourse.bass as bass
from concourse import mybir

F32 = mybir.dt.float32
U32 = mybir.dt.uint32
I32 = mybir.dt.int32
ALU = mybir.AluOpType
ACT = mybir.ActivationFunctionType
AX = mybir.AxisListType

P = 128
D = 1024
KD = D // P
NS, NP = 512, 128
NT = NS + NP
TILES = NT // P
ST = NS // P
PT = ST
EPS = 1e-6

BH, BKV, BD = 8, 2, 64
AH, AQ, AV = 4, 64, 128
EVEN_IN = BH * BD + 2 * BKV * BD + AH * (2 * AQ + 2 * AV) + 4 * AH
C_QB, C_KB, C_VB = 0, BH * BD, (BH + BKV) * BD
C_QA = C_VB + BKV * BD
C_KA = C_QA + AH * AQ
C_VA = C_KA + AH * AQ
C_OA = C_VA + AH * AV
C_GA = C_OA + AH * AV

CH, CQL, CKVL, CNOPE, CROPE, CV = 8, 384, 256, 64, 32, 64
CQK = CNOPE + CROPE
DR, RGB, RGW = 512, 8, 64
ODD_IN = CQL + CKVL + CROPE + 2 * DR
ODD_TOK = CQL + CKVL + CROPE

NE, FF = 16, 512
CAPS, CAPP = NS * 2 // NE, NP * 2 // NE
CAP = CAPS + CAPP
FB = FF // P


class Steps:

    def __init__(self, eng, sem):
        self.eng, self.sem, self.n = eng, sem, 0

    def __call__(self, ins):
        self.n += 1
        ins.then_inc(self.sem, 1)
        return self.n

    def wait(self):
        self.eng.wait_ge(self.sem, self.n)

    def link(self, ins):
        self(ins)
        self.wait()


class Carve:

    def __init__(self, ap, at=0):
        self.ap, self.at = ap, at

    def __call__(self, *dims):
        n = 1
        for d in dims:
            n *= d
        assert self.at + n <= self.ap.shape[1], (self.at, n, self.ap.shape)
        a = self.ap[:, self.at:self.at + n]
        self.at += n
        if len(dims) == 1:
            return a
        names = "abcde"[:len(dims)]
        spec = "p (" + " ".join(names) + ") -> p " + " ".join(names)
        return a.rearrange(spec, **{k: v for k, v in zip(names[1:], dims[1:])})


def build(nc, A, O):
    ctx = ExitStack()
    with ctx:
        def sb(name, shape, dt=F32):
            return ctx.enter_context(nc.sbuf_tensor(name, shape, dt))

        in_use = []

        def sem(name):
            in_use.append(nc.alloc_semaphore(name))
            return in_use[-1]

        def clear_semaphores():
            nc.clear_and_free_semaphores(in_use)
            in_use.clear()
            nc.all_engine_barrier()

        def dram(name, shape):
            return nc.dram_tensor(name, shape, F32, kind="Internal").ap()

        x_rows = dram("x_rows", [NT, D])
        xm_rows = dram("xm_rows", [NT, D])
        mod_rows = dram("mod_rows", [2, 2, 6 * D])

        ring = sb("ring", [P, 6, 4096])
        xT = sb("xT", [P, KD, NT])
        xr = sb("xr", [P, TILES, D])
        proj = sb("proj", [P, TILES, EVEN_IN])
        ident = sb("ident", [P, P])
        small = sb("small", [P, 640])
        hold = sb("hold", [P, 2, D])
        psum = ctx.enter_context(nc.psum_tensor("psum", [P, 8, 512], F32))

        def bank(n, w=512):
            return psum[:, n, 0:w]

        ringf = ring[:, :, :].rearrange("p a b -> p (a b)")
        projf = proj[:, :, :].rearrange("p a b -> p (a b)")

        def modulation():
            s = {n: sem("mod_" + n) for n in ("consts", "cT", "silu", "used", "sum", "evac", "turned", "rows", "stored")}
            s_in = [sem(f"mod_in{i}") for i in range(3)]
            ada = ringf.rearrange("p (s k n) -> p s k n", s=3, k=KD)
            cs = Carve(projf)
            c_rows, cT = cs(P), cs(2 * KD)
            modT, bias, rows = cs(2, 2, 48), cs(2, P), cs(2, P)
            with nc.Block("modulation") as block:
                @block.sync
                def _(sp):
                    sp.dma_start(ident[:, :], A["ident"]).then_inc(s["consts"], 16)
                    sp.dma_start(c_rows[0:KD, :], A["c"].rearrange("a (k p) -> (a k) p", p=P)).then_inc(s["consts"], 16)
                    sp.dma_start(c_rows[KD:2 * KD, :], A["c_ctx"].rearrange("(k p) -> k p", p=P)).then_inc(s["consts"], 16)
                    for l in range(2):
                        for cond in range(2):
                            sp.dma_start(bias[48 * cond:48 * cond + 48, l, :],
                                         A["ada_b"][l].rearrange("(n p) -> n p", p=P)).then_inc(s["consts"], 16)
                    for g in range(12):
                        if g >= 3:
                            sp.wait_ge(s["used"], g - 2)
                        sp.dma_start(ada[:, g % 3], A["ada_w"][g // 6, :, (g % 6) * D:(g % 6 + 1) * D]
                                     .rearrange("(k p) n -> p k n", p=P)).then_inc(s_in[g % 3], 16)
                    for l in range(2):
                        sp.wait_ge(s["rows"], l + 1)
                        sp.dma_start(mod_rows[l].rearrange("c (n p) -> (c n) p", p=P), rows[0:96, l, :]).then_inc(s["stored"], 16)
                    sp.wait_ge(s["stored"], 32)

                @block.tensor
                def _(pe):
                    pe.wait_ge(s["consts"], 16 * 7)
                    pe.transpose(bank(0)[:, 0:2 * KD], c_rows[0:2 * KD, :], ident[0:2 * KD, 0:2 * KD]).then_inc(s["cT"], 1)
                    pe.wait_ge(s["silu"], 1)
                    for g in range(12):
                        pe.wait_ge(s_in[g % 3], 16 * (g // 3 + 1))
                        for b in range(8):
                            at = 2 * ((g % 6) * 8 + b)
                            for k in range(KD):
                                mm = pe.matmul(bank(2 + g // 6)[:, at:at + 2], ada[:, g % 3, k, b * P:(b + 1) * P],
                                               cT[:, k::KD], start=(k == 0), stop=(k == KD - 1))
                        mm.then_inc(s["used"], 1)
                    for l in range(2):
                        pe.wait_ge(s["evac"], l + 1)
                        pe.transpose(bank(4 + l)[0:96, 0:P], modT[:, l].rearrange("p c n -> p (c n)"),
                                     ident[:, :]).then_inc(s["turned"], 1)

                @block.scalar
                def _(act):
                    act.wait_ge(s["cT"], 1)
                    act.activation(cT, bank(0)[:, 0:2 * KD], ACT.Silu).then_inc(s["silu"], 1)

                @block.vector
                def _(dve):
                    for l in range(2):
                        dve.wait_ge(s["used"], 6 * (l + 1))
                        dve.tensor_copy(modT[:, l], bank(2 + l)[:, 0:96].rearrange("p (n c) -> p c n", c=2)).then_inc(s["evac"], 1)
                    for l in range(2):
                        dve.wait_ge(s["turned"], l + 1)
                        dve.tensor_tensor(rows[0:96, l, :], bank(4 + l)[0:96, 0:P], bias[0:96, l, :], ALU.add).then_inc(s["rows"], 1)

        def norm_in(l, w_slots, w_sem):
            s = {n: sem(f"n{l}_{n}") for n in ("rows", "mods", "hold", "sq", "root", "own", "scaled", "xm", "turned", "copied")}
            s_x = [sem(f"n{l}_x{t}") for t in range(TILES)]
            cs = Carve(projf)
            mods, nw = cs(2, 2, D), cs(D)
            xm = cs(2, D)
            junk = cs(D)
            ssq = small[:, 0:TILES]
            rstd = small[:, 8:8 + TILES]
            with nc.Block(f"norm_in_{l}") as block:
                @block.sync
                def _(sp):
                    for t in range(TILES):
                        if l == 0:
                            src = A["x_sample"][0, t * P:(t + 1) * P, :] if t < ST else A["x_prompt"][0]
                        else:
                            src = x_rows[t * P:(t + 1) * P, :]
                        sp.dma_start(xr[:, t, :], src).then_inc(s_x[t], 16)
                    for cond in range(2):
                        for j in range(2):
                            sp.dma_start(mods[:, cond, j, :], mod_rows[l, cond:cond + 1, j * D:(j + 1) * D].to_broadcast([P, D])).then_inc(s["mods"], 16)
                    sp.dma_start(nw, A["norm1_w"][l:l + 1, :].to_broadcast([P, D])).then_inc(s["mods"], 16)
                    for dst, src in w_slots:
                        sp.dma_start(dst, src).then_inc(w_sem, 16)
                    for cond in range(2):
                        sp.dma_start(hold[:, cond, :], mod_rows[l, cond:cond + 1, 2 * D:3 * D].to_broadcast([P, D])).then_inc(s["hold"], 16)
                    sp.wait_ge(s["hold"], 32)

                @block.scalar
                def _(act):
                    own = Steps(act, s["sq"])
                    for t in range(TILES):
                        act.wait_ge(s_x[t], 16)
                        own.link(act.activation(junk, xr[:, t, :], ACT.Square, accum_out=ssq[:, t:t + 1]))
                    act.activation(rstd, ssq, ACT.Sqrt, scale=1.0 / D, bias=EPS).then_inc(s["root"], 1)
                    for t in range(TILES):
                        for h in range(2):
                            act.wait_ge(s["turned"], 2 * t + h + 1)
                            act.activation(xT[:, 4 * h:4 * h + 4, t * P:(t + 1) * P],
                                           bank(2 * (t % 2) + h).rearrange("p (k c) -> p k c", k=4), ACT.Copy).then_inc(s["copied"], 1)

                @block.vector
                def _(dve):
                    own = Steps(dve, s["own"])
                    dve.wait_ge(s["mods"], 16 * 5)
                    for cond in range(2):
                        own(dve.scalar_tensor_tensor(out=mods[:, cond, 1, :], in0=mods[:, cond, 1, :], scalar=1.0,
                                                     in1=nw, op0=ALU.add, op1=ALU.mult))
                    dve.wait_ge(s["root"], 1)
                    own.link(dve.reciprocal(rstd, rstd))
                    for t in range(TILES):
                        cond = t // ST
                        if t >= 2:
                            dve.wait_ge(s["turned"], 2 * (t - 1))
                            dve.wait_ge(s["xm"], t - 1)
                        dve.scalar_tensor_tensor(out=xm[:, t % 2, :], in0=xr[:, t, :], scalar=rstd[:, t:t + 1],
                                                 in1=mods[:, cond, 1, :], op0=ALU.mult, op1=ALU.mult).then_inc(s["scaled"], 1)

                @block.gpsimd
                def _(pool):
                    pool.wait_ge(s["mods"], 16 * 5)
                    for t in range(TILES):
                        pool.wait_ge(s["scaled"], t + 1)
                        pool.tensor_tensor(xm[:, t % 2, :], xm[:, t % 2, :], mods[:, t // ST, 0, :], ALU.add).then_inc(s["xm"], 1)

                @block.tensor
                def _(pe):
                    for t in range(TILES):
                        pe.wait_ge(s["xm"], t + 1)
                        for h in range(2):
                            if t >= 2:
                                pe.wait_ge(s["copied"], 2 * (t - 2) + h + 1)
                            for k in range(4):
                                mm = pe.transpose(bank(2 * (t % 2) + h)[:, k * P:(k + 1) * P],
                                                  xm[:, t % 2, (4 * h + k) * P:(4 * h + k + 1) * P], ident[:, :])
                            mm.then_inc(s["turned"], 1)

        W_IN_CUTS = [(c, min(512, EVEN_IN - c)) for c in range(0, EVEN_IN, 512)]
        w_in_sem = sem("w_in")
        even_w = [(ring[:, i, 0:KD * n].rearrange("p (k n) -> p k n", k=KD),
                   A["ev_w_in"][0, :, c:c + n].rearrange("(k p) n -> p k n", p=P)) for i, (c, n) in enumerate(W_IN_CUTS)]

        def project_even():
            s_mm, s_act, s_dve = sem("pe_mm"), sem("pe_act"), sem("pe_dve")
            units = [(i, t) for i in range(len(W_IN_CUTS)) for t in range(TILES)]
            with nc.Block("project_even") as block:
                @block.tensor
                def _(pe):
                    pe.wait_ge(w_in_sem, 16 * len(W_IN_CUTS))
                    for u, (i, t) in enumerate(units):
                        n = W_IN_CUTS[i][1]
                        if u >= 8:
                            pe.wait_ge(s_act if u % 2 == 0 else s_dve, (u - 8) // 2 + 1)
                        for k in range(KD):
                            mm = pe.matmul(bank(u % 8, n), xT[:, k, t * P:(t + 1) * P], even_w[i][0][:, k, :],
                                           start=(k == 0), stop=(k == KD - 1))
                        mm.then_inc(s_mm, 1)

                def copies(eng, which, done):
                    for u, (i, t) in enumerate(units):
                        if u % 2 != which:
                            continue
                        c, n = W_IN_CUTS[i]
                        eng.wait_ge(s_mm, u + 1)
                        if which == 0:
                            ins = eng.activation(proj[:, t, c:c + n], bank(u % 8, n), ACT.Copy)
                        else:
                            ins = eng.tensor_copy(proj[:, t, c:c + n], bank(u % 8, n))
                        ins.then_inc(done, 1)

                @block.scalar
                def _(act):
                    copies(act, 0, s_act)

                @block.vector
                def _(dve):
                    copies(dve, 1, s_dve)

        sc = Carve(ringf, 2 * 4096)
        qT = sc(BH // 2, NT)
        kT = sc(NT + P)
        vctx = sc(BKV * BD)
        mqT, mkT = sc(2, NT), sc(2, NT)
        vaug = sc(TILES, AH, AV + 1)
        cols = sc(4, 2, TILES, AH)
        dec = sc(2, 2, TILES)
        carry = sc(2, 2, AV + 1)
        carryp = sc(2, 2, AV + 1)
        masks = sc(2, P)
        sel = sc(AH, P)
        selpair = sc(2, P)
        negM = sc(2, TILES, P)
        EVEN_TOP = sc.at
        scr_k = Carve(ringf, EVEN_TOP)

        def prepare_even():
            s = {n: sem("ep_" + n) for n in ("in", "own", "act", "pool", "gates", "gT", "sq", "ssq", "rs", "cos",
                                             "rot", "qk", "kcache", "out", "m_t", "m_c", "q_t", "q_c", "rows", "c_t", "ex", "exd")}
            cs = Carve(xT[:, :, :].rearrange("p k n -> p (k n)"))
            sq = cs(TILES, 640)
            s2 = Carve(ringf, EVEN_TOP)
            rotb = s2(ST, 640)
            gb = s2(16)
            ssq, rs = small[:, 0:50], small[:, 64:114]
            L = cs(2, NT)[0:4]
            tabs, wqk = cs(ST, 2, BD), cs(2, BD)
            Bc = s2(2, NT)[0:4]
            hc = Carve(ringf, 0)
            a_, M, W1, EN = (hc(2, NT)[0:4] for _ in range(4))
            G = Carve(ringf, 4 * NT)(4, NT)[0:4]
            WK = hc(2, NT)[0:4]
            rst = hc(NT)[0:4]
            mp = small[0:4, 128:138].rearrange("p (d t) -> p d t", d=2)
            mn = small[0:4, 144:154].rearrange("p (d t) -> p d t", d=2)
            decr = small[0:4, 160:170].rearrange("p (d t) -> p d t", d=2)
            ORDER = [list(range(ST)), list(range(ST - 1, -1, -1))]
            qk = proj[:, :, 0:640]

            def by_group(x):
                return x.rearrange("p (g j d) -> p g j d", g=BKV, d=BD)

            def paired(t):
                return proj[:, t, 0:512].rearrange("p (j g d) -> p g j d", g=BKV, d=BD)

            with nc.Block("prepare_even") as block:
                @block.sync
                def _(sp):
                    n = 0
                    st = A["state_mlstm_C"][0, 0]
                    sn = A["state_mlstm_n"][0, 0]
                    for r in range(2):
                        for d in range(2):
                            sp.dma_start(carry[r * 64:r * 64 + 64, d, :, 0:AV],
                                         st[d, r::2].rearrange("j d e -> d j e")).then_inc(s["in"], 16)
                            with nc.allow_non_contiguous_dma(reason="256 words"):
                                sp.dma_start(carry[r * 64:r * 64 + 64, d, :, AV:AV + 1],
                                             sn[d, r::2].rearrange("j (d e) -> d j e", e=1)).then_inc(s["in"], 16)
                            n += 2
                    with nc.allow_non_contiguous_dma(reason="8 words"):
                        for d in range(2):
                            sp.dma_start(mp[:, d, ORDER[d][0]:ORDER[d][0] + 1],
                                         A["state_mlstm_m"][0, 0, d].rearrange("(h e) -> h e", e=1)).then_inc(s["in"], 16)
                            n += 1
                    for dst, src in [(tabs, A["rope_b"]), (masks, A["masks"]), (sel[0:4], A["sel"]),
                                     (selpair[0:4], A["selpair"]), (rst, A["rst"]),
                                     (wqk[:, 0, :], A["gqa_q_norm"].to_broadcast([P, BD])),
                                     (wqk[:, 1, :], A["gqa_k_norm"].to_broadcast([P, BD])),
                                     (gb, A["mlstm_gate_b"].to_broadcast([P, 16])),
                                     (vctx, A["cache_gqa_v"][0, 0].rearrange("s h d -> s (h d)")),
                                     (rotb[:, 0, 0:P], A["cache_gqa_k"][0, 0].rearrange("s h d -> s (h d)"))]:
                        sp.dma_start(dst, src).then_inc(s["in"], 16)
                        n += 1
                    sp.in_count = n
                    sp.wait_ge(s["kcache"], 1)
                    sp.dma_start(O[5][0, 0].rearrange("s h d -> s (h d)"), proj[:, PT, C_KB:C_KB + P]).then_inc(s["out"], 16)
                    sp.dma_start(O[6][0, 0].rearrange("s h d -> s (h d)"), proj[:, PT, C_VB:C_VB + P]).then_inc(s["out"], 16)
                    sp.wait_ge(s["out"], 32)
                LOADS = 16 * (8 + 2 + 10)

                @block.gpsimd
                def _(pool):
                    for t in range(TILES):
                        pool.tensor_scalar(proj[:, t, C_KA:C_KA + AH * AQ], proj[:, t, C_KA:C_KA + AH * AQ],
                                           AQ ** -0.5, None, ALU.mult).then_inc(s["pool"], 1)
                    pool.memset(vaug[:, :, :, AV:AV + 1], 1.0).then_inc(s["rows"], 1)
                    for t in range(TILES):
                        pool.tensor_copy(vaug[:, t, :, 0:AV], proj[:, t, C_VA:C_VA + AH * AV].rearrange("p (h e) -> p h e", h=AH)).then_inc(s["rows"], 1)
                    pool.wait_ge(s["in"], LOADS)
                    pool.wait_ge(s["kcache"], 1)
                    pool.wait_ge(s["m_t"], 2 * TILES + 1)
                    for t in range(ST):
                        x = proj[:, t, 0:640].rearrange("p (h a u i) -> p h a u i", a=2, u=2, i=16)
                        o = rotb[:, t, :].rearrange("p (h a u i) -> p h a u i", a=2, u=2, i=16)
                        sn = tabs[:, t, 1, :].rearrange("p (a u i) -> p a u i", a=2, u=2)
                        for u in range(2):
                            for a in range(2):
                                pool.tensor_tensor(o[:, :, a, u, :], x[:, :, a, 1 - u, :],
                                                   sn[:, a, u, :].unsqueeze(1).to_broadcast([P, 10, 16]), ALU.mult).then_inc(s["rot"], 1)

                @block.vector
                def _(dve):
                    own = Steps(dve, s["own"])
                    dve.wait_ge(s["in"], LOADS)
                    dve.tensor_tensor(proj[:, :, C_GA:C_GA + 16], proj[:, :, C_GA:C_GA + 16],
                                      gb.unsqueeze(1).to_broadcast([P, TILES, 16]), ALU.add).then_inc(s["gates"], 1)
                    dve.memset(mp[:, :, PT:PT + 1], 0.0).then_inc(s["own"], 1)
                    own.n += 1
                    dve.wait_ge(s["sq"], 1)
                    dve.tensor_reduce(ssq.rearrange("p (t h) -> p t h", t=TILES),
                                      sq.rearrange("p t (h d) -> p t h d", d=BD), AX.X, ALU.add).then_inc(s["ssq"], 1)
                    for c in range(5):
                        dve.wait_ge(s["gT"], 20)
                        own(dve.tensor_copy(G.rearrange("p k n -> p (k n)")[:, c * 512:(c + 1) * 512], psum[0:4, c, :]))
                    own.wait()
                    own.link(dve.tensor_scalar(L, G[:, 1::2, :], 0.0, None, ALU.min))
                    dve.wait_ge(s["rs"], 1)
                    own.link(dve.reciprocal(rs, rs))
                    r3 = rs.rearrange("p (t h) -> p t h", t=TILES)
                    for t in range(TILES):
                        own.link(dve.tensor_tensor(proj[:, t, 0:640].rearrange("p (h d) -> p h d", d=BD),
                                              proj[:, t, 0:640].rearrange("p (h d) -> p h d", d=BD),
                                              r3[:, t].unsqueeze(2).to_broadcast([P, 10, BD]), ALU.mult))
                        own(dve.tensor_tensor(proj[:, t, 0:512].rearrange("p (h d) -> p h d", d=BD),
                                              proj[:, t, 0:512].rearrange("p (h d) -> p h d", d=BD),
                                              wqk[:, 0:1, :].to_broadcast([P, BH, BD]), ALU.mult))
                        own.link(dve.tensor_tensor(proj[:, t, 512:640].rearrange("p (h d) -> p h d", d=BD),
                                              proj[:, t, 512:640].rearrange("p (h d) -> p h d", d=BD),
                                              wqk[:, 1:2, :].to_broadcast([P, BKV, BD]), ALU.mult))
                    dve.sem_inc(s["kcache"], 1)
                    for t in range(ST):
                        own(dve.tensor_tensor(sq[:, t, :].rearrange("p (h d) -> p h d", d=BD),
                                              proj[:, t, 0:640].rearrange("p (h d) -> p h d", d=BD),
                                              tabs[:, t, 0:1, :].to_broadcast([P, 10, BD]), ALU.mult))
                    dve.wait_ge(s["own"], own.n)
                    dve.wait_ge(s["rot"], 16)
                    for t in range(ST):
                        own(dve.tensor_tensor(paired(t), by_group(sq[:, t, 0:512]), by_group(rotb[:, t, 0:512]), ALU.add))
                        own.link(dve.tensor_tensor(proj[:, t, 512:640], sq[:, t, 512:640], rotb[:, t, 512:640], ALU.add))
                        dve.sem_inc(s["qk"], 1)
                    own.link(dve.tensor_copy(sq[:, PT, 0:512], proj[:, PT, 0:512]))
                    own.link(dve.tensor_copy(paired(PT), by_group(sq[:, PT, 0:512])))
                    dve.sem_inc(s["qk"], 1)
                    dve.wait_ge(s["act"], 4)
                    own.link(dve.tensor_tensor(L, L, Bc, ALU.subtract))
                    own(dve.tensor_tensor_scan(Bc[:, 0, :], rst, L[:, 0, :], 0.0, ALU.mult, ALU.add))
                    own.link(dve.tensor_tensor_scan(Bc[:, 1, ::-1], rst, L[:, 1, ::-1], 0.0, ALU.mult, ALU.add))
                    own.link(dve.tensor_tensor(a_, G[:, 0::2, :], Bc, ALU.subtract))
                    for step in range(ST + 1):
                        for d in range(2):
                            t = PT if step == ST else ORDER[d][step]
                            lo, hi = t * P, (t + 1) * P
                            if d == 0:
                                src, dst, end = a_[:, 0, lo:hi], M[:, 0, lo:hi], hi - 1
                            else:
                                stop = lo - 1 if lo else None
                                src, dst, end = a_[:, 1, hi - 1:stop:-1], M[:, 1, hi - 1:stop:-1], lo
                            own.link(dve.tensor_tensor_scan(dst, src, src, mp[:, d, t:t + 1], ALU.max, ALU.max))
                            own.link(dve.tensor_tensor(mn[:, d, t:t + 1], Bc[:, d, end:end + 1], M[:, d, end:end + 1], ALU.add))
                            if step < ST - 1:
                                nxt = ORDER[d][step + 1]
                                own.link(dve.tensor_copy(mp[:, d, nxt:nxt + 1], mn[:, d, t:t + 1]))
                    own(dve.tensor_tensor(EN, Bc, M, ALU.add))
                    for d in range(2):
                        Mt = M[:, d, :].rearrange("p (t n) -> p t n", t=TILES)
                        At = a_[:, d, :].rearrange("p (t n) -> p t n", t=TILES)
                        own(dve.tensor_tensor(W1[:, d, :].rearrange("p (t n) -> p t n", t=TILES), Mt,
                                              mp[:, d, :].unsqueeze(2).to_broadcast([4, TILES, P]), ALU.subtract))
                        e = P - 1 if d == 0 else 0
                        own(dve.tensor_tensor(WK[:, d, :].rearrange("p (t n) -> p t n", t=TILES), At,
                                              Mt[:, :, e:e + 1].to_broadcast([4, TILES, P]), ALU.subtract))
                    own.link(dve.tensor_scalar(negM[0:4].rearrange("p d t n -> p (d t n)"), M.rearrange("p d n -> p (d n)"), -1.0, None, ALU.mult))
                    dve.sem_inc(s["ex"], 1)
                    dve.wait_ge(s["exd"], 3)
                    for d in range(2):
                        e = P - 1 if d == 0 else 0
                        own.link(dve.tensor_copy(decr[:, d, :], W1[:, d, e::P]))
                    dve.sem_inc(s["ex"], 1)
                    dve.wait_ge(s["c_t"], 1)
                    own(dve.tensor_copy(cols.rearrange("p k d t h -> p (k d t h)"), bank(6, 160)))
                    own(dve.tensor_copy(dec.rearrange("p j d t -> p (j d t)"), bank(7, 20)))

                @block.scalar
                def _(act):
                    own = Steps(act, s["act"])
                    for t in range(TILES):
                        ins = act.activation(sq[:, t, :], proj[:, t, 0:640], ACT.Square)
                        if t < TILES - 1:
                            act.maybe = ins
                            ins.then_inc(s["cos"], 1)
                        else:
                            ins.then_inc(s["cos"], 1)
                    act.wait_ge(s["cos"], TILES)
                    act.sem_inc(s["sq"], 1)
                    act.wait_ge(s["ssq"], 1)
                    act.activation(rs, ssq, ACT.Sqrt, scale=1.0 / BD, bias=EPS).then_inc(s["rs"], 1)
                    act.wait_ge(s["own"], 6)
                    own.link(act.activation(Bc, G[:, 1::2, :], ACT.Abs))
                    own.link(act.activation(Bc, Bc, ACT.Exp, scale=-1.0))
                    own.link(act.activation(Bc, Bc, ACT.Ln, bias=1.0))
                    own(act.activation(small[0:1, 600:601], Bc[0:1, 0, 0:1], ACT.Copy))
                    for n in range(2 * TILES):
                        act.wait_ge(s["m_t"], n + 1)
                        dst = (mqT, mkT)[n % 2]
                        act.activation(dst[:, :, (n // 2) * P:(n // 2 + 1) * P],
                                       bank(6 + n % 2, 256).rearrange("p (j c) -> p j c", j=2), ACT.Copy).then_inc(s["m_c"], 1)
                    act.wait_ge(s["m_t"], 2 * TILES + 1)
                    act.activation(kT[:, 0:P], bank(6, P), ACT.Copy).then_inc(s["m_c"], 1)
                    act.wait_ge(s["ex"], 1)
                    act.activation(W1, W1, ACT.Exp, scale=-1.0).then_inc(s["exd"], 1)
                    act.activation(EN, EN, ACT.Exp, scale=-1.0).then_inc(s["exd"], 1)
                    act.activation(WK, WK, ACT.Exp).then_inc(s["exd"], 1)
                    for t in range(TILES):
                        act.wait_ge(s["q_t"], t + 1)
                        act.activation(qT[:, :, t * P:(t + 1) * P], bank(2 * (t % 2)).rearrange("p (j c) -> p j c", j=4), ACT.Copy).then_inc(s["q_c"], 1)
                        act.activation(kT[:, (t + 1) * P:(t + 2) * P], bank(2 * (t % 2) + 1, P), ACT.Copy).then_inc(s["q_c"], 1)

                @block.tensor
                def _(pe):
                    pe.wait_ge(s["gates"], 1)
                    for kind in range(4):
                        for t in range(TILES):
                            at = kind * NT + t * P
                            pe.transpose(psum[0:4, at // 512, at % 512:at % 512 + P], proj[:, t, C_GA + 4 * kind:C_GA + 4 * kind + 4],
                                         ident[:, :]).then_inc(s["gT"], 1)
                    for n in range(2 * TILES):
                        t = n // 2
                        if n % 2:
                            pe.wait_ge(s["pool"], t + 1)
                        if n >= 2:
                            pe.wait_ge(s["m_c"], n - 1)
                        c0 = (C_QA, C_KA)[n % 2]
                        for j in range(2):
                            mm = pe.transpose(bank(6 + n % 2)[:, j * P:(j + 1) * P], proj[:, t, c0 + j * P:c0 + (j + 1) * P], ident[:, :])
                        mm.then_inc(s["m_t"], 1)
                    pe.wait_ge(s["in"], LOADS)
                    pe.wait_ge(s["m_c"], 2 * TILES - 1)
                    pe.transpose(bank(6, P), rotb[:, 0, 0:P], ident[:, :]).then_inc(s["m_t"], 1)
                    pe.wait_ge(s["own"], 6)
                    for t in range(TILES):
                        pe.wait_ge(s["qk"], t + 1)
                        if t >= 2:
                            pe.wait_ge(s["q_c"], 2 * (t - 1))
                        for j in range(4):
                            pe.transpose(bank(2 * (t % 2))[:, j * P:(j + 1) * P],
                                         proj[:, t, j * P:(j + 1) * P], ident[:, :])
                        pe.transpose(bank(2 * (t % 2) + 1, P), proj[:, t, 512:640], ident[:, :]).then_inc(s["q_t"], 1)
                    pe.wait_ge(s["ex"], 2)
                    pe.wait_ge(s["m_c"], 2 * TILES + 1)
                    for kind, src in enumerate((a_, W1, EN, WK)):
                        for d in range(2):
                            for t in range(TILES):
                                at = ((kind * 2 + d) * TILES + t) * AH
                                pe.transpose(bank(6)[:, at:at + 4], src[:, d, t * P:(t + 1) * P], ident[0:4, 0:4])
                    for j in range(2):
                        mm = pe.matmul(bank(7)[:, 10 * j:10 * j + 10], selpair[0:4, j, :], decr.rearrange("p d t -> p (d t)"), start=True, stop=True)
                    mm.then_inc(s["c_t"], 1)
            return mn

        def mlstm(mn):
            s = {n: sem("ml_" + n) for n in ("st", "eb", "E", "W", "mix", "inter", "num", "own", "kw", "upd", "carry", "out", "h")}
            s2 = Carve(ringf, EVEN_TOP)
            E = s2(2, 4, P)
            KW = s2(AH, AQ)
            its = s2(2, 2, AV + 1)
            num = s2(2, 2, AV + 1)
            dn = small[:, 0:4]
            dn2 = small[:, 4:8]
            units = []
            for i in range(ST):
                units += [(0, i), (1, ST - 1 - i)]
            units += [(0, PT), (1, PT)]
            first = {}
            for u, (d, t) in enumerate(units):
                first.setdefault(t, u)
            HA = proj[:, :, C_VA:C_VA + AH * AV]

            def col(kind, d, t, h):
                return cols[:, kind, d, t, h:h + 1]

            with nc.Block("mlstm") as block:
                @block.tensor
                def _(pe):
                    n_inter = 0
                    for u, (d, t) in enumerate(units):
                        tok = slice(t * P, (t + 1) * P)
                        if u >= 1:
                            pe.wait_ge(s["W"], u)
                        for j in range(2):
                            for r in range(2):
                                mm = pe.matmul(psum[:, r, j * P:(j + 1) * P], mkT[r * 64:r * 64 + 64, j, tok],
                                               mqT[r * 64:r * 64 + 64, j, tok], start=True, stop=True)
                        mm.then_inc(s["st"], 1)
                        if u >= 1:
                            pe.wait_ge(s["E"], u)
                        for i in range(4):
                            r, j = i // 2, i % 2
                            pe.matmul(psum[:, 2, i * P:(i + 1) * P], ident[:, :], masks[:, d, :], start=(i == 0), stop=False, skip_group_check=True)
                        for i in range(4):
                            r, j = i // 2, i % 2
                            mm = pe.matmul(psum[:, 2, i * P:(i + 1) * P], sel[0:4, 2 * j + r, :], negM[0:4, d, t, :],
                                           start=False, stop=(i == 3), skip_group_check=True)
                        mm.then_inc(s["eb"], 1)
                        if t != PT:
                            if u >= 2:
                                pe.wait_ge(s["carry"], u - 1)
                            if u >= 1:
                                pe.wait_ge(s["inter"], n_inter)
                            for j in range(2):
                                for r in range(2):
                                    mm = pe.matmul(psum[:, 5 + r, j * 129:(j + 1) * 129], mqT[r * 64:r * 64 + 64, j, tok],
                                                   carry[r * 64:r * 64 + 64, d, j, :], start=True, stop=True)
                            n_inter += 1
                            mm.then_inc(s["mix"], 1)
                        pe.wait_ge(s["kw"], u + 1)
                        if u >= 1:
                            pe.wait_ge(s["carry"], u)
                        for j in range(2):
                            for r in range(2):
                                mm = pe.matmul(psum[r * 64:r * 64 + 64, 7, j * 129:(j + 1) * 129], KW[:, 2 * j + r, :],
                                               vaug[:, t, 2 * j + r, :], start=True, stop=True)
                        mm.then_inc(s["upd"], 1)
                        pe.wait_ge(s["W"], u + 1)
                        if u >= 1:
                            pe.wait_ge(s["num"], u)
                        for j in range(2):
                            for r in range(2):
                                mm = pe.matmul(psum[:, 3 + r, j * 129:(j + 1) * 129], E[:, u % 2, 2 * r + j, :],
                                               vaug[:, t, 2 * j + r, :], start=True, stop=True)
                        mm.then_inc(s["out"], 1)

                @block.scalar
                def _(act):
                    n_inter = 0
                    for u, (d, t) in enumerate(units):
                        act.wait_ge(s["eb"], u + 1)
                        if u >= 2:
                            act.wait_ge(s["out"], u - 1)
                        for i in range(4):
                            r, j = i // 2, i % 2
                            mm = act.activation(E[:, u % 2, i, :], psum[:, 2, i * P:(i + 1) * P], ACT.Exp, bias=col(0, d, t, 2 * j + r))
                        mm.then_inc(s["E"], 1)
                        if t != PT:
                            n_inter += 1
                            act.wait_ge(s["mix"], n_inter)
                            if u >= 1:
                                act.wait_ge(s["num"], u)
                            for r in range(2):
                                for j in range(2):
                                    mm = act.activation(its[:, r, j, :], psum[:, 5 + r, j * 129:(j + 1) * 129], ACT.Copy,
                                                        scale=col(1, d, t, 2 * j + r))
                            mm.then_inc(s["inter"], 1)

                @block.vector
                def _(dve):
                    own = Steps(dve, s["own"])
                    n_inter = 0
                    for u, (d, t) in enumerate(units):
                        if u >= 1:
                            dve.wait_ge(s["upd"], u)
                        dve.tensor_tensor(KW, proj[:, t, C_KA:C_KA + AH * AQ].rearrange("p (h d) -> p h d", d=AQ),
                                          cols[:, 3, d, t, :].unsqueeze(2).to_broadcast([P, AH, AQ]), ALU.mult).then_inc(s["kw"], 1)
                        dve.wait_ge(s["st"], u + 1)
                        dve.wait_ge(s["E"], u + 1)
                        dve.tensor_tensor(E[:, u % 2].rearrange("p (r j) n -> p r (j n)", r=2), E[:, u % 2].rearrange("p (r j) n -> p r (j n)", r=2),
                                          psum[:, 0:2, 0:2 * P], ALU.mult).then_inc(s["W"], 1)
                        dve.wait_ge(s["upd"], u + 1)
                        if t == PT:
                            dve.tensor_copy(carryp[:, d].rearrange("p j e -> p (j e)"), bank(7, 258)).then_inc(s["carry"], 1)
                        else:
                            dve.wait_ge(s["mix"], n_inter + 1)
                            for j in range(2):
                                ins = dve.scalar_tensor_tensor(out=carry[:, d, j, :], in0=carry[:, d, j, :], scalar=dec[:, j, d, t:t + 1],
                                                               in1=bank(7)[:, j * 129:(j + 1) * 129], op0=ALU.mult, op1=ALU.add)
                                if j == 0:
                                    own(ins)
                            ins.then_inc(s["carry"], 1)
                        dve.wait_ge(s["out"], u + 1)
                        o = psum[:, 3:5, 0:258]
                        nv = num.rearrange("p r j e -> p r (j e)")
                        if t == PT:
                            own.link(dve.tensor_copy(nv, o))
                        else:
                            n_inter += 1
                            dve.wait_ge(s["inter"], n_inter)
                            own.link(dve.tensor_tensor(nv, its.rearrange("p r j e -> p r (j e)"), o, ALU.add))
                        dve.sem_inc(s["num"], 1)
                        d4 = num[:, :, :, AV]
                        dn4 = dn.rearrange("p (r j) -> p r j", r=2)
                        dn24 = dn2.rearrange("p (r j) -> p r j", r=2)
                        own.link(dve.tensor_scalar(dn4, d4, -1.0, None, ALU.mult))
                        own.link(dve.tensor_tensor(dn4, dn4, d4, ALU.max))
                        own.link(dve.tensor_tensor(dn24, dn4, cols[:, 2, d, t, :].rearrange("p (j r) -> p r j", r=2), ALU.max))
                        own.link(dve.reciprocal(dn, dn2))
                        for i in range(4):
                            r, j = i // 2, i % 2
                            h = 2 * j + r
                            dst = HA[:, t, h * AV:(h + 1) * AV]
                            if first[t] == u:
                                ins = dve.tensor_scalar(dst, num[:, r, j, 0:AV], dn[:, i:i + 1], None, ALU.mult)
                            else:
                                ins = dve.scalar_tensor_tensor(out=dst, in0=num[:, r, j, 0:AV], scalar=dn[:, i:i + 1], in1=dst,
                                                               op0=ALU.mult, op1=ALU.add)
                            own(ins)
                        dve.wait_ge(s["own"], own.n)

                @block.sync
                def _(sp):
                    sp.wait_ge(s["carry"], len(units))
                    for d in range(2):
                        for r in range(2):
                            sp.dma_start(O[2][0, 0, d, r::2].rearrange("j d e -> d j e"), carryp[r * 64:r * 64 + 64, d, :, 0:AV]).then_inc(s["h"], 16)
                            with nc.allow_non_contiguous_dma(reason="words"):
                                sp.dma_start(O[3][0, 0, d, r::2].rearrange("j (d e) -> d j e", e=1), carryp[r * 64:r * 64 + 64, d, :, AV:AV + 1]).then_inc(s["h"], 16)
                        with nc.allow_non_contiguous_dma(reason="words"):
                            sp.dma_start(O[4][0, 0, d].rearrange("(h e) -> h e", e=1), mn[:, d, PT:PT + 1]).then_inc(s["h"], 16)
                    sp.wait_ge(s["h"], 16 * 10)

        def attention(name, heads, scale, q_of, k_of, v_of, out_of, tmp):
            s = {n: sem(f"{name}_{n}") for n in ("s", "max", "p", "t", "c0", "c1", "o", "r", "out", "own")}
            Pb, PTb = tmp(2, NT), tmp(2, NT)
            mx, nb, rsum, rr = (small[:, 200 + 8 * i:202 + 8 * i] for i in range(4))
            units = [(h, t) for h in range(heads) for t in range(TILES)]
            nk = [TILES if t < ST else 1 for _, t in units]
            N = len(units)

            with nc.Block(name) as block:
                @block.tensor
                def _(pe):
                    for i in range(N + 2):
                        if i < N:
                            h, t = units[i]
                            b = 2 * (i % 2)
                            if i >= 2:
                                pe.wait_ge(s["p"], i - 1)
                            k = k_of(h, t)
                            w = k.shape[1]
                            for lo in range(0, w, 512):
                                hi = min(w, lo + 512)
                                mm = pe.matmul(psum[:, b + lo // 512, 0:hi - lo], q_of(h, t), k[:, lo:hi], start=True, stop=True)
                            mm.then_inc(s["s"], 1)
                        if 1 <= i <= N:
                            u = i - 1
                            pe.wait_ge(s["p"], u + 1)
                            if u >= 1:
                                pe.wait_ge(s["c0"], u)
                                pe.wait_ge(s["c1"], u)
                            for j in range(nk[u]):
                                mm = pe.transpose(psum[:, 4 + j // 4, (j % 4) * P:(j % 4 + 1) * P], Pb[:, u % 2, j * P:(j + 1) * P], ident[:, :])
                            mm.then_inc(s["t"], 1)
                        if i >= 2:
                            u = i - 2
                            h, t = units[u]
                            pe.wait_ge(s["c0"], u + 1)
                            pe.wait_ge(s["c1"], u + 1)
                            if u >= 2:
                                pe.wait_ge(s["out"], u - 1)
                            for j in range(nk[u]):
                                mm = pe.matmul(psum[:, 6 + u % 2, 0:64], PTb[:, u % 2, j * P:(j + 1) * P], v_of(h, t, j),
                                               start=(j == 0), stop=(j == nk[u] - 1))
                            mm.then_inc(s["o"], 1)

                def scores(u):
                    b = 2 * (u % 2)
                    return psum[:, b:b + 2, :].rearrange("p a n -> p (a n)")[:, 0:nk[u] * P]

                @block.vector
                def _(dve):
                    own = Steps(dve, s["own"])
                    for i in range(N + 2):
                        if i < N:
                            dve.wait_ge(s["s"], i + 1)
                            own.link(dve.tensor_reduce(mx[:, i % 2:i % 2 + 1], scores(i), AX.X, ALU.max))
                            if i >= 2:
                                dve.wait_ge(s["p"], i - 1)
                            dve.tensor_scalar(nb[:, i % 2:i % 2 + 1], mx[:, i % 2:i % 2 + 1], -scale, None, ALU.mult).then_inc(s["max"], 1)
                        if 1 <= i <= N:
                            u = i - 1
                            dve.wait_ge(s["t"], u + 1)
                            if u >= 2:
                                dve.wait_ge(s["o"], u - 1)
                            w = min(nk[u], 4) * P
                            dve.tensor_copy(PTb[:, u % 2, 0:w], psum[:, 4, 0:w]).then_inc(s["c0"], 1)
                            own.link(dve.reciprocal(rr[:, u % 2:u % 2 + 1], rsum[:, u % 2:u % 2 + 1]))
                        if i >= 2:
                            u = i - 2
                            dve.wait_ge(s["o"], u + 1)
                            dve.tensor_scalar(out_of(*units[u]), psum[:, 6 + u % 2, 0:64], rr[:, u % 2:u % 2 + 1], None, ALU.mult).then_inc(s["out"], 1)

                @block.scalar
                def _(act):
                    for i in range(N + 1):
                        if i < N:
                            act.wait_ge(s["max"], i + 1)
                            if i >= 2:
                                act.wait_ge(s["t"], i - 1)
                                act.wait_ge(s["out"], i - 1)
                            act.activation(Pb[:, i % 2, 0:nk[i] * P], scores(i), ACT.Exp, bias=nb[:, i % 2:i % 2 + 1], scale=scale,
                                           accum_out=rsum[:, i % 2:i % 2 + 1]).then_inc(s["p"], 1)
                        if i >= 1:
                            u = i - 1
                            act.wait_ge(s["t"], u + 1)
                            if u >= 2:
                                act.wait_ge(s["o"], u - 1)
                            if nk[u] > 4:
                                act.activation(PTb[:, u % 2, 4 * P:5 * P], psum[:, 5, 0:P], ACT.Copy).then_inc(s["c1"], 1)
                            else:
                                act.sem_inc(s["c1"], 1)

        def mix_even():
            s = {n: sem("mx_" + n) for n in ("w", "sq", "act", "ssq", "root", "sig", "own", "ready", "turned", "copied")}
            s2 = Carve(ringf, EVEN_TOP)
            HA = proj[:, :, C_VA:C_VA + 512]
            w = s2(512)
            sq = Carve(ringf, 0)(TILES, 512)
            ssq, rs = small[:, 0:20], small[:, 32:52]
            with nc.Block("mix_even") as block:
                @block.sync
                def _(sp):
                    sp.dma_start(w, A["mlstm_norm_w"].to_broadcast([P, 512])).then_inc(s["w"], 16)

                @block.scalar
                def _(act):
                    act.activation(sq, HA, ACT.Square).then_inc(s["sq"], 1)
                    act.activation(proj[:, :, C_OA:C_OA + 512], proj[:, :, C_OA:C_OA + 512], ACT.Sigmoid).then_inc(s["sig"], 1)
                    act.wait_ge(s["ssq"], 1)
                    act.activation(rs, ssq, ACT.Sqrt, scale=1.0 / AV, bias=EPS).then_inc(s["root"], 1)
                    for n in range(2 * TILES):
                        act.wait_ge(s["turned"], n + 1)
                        t, h = n // 2, n % 2
                        act.activation(xT[:, 4 * h:4 * h + 4, t * P:(t + 1) * P], bank(n % 4).rearrange("p (k c) -> p k c", k=4), ACT.Copy).then_inc(s["copied"], 1)

                @block.vector
                def _(dve):
                    own = Steps(dve, s["own"])
                    dve.wait_ge(s["sq"], 1)
                    dve.tensor_reduce(ssq.rearrange("p (t h) -> p t h", t=TILES), sq.rearrange("p t (h d) -> p t h d", d=AV), AX.X, ALU.add).then_inc(s["ssq"], 1)
                    dve.wait_ge(s["root"], 1)
                    own.link(dve.reciprocal(rs, rs))
                    dve.wait_ge(s["w"], 16)
                    dve.wait_ge(s["sig"], 1)
                    for t in range(TILES):
                        h3 = HA[:, t].rearrange("p (h d) -> p h d", d=AV)
                        own.link(dve.tensor_tensor(h3, h3, rs[:, 4 * t:4 * t + 4].unsqueeze(2).to_broadcast([P, AH, AV]), ALU.mult))
                        own.link(dve.tensor_tensor(HA[:, t], HA[:, t], w, ALU.mult))
                        dve.tensor_tensor(HA[:, t], HA[:, t], proj[:, t, C_OA:C_OA + 512], ALU.mult).then_inc(s["ready"], 1)

                @block.tensor
                def _(pe):
                    for n in range(2 * TILES):
                        t, h = n // 2, n % 2
                        if h:
                            pe.wait_ge(s["ready"], t + 1)
                        if n >= 4:
                            pe.wait_ge(s["copied"], n - 3)
                        c0 = C_VA if h else 0
                        for k in range(4):
                            mm = pe.transpose(bank(n % 4)[:, k * P:(k + 1) * P], proj[:, t, c0 + k * P:c0 + (k + 1) * P], ident[:, :])
                        mm.then_inc(s["turned"], 1)

        idx = sb("idx", [CAP, NE], I32)
        gate = sb("gate", [CAP, NE])

        def out_and_route(l, w_out):
            s = {n: sem(f"o{l}_{n}") for n in ("w", "mods", "mm", "gx", "x", "sq", "xst", "root", "own", "sc", "xm", "turned", "copied",
                                              "lg", "mx", "ex", "sm", "aff", "affT", "top", "it", "st", "row0", "row1")}
            wv = ringf[:, 0:2 * 4096].rearrange("p (k n) -> p k n", k=KD)
            cs = Carve(projf)
            mods, nw = cs(2, 2, D), cs(D)
            xm, junk = cs(2, D), cs(D)
            rw = cs(KD, NE)
            g = cs(512)
            affT = cs(NT)
            vals, idxf = cs(CAP), cs(CAP)
            idxu = cs(CAP)
            soft = cs(TILES, NE)
            ssq, rstd, mxs, sums = small[:, 0:5], small[:, 8:13], small[:, 16:21], small[:, 24:29]
            iu = idxu.bitcast(U32)
            with nc.Block(f"out_{l}") as block:
                @block.sync
                def _(sp):
                    sp.dma_start(wv, w_out.rearrange("(k p) n -> p k n", p=P)).then_inc(s["w"], 16)
                    for cond in range(2):
                        for j in range(2):
                            sp.dma_start(mods[:, cond, j, :], mod_rows[l, cond:cond + 1, (3 + j) * D:(4 + j) * D].to_broadcast([P, D])).then_inc(s["mods"], 16)
                    sp.dma_start(nw, A["norm2_w"][l:l + 1, :].to_broadcast([P, D])).then_inc(s["mods"], 16)
                    with nc.allow_non_contiguous_dma(reason="64-byte rows"):
                        sp.dma_start(rw, A["router_w"][l].rearrange("(k p) e -> p k e", p=P)).then_inc(s["mods"], 16)
                    for t in range(TILES):
                        sp.wait_ge(s["x"], 2 * (t + 1))
                        sp.dma_start(x_rows[t * P:(t + 1) * P, :], xr[:, t, :]).then_inc(s["st"], 16)
                    for t in range(TILES):
                        sp.wait_ge(s["xm"], t + 1)
                        sp.dma_start(xm_rows[t * P:(t + 1) * P, :], xm[:, t % 2, :]).then_inc(s[f"row{t % 2}"], 16)
                    sp.wait_ge(s["st"], 16 * TILES)
                    sp.wait_ge(s["row0"], 16 * 3)
                    sp.wait_ge(s["row1"], 16 * 2)

                def logits(pe, t):
                    pe.wait_ge(s["copied"], 2 * t + 2)
                    for k in range(KD):
                        mm = pe.matmul(bank(7)[:, t * NE:(t + 1) * NE], xT[:, k, t * P:(t + 1) * P], rw[:, k, :], start=(k == 0), stop=(k == KD - 1))
                    mm.then_inc(s["lg"], 1)

                @block.tensor
                def _(pe):
                    pe.wait_ge(s["w"], 16)
                    for u in range(2 * TILES):
                        t, h = u // 2, u % 2
                        if u >= 4:
                            pe.wait_ge(s["gx"], u - 3)
                        for k in range(KD):
                            mm = pe.matmul(bank(u % 4), xT[:, k, t * P:(t + 1) * P], wv[:, k, h * 512:(h + 1) * 512], start=(k == 0), stop=(k == KD - 1))
                        mm.then_inc(s["mm"], 1)
                    pe.wait_ge(s["mods"], 16 * 6)
                    for t in range(TILES):
                        pe.wait_ge(s["xm"], t + 1)
                        for h in range(2):
                            if t >= 1:
                                pe.wait_ge(s["copied"], 2 * (t - 1) + h + 1)
                            for k in range(4):
                                mm = pe.transpose(bank(4 + h)[:, k * P:(k + 1) * P], xm[:, t % 2, (4 * h + k) * P:(4 * h + k + 1) * P], ident[:, :])
                            mm.then_inc(s["turned"], 1)
                        if t >= 1:
                            logits(pe, t - 1)
                    logits(pe, TILES - 1)
                    for t in range(TILES):
                        pe.wait_ge(s["aff"], 1)
                        mm = pe.transpose(psum[0:NE, 6 + (t // 4), (t % 4) * P:(t % 4 + 1) * P], soft[:, t, :], ident[:, :])
                    mm.then_inc(s["affT"], 1)
                    pe.wait_ge(s["top"], 1)
                    pe.transpose(bank(4)[0:CAP, 0:NE], idxf[0:NE, :], ident[0:NE, 0:NE])
                    pe.transpose(bank(4)[0:CAP, NE:2 * NE], vals[0:NE, :], ident[0:NE, 0:NE]).then_inc(s["it"], 1)

                @block.vector
                def _(dve):
                    own = Steps(dve, s["own"])
                    for u in range(2 * TILES):
                        t, h = u // 2, u % 2
                        dve.wait_ge(s["mm"], u + 1)
                        dve.tensor_tensor(g, bank(u % 4), hold[:, t // ST, h * 512:(h + 1) * 512], ALU.mult).then_inc(s["gx"], 1)
                        dve.wait_ge(s["gx"], u + 1)
                        dve.tensor_tensor(xr[:, t, h * 512:(h + 1) * 512], xr[:, t, h * 512:(h + 1) * 512], g, ALU.add).then_inc(s["x"], 1)
                        dve.wait_ge(s["x"], u + 1)
                    dve.wait_ge(s["mods"], 16 * 6)
                    for cond in range(2):
                        own(dve.scalar_tensor_tensor(out=mods[:, cond, 1, :], in0=mods[:, cond, 1, :], scalar=1.0, in1=nw, op0=ALU.add, op1=ALU.mult))
                    dve.wait_ge(s["root"], 1)
                    own.link(dve.reciprocal(rstd, rstd))
                    for t in range(TILES):
                        if t >= 2:
                            dve.wait_ge(s["turned"], 2 * (t - 1))
                            dve.wait_ge(s[f"row{t % 2}"], 16 * (t // 2))
                        own.link(dve.scalar_tensor_tensor(out=xm[:, t % 2, :], in0=xr[:, t, :], scalar=rstd[:, t:t + 1], in1=mods[:, t // ST, 1, :],
                                                     op0=ALU.mult, op1=ALU.mult))
                        dve.tensor_tensor(xm[:, t % 2, :], xm[:, t % 2, :], mods[:, t // ST, 0, :], ALU.add).then_inc(s["xm"], 1)
                        dve.wait_ge(s["xm"], t + 1)
                    lg = bank(7)[:, 0:TILES * NE].rearrange("p (t e) -> p t e", e=NE)
                    dve.wait_ge(s["lg"], TILES)
                    own.link(dve.tensor_reduce(mxs, lg, AX.X, ALU.max))
                    dve.tensor_tensor(soft, lg, mxs.unsqueeze(2).to_broadcast([P, TILES, NE]), ALU.subtract).then_inc(s["mx"], 1)
                    dve.wait_ge(s["ex"], 1)
                    own.link(dve.tensor_reduce(sums, soft, AX.X, ALU.add))
                    own.link(dve.reciprocal(sums, sums))
                    dve.tensor_tensor(soft, soft, sums.unsqueeze(2).to_broadcast([P, TILES, NE]), ALU.mult).then_inc(s["aff"], 1)
                    dve.wait_ge(s["affT"], 1)
                    own(dve.tensor_copy(affT[0:NE, 0:512], psum[0:NE, 6, :]))
                    own.link(dve.tensor_copy(affT[0:NE, 512:640], psum[0:NE, 7, 0:P]))
                    for lo, n, at, cap in ((0, NS, 0, CAPS), (NS, NP, CAPS, CAPP)):
                        a = affT[0:NE, lo:lo + n]
                        for r in range(cap // 8):
                            v8 = vals[0:NE, at + 8 * r:at + 8 * r + 8]
                            own.link(dve.max(v8, a))
                            own.link(dve.max_index(iu[0:NE, at + 8 * r:at + 8 * r + 8], v8, a))
                            own.link(dve.match_replace(a, v8, a, -1.0))
                    own.link(dve.tensor_copy(idxf[0:NE, :], iu[0:NE, :]))
                    own.link(dve.tensor_scalar(idxf[0:NE, CAPS:CAP], idxf[0:NE, CAPS:CAP], float(NS), None, ALU.add))
                    dve.sem_inc(s["top"], 1)
                    dve.wait_ge(s["it"], 1)
                    own(dve.tensor_copy(idx[:, :], bank(4)[0:CAP, 0:NE]))
                    own(dve.tensor_copy(gate[:, :], bank(4)[0:CAP, NE:2 * NE]))

                @block.scalar
                def _(act):
                    for t in range(TILES):
                        act.wait_ge(s["x"], 2 * (t + 1))
                        act.activation(junk, xr[:, t, :], ACT.Square, accum_out=ssq[:, t:t + 1]).then_inc(s["sq"], 1)
                        act.wait_ge(s["sq"], t + 1)
                    act.activation(rstd, ssq, ACT.Sqrt, scale=1.0 / D, bias=EPS).then_inc(s["root"], 1)
                    for n in range(2 * TILES):
                        act.wait_ge(s["turned"], n + 1)
                        t, h = n // 2, n % 2
                        if n == 0:
                            act.wait_ge(s["mm"], 2 * TILES)
                        act.activation(xT[:, 4 * h:4 * h + 4, t * P:(t + 1) * P], bank(4 + h).rearrange("p (k c) -> p k c", k=4), ACT.Copy).then_inc(s["copied"], 1)
                    act.wait_ge(s["mx"], 1)
                    act.activation(soft, soft, ACT.Exp).then_inc(s["ex"], 1)

        def experts(l):
            s = {n: sem(f"x{l}_{n}") for n in ("g2", "idx", "gcol", "gat0", "gat1", "go", "xT", "xC", "hg", "hu", "hs", "hid", "y", "yw", "ye",
                                              "yed", "wg0", "wg1", "wu0", "wu1", "wd0", "wd1", "idxd", "sc")}
            cs = Carve(projf)
            g2 = cs(D)
            xg = cs(2, D)
            ye = cs(2, D)
            tmp = cs(D)
            sg = cs(FB * CAP)
            hid = cs(2, FB, CAP)
            xgT = cs(2, KD, CAP)
            gc = cs(2)
            ic = sb(f"ic{l}", [CAP, 2], I32)
            wslot = [[ring[:, 3 * q + i, :] for i in range(3)] for q in range(2)]

            def wait(eng, sm, e, back, per=1):
                if isinstance(e, int):
                    if e - back + 1 > 0:
                        eng.wait_ge(sm, (e - back + 1) * per)
                else:
                    eng.wait_ge(sm, (e - back + 1) * per)

            with nc.Block(f"experts_{l}") as block:
                def pairs(eng, body):
                    body(0)
                    with eng.Fori(1, NE // 2 - 1) as i:
                        body(i)
                    body(NE // 2 - 1)

                @block.sync
                def _(sp):
                    for cond, lo, hi in ((0, 0, CAPS), (1, CAPS, CAP)):
                        sp.dma_start(g2[lo:hi, :], mod_rows[l, cond:cond + 1, 5 * D:6 * D].to_broadcast([hi - lo, D])).then_inc(s["g2"], 16)

                    def body(i):
                        for q in range(2):
                            e = 2 * i + q
                            first = isinstance(i, int) and i == 0
                            for n, (nm, wn, done) in enumerate((("wg", "exp_w_gate", "hg"), ("wu", "exp_w_up", "hu"), ("wd", "exp_w_down", "y"))):
                                if not first:
                                    sp.wait_ge(s[done], 2 * i + q - 1)
                                src = A[wn][l][bass.ds(e, 1)].rearrange("a (k p) n -> p (a k) n", p=P)
                                k = KD if n < 2 else FB
                                sp.dma_start(wslot[q][n].rearrange("p (k n) -> p k n", k=k), src).then_inc(s[f"{nm}{q}"], 16)
                    pairs(sp, body)

                @block.gpsimd
                def _(pool):
                    def gather(e, q, first):
                        if not first:
                            pool.wait_ge(s["sc"], 16 * (e - 1))
                        pool.tensor_copy(ic[:, q:q + 1], idx[:, bass.ds(e, 1)]).then_inc(s["idx"], 1)
                        pool.wait_ge(s["idx"], e + 1)
                        if not first:
                            pool.wait_ge(s["xT"], e - 1)
                        pool.sem_inc(s["go"], 1)
                        pool.indirect_dma_start(xg[0:CAP, q, :], None, xm_rows, bass.IndirectOffsetOnAxis(ap=ic[:, q:q + 1], axis=0)).then_inc(s[f"gat{q}"], 16)

                    def scatter(e, q):
                        pool.wait_ge(s["ye"], e + 1)
                        pool.sem_inc(s["go"], 1)
                        pool.indirect_dma_start(x_rows, bass.IndirectOffsetOnAxis(ap=ic[:, q:q + 1], axis=0), ye[0:CAP, q, :], None,
                                                compute_op=ALU.add).then_inc(s["sc"], 16)
                        pool.wait_ge(s["sc"], 16 * (e + 1))

                    gather(0, 0, True)
                    gather(1, 1, True)

                    def body(i):
                        last = isinstance(i, int) and i == NE // 2 - 1
                        for q in range(2):
                            scatter(2 * i + q, q)
                            if not last:
                                gather(2 * i + q + 2, q, False)
                    pairs(pool, body)

                @block.tensor
                def _(pe):
                    def turn(e, q, n, first):
                        pe.wait_ge(s[f"gat{q}"], 16 * n)
                        if not first:
                            pe.wait_ge(s["xC"], 2 * e)
                        for h in range(2):
                            for k in range(4):
                                mm = pe.transpose(bank(h)[:, k * CAP:(k + 1) * CAP], xg[0:CAP, q, (4 * h + k) * P:(4 * h + k + 1) * P], ident[0:CAP, 0:CAP])
                        mm.then_inc(s["xT"], 1)

                    turn(0, 0, 1, True)

                    def body(i):
                        static = isinstance(i, int)
                        for q in range(2):
                            e = 2 * i + q
                            first = static and e == 0
                            last = static and e == NE - 1
                            pe.wait_ge(s["xC"], 2 * e + 2)
                            for n, (nm, done) in enumerate((("wg", "hg"), ("wu", "hu"))):
                                pe.wait_ge(s[f"{nm}{q}"], 16 * (i + 1))
                                if not first:
                                    pe.wait_ge(s["hs" if n == 0 else "hid"], e)
                                w = wslot[q][n].rearrange("p (k n) -> p k n", k=KD)
                                for f in range(FB):
                                    for k in range(KD):
                                        mm = pe.matmul(bank(2 + n)[:, f * CAP:(f + 1) * CAP], w[:, k, f * P:(f + 1) * P], xgT[:, q, k, :],
                                                       start=(k == 0), stop=(k == KD - 1))
                                mm.then_inc(s[done], 1)
                            if not last:
                                turn(e + 1, 1 - q, i + 1 + q, False)
                            pe.wait_ge(s["hid"], e + 1)
                            pe.wait_ge(s[f"wd{q}"], 16 * (i + 1))
                            if not first:
                                pe.wait_ge(s["yw"], 2 * e)
                            w = wslot[q][2].rearrange("p (k n) -> p k n", k=FB)
                            for h in range(2):
                                for f in range(FB):
                                    mm = pe.matmul(bank(4 + h)[0:CAP, :], hid[:, q, f, :], w[:, f, h * 512:(h + 1) * 512], start=(f == 0), stop=(f == FB - 1))
                            mm.then_inc(s["y"], 1)
                    pairs(pe, body)

                @block.scalar
                def _(act):
                    def turn_copy(e, q, first):
                        act.wait_ge(s["xT"], e + 1)
                        if not first:
                            act.wait_ge(s["hu"], e - 1)
                        act.activation(xgT[:, q, 0:4, :], bank(0)[:, 0:4 * CAP].rearrange("p (k c) -> p k c", k=4), ACT.Copy).then_inc(s["xC"], 1)
                        act.activation(xgT[:, q, 4:8, :], bank(1)[:, 0:4 * CAP].rearrange("p (k c) -> p k c", k=4), ACT.Copy).then_inc(s["xC"], 1)
                    turn_copy(0, 0, True)

                    def body(i):
                        static = isinstance(i, int)
                        for q in range(2):
                            e = 2 * i + q
                            first = static and e == 0
                            act.wait_ge(s["hg"], e + 1)
                            if not first:
                                act.wait_ge(s["hid"], e)
                            act.activation(sg, bank(2)[:, 0:FB * CAP], ACT.Silu).then_inc(s["hs"], 1)
                            if not (static and e == NE - 1):
                                turn_copy(e + 1, 1 - q, first)
                    pairs(act, body)

                @block.vector
                def _(dve):
                    dve.wait_ge(s["g2"], 32)

                    def body(i):
                        static = isinstance(i, int)
                        for q in range(2):
                            e = 2 * i + q
                            first2 = static and i == 0
                            if not first2:
                                dve.wait_ge(s["ye"], e - 1)
                            dve.tensor_copy(gc[0:CAP, q:q + 1], gate[:, bass.ds(e, 1)]).then_inc(s["gcol"], 1)
                            dve.wait_ge(s["gcol"], e + 1)
                            dve.wait_ge(s["hs"], e + 1)
                            dve.wait_ge(s["hu"], e + 1)
                            if not first2:
                                dve.wait_ge(s["y"], e - 1)
                            dve.tensor_tensor(hid[:, q].rearrange("p f c -> p (f c)"), sg, bank(3)[:, 0:FB * CAP], ALU.mult).then_inc(s["hid"], 1)
                            dve.wait_ge(s["y"], e + 1)
                            if not first2:
                                dve.wait_ge(s["sc"], 16 * (e - 1))
                            for h in range(2):
                                dve.scalar_tensor_tensor(out=ye[0:CAP, q, h * 512:(h + 1) * 512], in0=bank(4 + h)[0:CAP, :], scalar=gc[0:CAP, q:q + 1],
                                                         in1=g2[0:CAP, h * 512:(h + 1) * 512], op0=ALU.mult, op1=ALU.mult).then_inc(s["yw"], 1)
                            dve.wait_ge(s["yw"], 2 * e + 2)
                            dve.sem_inc(s["ye"], 1)
                    pairs(dve, body)

        pc = Carve(projf)
        po = pc(TILES, ODD_TOK)
        XL = NT + 6
        XS, XPR = 2, NS + 5
        xp = pc(4, XL)
        xg = pc(4, NT)
        rgbd = pc(16, P)
        ODD_CUTS = [(0, 512), (512, ODD_TOK - 512), (ODD_TOK, 512), (ODD_TOK + 512, 512)]
        odd_w = [(ring[:, i, 0:KD * n].rearrange("p (k n) -> p k n", k=KD),
                  A["od_w_in"][0, :, c:c + n].rearrange("(k p) n -> p k n", p=P)) for i, (c, n) in enumerate(ODD_CUTS)]

        def project_odd(w_sem):
            s_mm, s_act, s_dve, s_z = sem("po_mm"), sem("po_act"), sem("po_dve"), sem("po_zero")
            units = []
            for i in range(2):
                c, n = ODD_CUTS[i]
                for t in range(TILES):
                    units.append(([xT[:, k, t * P:(t + 1) * P] for k in range(KD)], [odd_w[i][0][:, k, :] for k in range(KD)], n, po[:, t, c:c + n]))
            for f in range(8):
                w = odd_w[2 + f // 4][0]
                for lo, n in ((0, NS), (NS, NP)):
                    dst = xp[:, f, (XS if lo == 0 else XPR):(XS if lo == 0 else XPR) + n] if f < 4 else xg[:, f - 4, lo:lo + n]
                    units.append(([w[:, k, (f % 4) * P:(f % 4 + 1) * P] for k in range(KD)], [xT[:, k, lo:lo + n] for k in range(KD)], n, dst))
            with nc.Block("project_odd") as block:
                @block.tensor
                def _(pe):
                    pe.wait_ge(w_sem, 16 * len(ODD_CUTS))
                    for u, (st, mv, n, _) in enumerate(units):
                        if u >= 8:
                            pe.wait_ge(s_act if u % 2 == 0 else s_dve, (u - 8) // 2 + 1)
                        for k in range(KD):
                            mm = pe.matmul(bank(u % 8, n), st[k], mv[k], start=(k == 0), stop=(k == KD - 1))
                        mm.then_inc(s_mm, 1)

                @block.gpsimd
                def _(pool):
                    for lo, hi in ((0, XS), (XS + NS, XPR), (XPR + NP, XL)):
                        pool.memset(xp[:, :, lo:hi], 0.0).then_inc(s_z, 1)
                    pool.memset(rgbd, 0.0).then_inc(s_z, 1)

                @block.scalar
                def _(act):
                    for u, (_, _, n, dst) in enumerate(units):
                        if u % 2 == 0:
                            act.wait_ge(s_mm, u + 1)
                            act.activation(dst, bank(u % 8, n), ACT.Copy).then_inc(s_act, 1)

                @block.vector
                def _(dve):
                    for u, (_, _, n, dst) in enumerate(units):
                        if u % 2:
                            dve.wait_ge(s_mm, u + 1)
                            dve.tensor_copy(dst, bank(u % 8, n)).then_inc(s_dve, 1)

        oc = Carve(ringf)
        kT2 = oc(CH, NT + P)
        v2 = oc(TILES + 1, CH * CV)
        ODD_TOP = oc.at
        qT2 = xT[:, :, :]

        def prepare_odd():
            s = {n: sem("od_" + n) for n in ("in", "ckc", "sq", "root", "own", "norm", "rotk", "t", "tc", "mm", "mc", "ck", "krc", "kr", "krd",
                                             "qmm", "qc", "rotq", "q2", "qt", "qtc", "out", "vm")}
            cs = Carve(ringf, ODD_TOP)
            cqT, ckvT = cs(3, NT), cs(2, NT + P)
            Q = cs(TILES, CH * CQK)
            wuq = cs(3, CH * CQK)
            wkn, wv = cs(2, CH * CNOPE), cs(2, CH * CV)
            tabs = cs(ST, 2, CROPE)
            nq, nkv = cs(CQL), cs(CKVL)
            ra, rb = cs(ST, CH * CROPE), cs(ST, CH * CROPE)
            ck_rows = rb[:, 0, :]
            kr_rows = ra[:, 0, 0:CROPE]
            junk = rb[:, 1:3, :].rearrange("p a b -> p (a b)")
            ssq, rs = small[:, 0:10], small[:, 16:26]
            krot = small[:, 32:32 + 2 * ST * CROPE].rearrange("p (a t d) -> p a t d", a=2, t=ST)
            LOADS = 16 * 10
            KR0 = CQL + CKVL

            def quarters(x, lead):
                return x.rearrange(f"p {lead} (a u i) -> p {lead} a u i", a=2, u=2)

            with nc.Block("prepare_odd") as block:
                @block.sync
                def _(sp):
                    sp.dma_start(wuq, A["mla_w_uq"][0].rearrange("(k p) n -> p k n", p=P)).then_inc(s["in"], 16)
                    u4 = A["mla_w_ukv"][0].rearrange("(k p) (h u d) -> k u p h d", p=P, u=2, d=CNOPE)
                    for k in range(2):
                        sp.dma_start(wkn[:, k, :].rearrange("p (h d) -> p h d", d=CNOPE), u4[k, 0]).then_inc(s["in"], 16)
                        sp.dma_start(wv[:, k, :].rearrange("p (h d) -> p h d", d=CV), u4[k, 1]).then_inc(s["in"], 16)
                    for dst, src in [(tabs, A["rope_c"]), (nq, A["mla_q_norm"].to_broadcast([P, CQL])), (nkv, A["mla_kv_norm"].to_broadcast([P, CKVL])),
                                     (ck_rows, A["cache_mla_ckv"][0, 0]), (kr_rows, A["cache_mla_krope"][0, 0])]:
                        sp.dma_start(dst, src).then_inc(s["in"], 16)
                    for d in range(2):
                        for kind, nm in enumerate(("rg_wa", "rg_wx")):
                            for r in range(2):
                                b4 = rgbd.rearrange("p (d w f) n -> p d w f n", d=2, w=2)
                                sp.dma_start(b4[r * 64:r * 64 + 64, d, kind, :, r * 64:r * 64 + 64],
                                             A[nm][0, d].rearrange("(f r) a b -> r a f b", r=2)[r]).then_inc(s["out"], 16)
                    sp.wait_ge(s["norm"], TILES)
                    sp.dma_start(O[7][0, 0], po[:, PT, CQL:CQL + CKVL]).then_inc(s["out"], 16)
                    sp.dma_start(O[8][0, 0], po[:, PT, KR0:KR0 + CROPE]).then_inc(s["out"], 16)
                    sp.wait_ge(s["out"], 16 * 10)

                @block.scalar
                def _(act):
                    own = Steps(act, s["sq"])
                    act.wait_ge(s["t"], 1)
                    for t in range(TILES):
                        own.link(act.activation(junk[:, 0:CQL], po[:, t, 0:CQL], ACT.Square, scale=CQL ** -0.5, accum_out=ssq[:, 2 * t:2 * t + 1]))
                        own.link(act.activation(junk[:, 0:CKVL], po[:, t, CQL:CQL + CKVL], ACT.Square, scale=CKVL ** -0.5, accum_out=ssq[:, 2 * t + 1:2 * t + 2]))
                    act.activation(rs, ssq, ACT.Sqrt, bias=EPS).then_inc(s["root"], 1)
                    act.activation(ckvT[:, :, 0:P], bank(0, 256).rearrange("p (k c) -> p k c", k=2), ACT.Copy).then_inc(s["tc"], 1)
                    act.activation(kT2[64:96, 0, 0:P], psum[0:32, 0, 256:256 + P], ACT.Copy).then_inc(s["krc"], 1)
                    for t in range(TILES):
                        b = 1 + t % 2
                        act.wait_ge(s["t"], t + 2)
                        act.activation(cqT[:, :, t * P:(t + 1) * P], bank(b, 384).rearrange("p (k c) -> p k c", k=3), ACT.Copy).then_inc(s["tc"], 1)
                        act.activation(ckvT[:, :, (t + 1) * P:(t + 2) * P], bank(2 + b, 256).rearrange("p (k c) -> p k c", k=2), ACT.Copy).then_inc(s["tc"], 1)
                        act.activation(kT2[64:96, 0, (t + 1) * P:(t + 2) * P], psum[0:32, 2 + b, 256:256 + P], ACT.Copy).then_inc(s["krc"], 1)
                    for n in range(2 * TILES):
                        act.wait_ge(s["qmm"], n + 1)
                        t, c = n // 2, n % 2
                        act.activation(Q[:, t, c * 384:(c + 1) * 384], bank(5 + n % 2, 384), ACT.Copy).then_inc(s["qc"], 1)
                    for n in range(2 * TILES):
                        act.wait_ge(s["qt"], n + 1)
                        t, c = n // 2, n % 2
                        act.activation(qT2[0:CQK, 4 * c:4 * c + 4, t * P:(t + 1) * P], psum[0:CQK, 5 + n % 2, :].rearrange("p (h c) -> p h c", h=4),
                                       ACT.Copy).then_inc(s["qtc"], 1)

                @block.vector
                def _(dve):
                    own = Steps(dve, s["own"])
                    dve.wait_ge(s["in"], LOADS)
                    dve.wait_ge(s["root"], 1)
                    own.link(dve.reciprocal(rs, rs))
                    kr = po[:, 0:ST, KR0:KR0 + CROPE]
                    own(dve.tensor_tensor(krot[:, 0], kr, tabs[:, :, 0, :], ALU.mult))
                    for u in range(2):
                        own(dve.tensor_tensor(krot[:, 1].rearrange("p t (a u i) -> p t a u i", a=2, u=2)[:, :, :, u, :],
                                              kr.rearrange("p t (a u i) -> p t a u i", a=2, u=2)[:, :, :, 1 - u, :],
                                              tabs[:, :, 1, :].rearrange("p t (a u i) -> p t a u i", a=2, u=2)[:, :, :, u, :], ALU.mult))
                    own.wait()
                    own.link(dve.tensor_tensor(kr, krot[:, 0], krot[:, 1], ALU.add))
                    for t in range(TILES):
                        own(dve.scalar_tensor_tensor(out=po[:, t, 0:CQL], in0=po[:, t, 0:CQL], scalar=rs[:, 2 * t:2 * t + 1], in1=nq, op0=ALU.mult, op1=ALU.mult))
                        own.link(dve.scalar_tensor_tensor(out=po[:, t, CQL:KR0], in0=po[:, t, CQL:KR0], scalar=rs[:, 2 * t + 1:2 * t + 2], in1=nkv, op0=ALU.mult, op1=ALU.mult))
                        dve.sem_inc(s["norm"], 1)
                    for n in range(8):
                        j, c = n // 2, n % 2
                        lo, w = (0, 512) if c == 0 else (512, 256)
                        dve.wait_ge(s["mm"], n + 1)
                        b = 7 if n % 2 else 0
                        own(dve.tensor_copy(kT2[0:64, 2 * j, lo:lo + w], psum[0:64, b, 0:w]))
                        dve.tensor_copy(kT2[0:64, 2 * j + 1, lo:lo + w], psum[64:128, b, 0:w]).then_inc(s["mc"], 1)
                    for n in range(TILES + 1):
                        dve.wait_ge(s["mm"], 8 + n + 1)
                        dve.tensor_copy(v2[:, n, :], bank(7 if n % 2 else 0)).then_inc(s["mc"], 1)
                    for t in range(ST):
                        dve.wait_ge(s["qc"], 2 * t + 2)
                        q3 = Q[:, t, :].rearrange("p (h d) -> p h d", d=CQK)[:, :, CNOPE:CQK]
                        a3 = ra[:, t, :].rearrange("p (h d) -> p h d", d=CROPE)
                        b3 = rb[:, t, :].rearrange("p (h d) -> p h d", d=CROPE)
                        own(dve.tensor_tensor(a3, q3, tabs[:, t, 0:1, :].to_broadcast([P, CH, CROPE]), ALU.mult))
                        sn = tabs[:, t, 1, :].rearrange("p (a u i) -> p a u i", a=2, u=2)
                        for u in range(2):
                            for a in range(2):
                                own(dve.tensor_tensor(quarters(b3, "h")[:, :, a, u, :], quarters(q3, "h")[:, :, a, 1 - u, :],
                                                      sn[:, a, u, :].unsqueeze(1).to_broadcast([P, CH, 8]), ALU.mult))
                        own.wait()
                        dve.tensor_tensor(q3, a3, b3, ALU.add).then_inc(s["q2"], 1)

                @block.gpsimd
                def _(pool):
                    pool.wait_ge(s["krc"], TILES + 1)
                    for h in range(1, CH):
                        pool.tensor_copy(kT2[64:96, h, :], kT2[64:96, 0, :]).then_inc(s["krd"], 1)

                @block.tensor
                def _(pe):
                    pe.wait_ge(s["in"], LOADS)
                    for k in range(2):
                        pe.transpose(bank(0)[:, k * P:(k + 1) * P], ck_rows[:, k * P:(k + 1) * P], ident[:, :])
                    pe.transpose(psum[0:32, 0, 256:256 + P], kr_rows, ident[:, :]).then_inc(s["t"], 1)
                    for t in range(TILES):
                        b = 1 + t % 2
                        pe.wait_ge(s["norm"], t + 1)
                        if t >= 2:
                            pe.wait_ge(s["tc"], 2 * (t - 1) + 1)
                            pe.wait_ge(s["krc"], t)
                        for k in range(3):
                            pe.transpose(bank(b)[:, k * P:(k + 1) * P], po[:, t, k * P:(k + 1) * P], ident[:, :])
                        for k in range(2):
                            pe.transpose(bank(2 + b)[:, k * P:(k + 1) * P], po[:, t, CQL + k * P:CQL + (k + 1) * P], ident[:, :])
                        pe.transpose(psum[0:32, 2 + b, 256:256 + P], po[:, t, KR0:KR0 + CROPE], ident[:, :]).then_inc(s["t"], 1)
                    for n in range(2 * TILES):
                        t, c = n // 2, n % 2
                        pe.wait_ge(s["tc"], 2 * t + 3)
                        if n >= 2:
                            pe.wait_ge(s["qc"], n - 1)
                        for k in range(3):
                            mm = pe.matmul(bank(5 + n % 2, 384), cqT[:, k, t * P:(t + 1) * P], wuq[:, k, c * 384:(c + 1) * 384], start=(k == 0), stop=(k == 2))
                        mm.then_inc(s["qmm"], 1)
                    pe.wait_ge(s["tc"], 2 * TILES + 1)
                    pe.wait_ge(s["krc"], TILES + 1)
                    for n in range(8 + TILES + 1):
                        b = 7 if n % 2 else 0
                        if n >= 2:
                            pe.wait_ge(s["mc"], n - 1)
                        for k in range(2):
                            if n < 8:
                                j, c = n // 2, n % 2
                                lo, w = (0, 512) if c == 0 else (512, 256)
                                mm = pe.matmul(bank(b, w), wkn[:, k, j * P:(j + 1) * P], ckvT[:, k, lo:lo + w], start=(k == 0), stop=(k == 1))
                            else:
                                mm = pe.matmul(bank(b), ckvT[:, k, (n - 8) * P:(n - 7) * P], wv[:, k, :], start=(k == 0), stop=(k == 1))
                        mm.then_inc(s["mm"], 1)
                    for n in range(2 * TILES):
                        t, c = n // 2, n % 2
                        if t < ST:
                            pe.wait_ge(s["q2"], t + 1)
                        pe.wait_ge(s["qc"], 2 * TILES)
                        if n >= 2:
                            pe.wait_ge(s["qtc"], n - 1)
                        for h in range(4):
                            mm = pe.transpose(psum[0:CQK, 5 + n % 2, h * P:(h + 1) * P], Q[:, t, (4 * c + h) * CQK:(4 * c + h + 1) * CQK], ident[:, :])
                        mm.then_inc(s["qt"], 1)

        def recurrence():
            s = {n: sem("rg_" + n) for n in ("in", "t", "prm", "ab", "act", "own", "mm", "sg", "ex", "q", "sqrt", "b", "h", "y", "out", "gelu", "conv", "pool")}
            cs = Carve(ringf)
            XW = XPR + NP - XS
            CW = XW
            CP = XPR - XS
            xc = cs(4, CW)
            R, I = cs(2, 4, CW), cs(2, 4, CW)
            th = cs(2, 4, CW)
            tq = cs(2, CW)
            prow = small[0:52, 0:128]
            prm = small[:, 128:180]
            sp_ = small[:, 192:200]
            e_, z_, z2, p_ = (small[:, 208 + 8 * i:216 + 8 * i] for i in range(4))
            ROWS = [("rg_conv_w", 16), ("rg_conv_b", 4), ("rg_ba", 8), ("rg_bx", 8), ("rg_lambda", 8), ("state_rglru_h", 8)]
            a_of = R
            at = {}
            n = 0
            for nm, c in ROWS:
                at[nm] = n
                n += c

            def prmcol(nm, i):
                return prm[:, at[nm] + i:at[nm] + i + 1]

            spans = ((0, 0, NS), (CP, NS, NP))
            units = [(d, kind, f) for d in range(2) for kind in range(2) for f in range(4)]
            with nc.Block("recurrence") as block:
                @block.sync
                def _(sp):
                    for nm, c in ROWS:
                        a = A[nm]
                        names = {3: "a b (f p) -> (a b f) p", 2: "a (f p) -> (a f) p", 4: "a b c (f p) -> (a b c f) p"}[len(a.shape)]
                        sp.dma_start(prow[at[nm]:at[nm] + c, :], a.rearrange(names, p=P)).then_inc(s["in"], 16)
                    sp.wait_ge(s["h"], 16)
                    for d in range(2):
                        e = CP + NP - 1 if d == 0 else CP
                        with nc.allow_non_contiguous_dma(reason="words"):
                            sp.dma_start(O[9][0, 0, d].rearrange("(f p) -> p f", p=P), th[:, d, :, e]).then_inc(s["out"], 16)
                    sp.wait_ge(s["out"], 32)

                @block.tensor
                def _(pe):
                    pe.wait_ge(s["in"], 16 * 6)
                    pe.transpose(bank(0)[:, 0:52], prow, ident[0:52, 0:52]).then_inc(s["t"], 1)
                    pe.wait_ge(s["prm"], 1)
                    for u, (d, kind, f) in enumerate(units):
                        pe.wait_ge(s["conv"], f + 1)
                        if u >= 4:
                            pe.wait_ge(s["sg"], u - 3)
                        b = 2 * (u % 4)
                        for i, (pl, _, w) in enumerate(spans):
                            mm = pe.matmul(bank(b + i, w), rgbd[:, (d * 2 + kind) * 4 + f, :], xc[:, f, pl:pl + w], start=True, stop=True)
                        mm.then_inc(s["mm"], 1)

                @block.scalar
                def _(act):
                    own = Steps(act, s["act"])
                    act.wait_ge(s["prm"], 1)
                    lam = prm[:, at["rg_lambda"]:at["rg_lambda"] + 8]
                    own.link(act.activation(e_, lam, ACT.Abs))
                    act.activation(e_, e_, ACT.Exp, scale=-1.0).then_inc(s["ab"], 1)
                    for u, (d, kind, f) in enumerate(units):
                        act.wait_ge(s["mm"], u + 1)
                        b = 2 * (u % 4)
                        dst = (R, I)[kind]
                        bias = prmcol(("rg_ba", "rg_bx")[kind], 4 * d + f)
                        own(act.activation(dst[:, d, f, 0:NS], bank(b), ACT.Sigmoid, bias=bias))
                        act.activation(dst[:, d, f, CP:CW], bank(b + 1, NP), ACT.Sigmoid, bias=bias).then_inc(s["sg"], 1)
                    act.wait_ge(s["q"], 1)
                    act.wait_ge(s["sg"], 16)
                    act.wait_ge(s["pool"], 2)
                    own.wait()
                    for d in range(2):
                        for f in range(4):
                            sc = sp_[:, 4 * d + f:4 * d + f + 1]
                            own.link(act.activation(th[:, d, f, :], R[:, d, f, :], ACT.Tanh, scale=sc))
                            act.activation(R[:, d, f, :], R[:, d, f, :], ACT.Exp, scale=sc).then_inc(s["ex"], 1)
                    for n in range(8):
                        act.wait_ge(s["b"], n + 1)
                        act.activation(th[:, n // 4, n % 4, :], th[:, n // 4, n % 4, :], ACT.Sqrt, scale=-1.0).then_inc(s["sqrt"], 1)
                    act.activation(xg, xg, ACT.Gelu_apprx_tanh).then_inc(s["gelu"], 1)

                @block.gpsimd
                def _(pool):
                    pool.memset(R[:, :, :, NS:CP], 0.0).then_inc(s["pool"], 1)
                    pool.memset(I[:, :, :, NS:CP], 0.0).then_inc(s["pool"], 1)
                    pool.wait_ge(s["pool"], 2)
                    for n in range(8):
                        d, f = n // 4, n % 4
                        pool.wait_ge(s["sg"], 8 * d + 4 + f + 1)
                        pool.tensor_tensor(I[:, d, f, :], I[:, d, f, :], xc[:, f, :], ALU.mult).then_inc(s["y"], 1)

                @block.vector
                def _(dve):
                    own = Steps(dve, s["own"])
                    dve.wait_ge(s["t"], 1)
                    dve.tensor_copy(prm, bank(0)[:, 0:52]).then_inc(s["prm"], 1)
                    dve.wait_ge(s["prm"], 1)
                    for f in range(4):
                        own.link(dve.tensor_scalar(xc[:, f, :], xp[:, f, 0:CW], prmcol("rg_conv_w", f), prmcol("rg_conv_b", f), ALU.mult, ALU.add))
                        for w in range(1, 4):
                            own.link(dve.scalar_tensor_tensor(out=xc[:, f, :], in0=xp[:, f, w:w + CW], scalar=prmcol("rg_conv_w", 4 * w + f),
                                                              in1=xc[:, f, :], op0=ALU.mult, op1=ALU.add))
                        dve.sem_inc(s["conv"], 1)
                    dve.wait_ge(s["ab"], 1)
                    own.link(dve.tensor_scalar(z_, e_, 2.0, None, ALU.add))
                    own.link(dve.reciprocal(z_, z_))
                    own.link(dve.tensor_tensor(z_, z_, e_, ALU.mult))
                    own.link(dve.tensor_tensor(z2, z_, z_, ALU.mult))
                    own.link(dve.tensor_scalar(p_, z2, 1.0 / 17, None, ALU.mult))
                    for k in range(15, 1, -2):
                        own.link(dve.scalar_tensor_tensor(out=p_, in0=p_, scalar=1.0 / k, in1=z2, op0=ALU.add, op1=ALU.mult))
                    own.link(dve.scalar_tensor_tensor(out=p_, in0=p_, scalar=1.0, in1=z_, op0=ALU.add, op1=ALU.mult))
                    own.link(dve.tensor_scalar(z2, prm[:, at["rg_lambda"]:at["rg_lambda"] + 8], -1.0, 0.0, ALU.mult, ALU.max))
                    own.link(dve.scalar_tensor_tensor(out=p_, in0=p_, scalar=2.0, in1=z2, op0=ALU.mult, op1=ALU.add))
                    dve.tensor_scalar(sp_, p_, -8.0, None, ALU.mult).then_inc(s["q"], 1)
                    for n in range(8):
                        d, f = n // 4, n % 4
                        dve.wait_ge(s["ex"], n + 1)
                        own.link(dve.tensor_tensor(tq[:, n % 2, :], R[:, d, f, :], R[:, d, f, :], ALU.mult))
                        dve.scalar_tensor_tensor(out=th[:, d, f, :], in0=tq[:, n % 2, :], scalar=1.0, in1=th[:, d, f, :], op0=ALU.add, op1=ALU.mult).then_inc(s["b"], 1)
                    for n in range(8):
                        d, f = n // 4, n % 4
                        dve.wait_ge(s["sqrt"], n + 1)
                        dve.wait_ge(s["y"], n + 1)
                        own.link(dve.tensor_tensor(I[:, d, f, :], I[:, d, f, :], th[:, d, f, :], ALU.mult))
                        for i, (pl, _, w) in enumerate(spans):
                            def run(x):
                                v = x[:, d, f, pl:pl + w]
                                return v if d == 0 else v[:, ::-1]
                            init = prmcol("state_rglru_h", 4 * d + f) if i == 0 else 0.0
                            dve.tensor_tensor_scan(run(th), run(R), run(I), init, ALU.mult, ALU.add).then_inc(s["h"], 1)
                    dve.wait_ge(s["h"], 16)
                    dve.wait_ge(s["gelu"], 1)
                    for f in range(4):
                        for pl, lo, w in spans:
                            own.link(dve.tensor_tensor(xc[:, f, pl:pl + w], th[:, 0, f, pl:pl + w], th[:, 1, f, pl:pl + w], ALU.add))
                            own(dve.tensor_tensor(xg[:, f, lo:lo + w], xg[:, f, lo:lo + w], xc[:, f, pl:pl + w], ALU.mult))

        def mix_odd():
            s = {n: sem("my_" + n) for n in ("turned", "copied", "pool")}
            with nc.Block("mix_odd") as block:
                @block.tensor
                def _(pe):
                    for t in range(TILES):
                        if t >= 2:
                            pe.wait_ge(s["copied"], t - 1)
                        for k in range(4):
                            mm = pe.transpose(bank(t % 2)[:, k * P:(k + 1) * P], po[:, t, k * P:(k + 1) * P], ident[:, :])
                        mm.then_inc(s["turned"], 1)

                @block.scalar
                def _(act):
                    for t in range(TILES):
                        act.wait_ge(s["turned"], t + 1)
                        act.activation(xT[:, 0:4, t * P:(t + 1) * P], bank(t % 2).rearrange("p (k c) -> p k c", k=4), ACT.Copy).then_inc(s["copied"], 1)

                @block.vector
                def _(dve):
                    dve.tensor_copy(xT[:, 4:8, :], xg).then_inc(s["pool"], 1)

        def final_norm():
            s = {n: sem("f_" + n) for n in ("w", "sq", "root", "own", "y", "out")}
            s_x = [sem(f"f_x{t}") for t in range(TILES)]
            cs = Carve(projf)
            nw, junk = cs(D), cs(D)
            ssq, rstd = small[:, 0:TILES], small[:, 8:8 + TILES]
            with nc.Block("final_norm") as block:
                @block.sync
                def _(sp):
                    for t in range(TILES):
                        sp.dma_start(xr[:, t, :], x_rows[t * P:(t + 1) * P, :]).then_inc(s_x[t], 16)
                    sp.dma_start(nw, A["final_norm_w"].rearrange("(a n) -> a n", a=1).to_broadcast([P, D])).then_inc(s["w"], 16)
                    for t in range(TILES):
                        sp.wait_ge(s["y"], t + 1)
                        dst = O[1][0, t * P:(t + 1) * P, :] if t < ST else O[0][0]
                        sp.dma_start(dst, xr[:, t, :]).then_inc(s["out"], 16)
                    sp.wait_ge(s["out"], 16 * TILES)

                @block.scalar
                def _(act):
                    for t in range(TILES):
                        act.wait_ge(s_x[t], 16)
                        act.activation(junk, xr[:, t, :], ACT.Square, accum_out=ssq[:, t:t + 1]).then_inc(s["sq"], 1)
                        act.wait_ge(s["sq"], t + 1)
                    act.activation(rstd, ssq, ACT.Sqrt, scale=1.0 / D, bias=EPS).then_inc(s["root"], 1)

                @block.vector
                def _(dve):
                    own = Steps(dve, s["own"])
                    dve.wait_ge(s["root"], 1)
                    own.link(dve.reciprocal(rstd, rstd))
                    dve.wait_ge(s["w"], 16)
                    for t in range(TILES):
                        dve.scalar_tensor_tensor(out=xr[:, t, :], in0=xr[:, t, :], scalar=rstd[:, t:t + 1], in1=nw, op0=ALU.mult, op1=ALU.mult).then_inc(s["y"], 1)

        modulation()
        norm_in(0, even_w, w_in_sem)
        project_even()
        mn = prepare_even()
        mlstm(mn)

        def even_keys(h, t):
            g = h // 4
            return kT[g * 64:g * 64 + 64, 0:NT] if t < ST else kT[g * 64:g * 64 + 64, NT:NT + P]

        def even_values(h, t, j):
            g = h // 4
            if t < ST and j == 0:
                return vctx[:, g * 64:g * 64 + 64]
            return proj[:, (j - 1) if t < ST else PT, C_VB + g * 64:C_VB + g * 64 + 64]

        attention("gqa", BH, BD ** -0.5, lambda h, t: qT[(h // 4) * 64:(h // 4) * 64 + 64, h % 4, t * P:(t + 1) * P],
                  even_keys, even_values, lambda h, t: proj[:, t, h * 64:(h + 1) * 64], Carve(ringf, EVEN_TOP))
        mix_even()
        out_and_route(0, A["ev_w_out"][0])
        experts(0)
        clear_semaphores()
        w_sem = sem("w_odd")
        norm_in(1, odd_w, w_sem)
        project_odd(w_sem)
        prepare_odd()
        attention("mla", CH, CQK ** -0.5, lambda h, t: qT2[0:CQK, h, t * P:(t + 1) * P],
                  lambda h, t: kT2[0:CQK, h, 0:NT] if t < ST else kT2[0:CQK, h, NT:NT + P],
                  lambda h, t, j: v2[:, j if t < ST else TILES, h * CV:(h + 1) * CV],
                  lambda h, t: po[:, t, h * CV:(h + 1) * CV], Carve(ringf, ODD_TOP))
        recurrence()
        mix_odd()
        out_and_route(1, A["od_w_out"][0])
        experts(1)
        final_norm()


def tables():
    import numpy as np
    def rope(half):
        inv = (np.float32(10000.0) ** (-np.arange(half, dtype=np.float32) / np.float32(half))).astype(np.float32)
        t = np.arange(NS)
        pos = [(t // 64).astype(np.float32), (t % 64).astype(np.float32)]
        out = np.zeros((NS, 2, 2, 2, half), np.float32)
        for a in range(2):
            ang = pos[a][:, None] * inv[None, :]
            out[:, 0, a, :, :] = np.cos(ang)[:, None, :]
            out[:, 1, a, 0, :] = -np.sin(ang)
            out[:, 1, a, 1, :] = np.sin(ang)
        return np.ascontiguousarray(out.reshape(ST, P, 2, 4 * half).transpose(1, 0, 2, 3))
    s_, t_ = np.arange(P)[:, None], np.arange(P)[None, :]
    masks = np.stack([np.where(s_ <= t_, 0.0, -1e30), np.where(s_ >= t_, 0.0, -1e30)], axis=1).astype(np.float32)
    sel = np.zeros((4, 4, P), np.float32)
    selpair = np.zeros((4, 2, P), np.float32)
    for h in range(4):
        sel[h, h] = 1
        selpair[h, h // 2, (h % 2) * 64:(h % 2) * 64 + 64] = 1
    rst = np.tile((np.arange(NT) % P != 0).astype(np.float32), (4, 1))
    return {"ident": np.eye(P, dtype=np.float32), "rope_b": rope(16), "rope_c": rope(8), "masks": masks, "sel": sel,
            "selpair": selpair, "rst": rst}


OUTS = [(1, NP, D), (1, NS, D), (1, 1, 2, AH, AQ, AV), (1, 1, 2, AH, AQ), (1, 1, 2, AH), (1, 1, NP, BKV, BD), (1, 1, NP, BKV, BD),
        (1, 1, NP, CKVL), (1, 1, NP, CROPE), (1, 1, 2, DR)]


def kernel(**inputs):
    import numpy as np
    import concourse.bacc as bacc
    from concourse.bass_utils import run_bass_kernel_spmd

    nc = bacc.Bacc("TRN2", target_bir_lowering=False, num_devices=1)
    arrays, A = {}, {}
    for name, a in [*inputs.items(), *tables().items()]:
        a = np.ascontiguousarray(a)
        arrays[f"in_{name}_dram"] = a
        A[name] = nc.dram_tensor(f"in_{name}_dram", a.shape, mybir.dt.from_np(a.dtype), kind="ExternalInput").ap()
    O = [nc.dram_tensor(f"out_{i}_dram", shape, F32, kind="ExternalOutput").ap() for i, shape in enumerate(OUTS)]
    build(nc, A, O)
    r = run_bass_kernel_spmd(nc, [arrays], core_ids=[0])
    return tuple(r.results[0][f"out_{i}_dram"] for i in range(len(OUTS)))
```

```python
from contextlib import ExitStack

import concourse.bass as bass
from concourse import mybir

F32 = mybir.dt.float32
U32 = mybir.dt.uint32
I32 = mybir.dt.int32
ALU = mybir.AluOpType
ACT = mybir.ActivationFunctionType
AX = mybir.AxisListType

P = 128
D = 1024
KD = D // P
NS, NP = 512, 128
NT = NS + NP
TILES = NT // P
ST = NS // P
PT = ST
EPS = 1e-6

BH, BKV, BD = 8, 2, 64
AH, AQ, AV = 4, 64, 128
EVEN_IN = BH * BD + 2 * BKV * BD + AH * (2 * AQ + 2 * AV) + 4 * AH
C_QB, C_KB, C_VB = 0, BH * BD, (BH + BKV) * BD
C_QA = C_VB + BKV * BD
C_KA = C_QA + AH * AQ
C_VA = C_KA + AH * AQ
C_OA = C_VA + AH * AV
C_GA = C_OA + AH * AV

CH, CQL, CKVL, CNOPE, CROPE, CV = 8, 384, 256, 64, 32, 64
CQK = CNOPE + CROPE
DR, RGB, RGW = 512, 8, 64
ODD_IN = CQL + CKVL + CROPE + 2 * DR
ODD_TOK = CQL + CKVL + CROPE

NE, FF = 16, 512
CAPS, CAPP = NS * 2 // NE, NP * 2 // NE
CAP = CAPS + CAPP
FB = FF // P


class Steps:

    def __init__(self, eng, sem):
        self.eng, self.sem, self.n = eng, sem, 0

    def __call__(self, ins):
        self.n += 1
        ins.then_inc(self.sem, 1)
        return self.n

    def wait(self):
        self.eng.wait_ge(self.sem, self.n)

    def link(self, ins):
        self(ins)
        self.wait()


class Carve:

    def __init__(self, ap, at=0):
        self.ap, self.at = ap, at

    def __call__(self, *dims):
        n = 1
        for d in dims:
            n *= d
        assert self.at + n <= self.ap.shape[1], (self.at, n, self.ap.shape)
        a = self.ap[:, self.at:self.at + n]
        self.at += n
        if len(dims) == 1:
            return a
        names = "abcde"[:len(dims)]
        spec = "p (" + " ".join(names) + ") -> p " + " ".join(names)
        return a.rearrange(spec, **{k: v for k, v in zip(names[1:], dims[1:])})


def build(nc, A, O):
    ctx = ExitStack()
    with ctx:
        def sb(name, shape, dt=F32):
            return ctx.enter_context(nc.sbuf_tensor(name, shape, dt))

        in_use = []

        def sem(name):
            in_use.append(nc.alloc_semaphore(name))
            return in_use[-1]

        def clear_semaphores():
            nc.clear_and_free_semaphores(in_use)
            in_use.clear()
            nc.all_engine_barrier()

        def dram(name, shape):
            return nc.dram_tensor(name, shape, F32, kind="Internal").ap()

        x_rows = dram("x_rows", [NT, D])
        xm_rows = dram("xm_rows", [NT, D])
        mod_rows = dram("mod_rows", [2, 2, 6 * D])

        ring = sb("ring", [P, 6, 4096])
        xT = sb("xT", [P, KD, NT])
        xr = sb("xr", [P, TILES, D])
        proj = sb("proj", [P, TILES, EVEN_IN])
        ident = sb("ident", [P, P])
        small = sb("small", [P, 640])
        hold = sb("hold", [P, 2, D])
        psum = ctx.enter_context(nc.psum_tensor("psum", [P, 8, 512], F32))

        def bank(n, w=512):
            return psum[:, n, 0:w]

        holdf = hold[:, :, :].rearrange("p a b -> p (a b)")
        ringf = ring[:, :, :].rearrange("p a b -> p (a b)")
        projf = proj[:, :, :].rearrange("p a b -> p (a b)")

        GRP = 4
        CHUNKS = [(l, j) for l in range(2) for j in range(3)]
        mc = Carve(small[:, 384:640])
        c_rows, cT = mc(P), mc(2 * KD)
        NMOD = 3
        mod_buf = [ring[:, 5, 0:2048], ring[:, 5, 2048:4096], hold[:, :, :].rearrange("p a b -> p (a b)")]
        modrow = sb("modrow", [P, 2, 512])
        xm = sb("xm", [P, 2, D])

        def piece_source(c, k):
            l, j = CHUNKS[c]
            return A["ada_w"][l, k * P:(k + 1) * P, j * 2048:(j + 1) * 2048]

        def piece_product(pe, c, k, buf, banks):
            for g in range(GRP):
                mm = pe.matmul(psum[32 * g:32 * g + 2, banks[c % 2], :], cT[:, k::KD], buf[:, g * 512:(g + 1) * 512],
                               start=(k == 0), stop=(k == KD - 1))
            return mm

        def load_bias(sp, c, loaded):
            l, j = CHUNKS[c]
            for g in range(GRP):
                at = j * 2048 + g * 512
                sp.dma_start(modrow[32 * g:32 * g + 2, c % 2, :], A["ada_b"][l:l + 1, at:at + 512].to_broadcast([2, 512])).then_inc(loaded, 16)

        def chunk_rows(dve, own, c, banks):
            for g in range(GRP):
                q = slice(32 * g, 32 * g + 2)
                own(dve.tensor_tensor(modrow[q, c % 2, :], psum[q, banks[c % 2], :], modrow[q, c % 2, :], ALU.add))
            own.wait()

        def store_chunk(sp, c, stored):
            l, j = CHUNKS[c]
            for g in range(GRP):
                at = j * 2048 + g * 512
                sp.dma_start(mod_rows[l, :, at:at + 512], modrow[32 * g:32 * g + 2, c % 2, :]).then_inc(stored, 16)

        def start():
            s = {n: sem("m_" + n) for n in ("consts", "bias", "cT", "silu", "done", "own", "rows", "stored")}
            s_in = [sem(f"m_in{k}") for k in range(KD)]
            bufs = [projf[:, 2048 * i:2048 * (i + 1)] for i in range(5)] + mod_buf
            with nc.Block("start") as block:
                @block.sync
                def _(sp):
                    sp.dma_start(c_rows[0:KD, :], A["c"].rearrange("a (k p) -> (a k) p", p=P)).then_inc(s["consts"], 16)
                    sp.dma_start(c_rows[KD:2 * KD, :], A["c_ctx"].rearrange("(k p) -> k p", p=P)).then_inc(s["consts"], 16)
                    sp.dma_start(ident[:, :], A["ident"]).then_inc(s["consts"], 16)
                    for k in range(KD):
                        sp.dma_start(bufs[k], piece_source(0, k)).then_inc(s_in[k], 16)
                    load_bias(sp, 0, s["bias"])
                    for t in range(TILES):
                        sp.dma_start(xr[:, t, :], A["x_sample"][0, t * P:(t + 1) * P, :] if t < ST else A["x_prompt"][0]).then_inc(x_in[t], 16)
                    sp.wait_ge(s["rows"], 1)
                    store_chunk(sp, 0, s["stored"])
                    sp.wait_ge(s["stored"], 16 * GRP)

                @block.tensor
                def _(pe):
                    pe.wait_ge(s["consts"], 16 * 3)
                    pe.transpose(bank(0)[:, 0:2 * KD], c_rows[0:2 * KD, :], ident[0:2 * KD, 0:2 * KD]).then_inc(s["cT"], 1)
                    pe.wait_ge(s["silu"], 1)
                    for k in range(KD):
                        pe.wait_ge(s_in[k], 16)
                        mm = piece_product(pe, 0, k, bufs[k], (6, 7))
                    mm.then_inc(s["done"], 1)

                @block.scalar
                def _(act):
                    act.wait_ge(s["cT"], 1)
                    act.activation(cT, bank(0)[:, 0:2 * KD], ACT.Silu).then_inc(s["silu"], 1)

                @block.vector
                def _(dve):
                    own = Steps(dve, s["own"])
                    dve.wait_ge(s["bias"], 16 * GRP)
                    dve.wait_ge(s["done"], 1)
                    chunk_rows(dve, own, 0, (6, 7))
                    dve.sem_inc(s["rows"], 1)

        def project(l, x_in, weights, w_in, units, pieces, late):
            s = {n: sem(f"n{l}_{n}") for n in ("mods", "ssq", "root", "own", "mown", "scaled", "xm", "turned", "copied", "mm", "act", "dve",
                                               "used", "rows", "stored0", "stored1", "bias0", "bias1", "late")}
            s_p = [sem(f"n{l}_p{i}") for i in range(NMOD)] if pieces else []
            if l == 0:
                place = [proj[:, i, 512:512 + D] for i in range(5)]
            else:
                place = [ring[:, 1, i * D:(i + 1) * D] for i in range(4)] + [ring[:, 2, 0:D]]
            shift, scale, nw = place[0:4:2], place[1:4:2], place[4]
            junk = psum[:, 6:8, :].rearrange("p a n -> p (a n)")
            ssq = small[:, 0:TILES]
            rstd = small[:, 8:8 + TILES]
            UB = 4
            plan = []
            left = list(range(len(pieces)))
            for u in range(len(units)):
                if u < TILES:
                    plan.append(("turn", u))
                plan.append(("unit", u))
                for _ in range(2):
                    if left and u >= 2:
                        plan.append(("piece", left.pop(0)))
            plan += [("piece", p) for p in left]
            with nc.Block(f"project_{l}") as block:
                @block.sync
                def _(sp):
                    if l:
                        for t in range(TILES):
                            sp.dma_start(xr[:, t, :], x_rows[t * P:(t + 1) * P, :]).then_inc(x_in[t], 16)
                    for cond in range(2):
                        for j in range(2):
                            sp.dma_start((shift, scale)[j][cond], mod_rows[l, cond:cond + 1, j * D:(j + 1) * D].to_broadcast([P, D])).then_inc(s["mods"], 16)
                    sp.dma_start(nw, A["norm1_w"][l:l + 1, :].to_broadcast([P, D])).then_inc(s["mods"], 16)
                    for i, (dst, src) in enumerate(weights):
                        sp.dma_start(dst, src).then_inc(w_in[i], 16)
                    stored = [0, 0]
                    if pieces:
                        load_bias(sp, pieces[0][0], s[f"bias{pieces[0][0] % 2}"])
                    for p, (c, k) in enumerate(pieces):
                        if p % KD == 6 and p + KD < len(pieces):
                            if c >= 2 and p > KD:
                                sp.wait_ge(s[f"stored{(c + 1) % 2}"], 16 * stored[(c + 1) % 2])
                            load_bias(sp, c + 1, s[f"bias{(c + 1) % 2}"])
                        if p >= NMOD:
                            sp.wait_ge(s["used"], p - NMOD + 1)
                        sp.dma_start(mod_buf[p % NMOD], piece_source(c, k)).then_inc(s_p[p % NMOD], 16)
                        if p % KD == 3 and p > KD:
                            sp.wait_ge(s["rows"], p // KD)
                            store_chunk(sp, c - 1, s[f"stored{(c - 1) % 2}"])
                            stored[(c - 1) % 2] += GRP
                    if pieces:
                        c = pieces[-1][0]
                        sp.wait_ge(s["rows"], len(pieces) // KD)
                        store_chunk(sp, c, s[f"stored{c % 2}"])
                        stored[c % 2] += GRP
                        for i in range(2):
                            sp.wait_ge(s[f"stored{i}"], 16 * stored[i])

                @block.tensor
                def _(pe):
                    for what, n in plan:
                        if what == "turn":
                            pe.wait_ge(s["xm"], n + 1)
                            for h in range(2):
                                if n >= 1:
                                    pe.wait_ge(s["copied"], 2 * (n - 1) + h + 1)
                                for k in range(4):
                                    mm = pe.transpose(bank(4 + h)[:, k * P:(k + 1) * P], xm[:, n % 2, (4 * h + k) * P:(4 * h + k + 1) * P], ident[:, :])
                                mm.then_inc(s["turned"], 1)
                        elif what == "unit":
                            st, mv, w, _, wi, need = units[n]
                            pe.wait_ge(w_in[wi], 16)
                            pe.wait_ge(s["copied"], 2 * need)
                            if n >= UB:
                                pe.wait_ge(s["act"] if n % 2 == 0 else s["dve"], (n - UB) // 2 + 1)
                            for k in range(KD):
                                mm = pe.matmul(bank(n % UB, w), st[k], mv[k], start=(k == 0), stop=(k == KD - 1))
                            mm.then_inc(s["mm"], 1)
                        else:
                            c, k = pieces[n]
                            pe.wait_ge(s_p[n % NMOD], 16 * (n // NMOD + 1))
                            if k == 0 and n >= 2 * KD:
                                pe.wait_ge(s["rows"], n // KD - 1)
                            piece_product(pe, c, k, mod_buf[n % NMOD], (6, 7)).then_inc(s["used"], 1)

                @block.scalar
                def _(act):
                    for t in range(TILES):
                        act.wait_ge(x_in[t], 16)
                        act.activation(junk, xr[:, t, :], ACT.Square, accum_out=ssq[:, t:t + 1]).then_inc(s["ssq"], 1)
                        act.wait_ge(s["ssq"], t + 1)
                    act.activation(rstd, ssq, ACT.Sqrt, scale=1.0 / D, bias=EPS).then_inc(s["root"], 1)
                    for what, n in plan:
                        if what == "turn":
                            for h in range(2):
                                act.wait_ge(s["turned"], 2 * n + h + 1)
                                act.activation(xT[:, 4 * h:4 * h + 4, n * P:(n + 1) * P], bank(4 + h).rearrange("p (k c) -> p k c", k=4),
                                               ACT.Copy).then_inc(s["copied"], 1)
                        elif what == "unit" and n % 2 == 0:
                            act.wait_ge(s["mm"], n + 1)
                            act.activation(units[n][3], bank(n % UB, units[n][2]), ACT.Copy).then_inc(s["act"], 1)

                @block.vector
                def _(dve):
                    own = Steps(dve, s["own"])
                    mown = Steps(dve, s["mown"])
                    dve.wait_ge(s["mods"], 16 * 5)
                    for cond in range(2):
                        own(dve.scalar_tensor_tensor(out=scale[cond], in0=scale[cond], scalar=1.0,
                                                     in1=nw, op0=ALU.add, op1=ALU.mult))
                    dve.wait_ge(s["root"], 1)
                    own.link(dve.reciprocal(rstd, rstd))

                    def scale_rows(t):
                        if t >= 2:
                            dve.wait_ge(s["turned"], 2 * (t - 1))
                        dve.scalar_tensor_tensor(out=xm[:, t % 2, :], in0=xr[:, t, :], scalar=rstd[:, t:t + 1],
                                                 in1=scale[t // ST], op0=ALU.mult, op1=ALU.mult).then_inc(s["scaled"], 1)
                    scale_rows(0)
                    scale_rows(1)
                    for what, n in plan:
                        if what == "turn" and n + 2 < TILES:
                            scale_rows(n + 2)
                        elif what == "unit" and n % 2:
                            dve.wait_ge(s["mm"], n + 1)
                            dve.tensor_copy(units[n][3], bank(n % UB, units[n][2])).then_inc(s["dve"], 1)
                        elif what == "piece" and n % KD == KD - 1:
                            c = pieces[n][0]
                            m = n // KD
                            dve.wait_ge(s["used"], n + 1)
                            dve.wait_ge(s[f"bias{c % 2}"], 16 * GRP * (m // 2 + 1))
                            chunk_rows(dve, mown, c, (6, 7))
                            dve.sem_inc(s["rows"], 1)

                @block.gpsimd
                def _(pool):
                    pool.wait_ge(s["mods"], 16 * 5)
                    for t in range(TILES):
                        pool.wait_ge(s["scaled"], t + 1)
                        pool.tensor_tensor(xm[:, t % 2, :], xm[:, t % 2, :], shift[t // ST], ALU.add).then_inc(s["xm"], 1)
                    late(pool, s["late"])

        W_IN_CUTS = [(c, min(512, EVEN_IN - c)) for c in range(0, EVEN_IN, 512)]
        even_w = [(ring[:, i, 0:KD * n].rearrange("p (k n) -> p k n", k=KD),
                   A["ev_w_in"][0, :, c:c + n].rearrange("(k p) n -> p k n", p=P)) for i, (c, n) in enumerate(W_IN_CUTS)]

        def token_units(cuts, w, dst):
            return [([xT[:, k, t * P:(t + 1) * P] for k in range(KD)], [w[i][0][:, k, :] for k in range(KD)], n, dst(t, c, n), i, t + 1)
                    for i, (c, n) in enumerate(cuts) for t in range(TILES)]

        sc = Carve(ringf, 2 * 4096)
        qT = sc(BKV, BH // BKV, NT)
        kT = sc(NT + P)
        vctx = sc(BKV * BD)
        ML_AT = sc.at
        mqT, mkT = sc(2, NT), sc(2, NT)
        vaug = sc(TILES, AH, AV + 1)
        cols = sc(4, 2, TILES, AH)
        dec = sc(2, 2, TILES)
        carry = sc(2, 2, AV + 1)
        carryp = sc(2, 2, AV + 1)
        masks = sc(2, P)
        sel = sc(AH, P)
        selpair = sc(2, P)
        ROT_AT = sc.at
        negM = sc(2, TILES, P)
        EVEN_TOP = sc.at

        def prepare_even():
            s = {n: sem("ep_" + n) for n in ("in", "own", "act", "pool", "gates", "gT", "sq", "ssq", "rs", "cos",
                                             "rot", "qk", "kcache", "out", "m_t", "m_c", "q_t", "q_c", "rows", "c_t", "ex", "exd")}
            cs = Carve(xT[:, :, :].rearrange("p k n -> p (k n)"))
            sq = cs(TILES, 640)
            rotb = Carve(ringf, ROT_AT)(ST, 640)
            gb = small[:, 192:208]
            ssq, rs = small[:, 0:50], small[:, 64:114]
            L = cs(2, NT)[0:4]
            tabs, wqk = cs(ST, 2, BD), cs(2, BD)
            Bc = holdf[0:4, 0:2 * NT].rearrange("p (d n) -> p d n", d=2)
            hc = Carve(ringf, 0)
            a_, M, W1, EN = (hc(2, NT)[0:4] for _ in range(4))
            G = Carve(ringf, 4 * NT)(4, NT)[0:4]
            WK = hc(2, NT)[0:4]
            rst = hc(NT)[0:4]
            mp = small[0:4, 128:138].rearrange("p (d t) -> p d t", d=2)
            mn = small[0:4, 144:154].rearrange("p (d t) -> p d t", d=2)
            decr = small[0:4, 160:170].rearrange("p (d t) -> p d t", d=2)
            ORDER = [list(range(ST)), list(range(ST - 1, -1, -1))]
            qk = proj[:, :, 0:640]

            def by_group(x):
                return x.rearrange("p (g j d) -> p g j d", g=BKV, d=BD)

            def paired(t):
                return proj[:, t, 0:512].rearrange("p (j g d) -> p g j d", g=BKV, d=BD)

            with nc.Block("prepare_even") as block:
                @block.sync
                def _(sp):
                    n = 0
                    st = A["state_mlstm_C"][0, 0]
                    sn = A["state_mlstm_n"][0, 0]
                    for r in range(2):
                        for d in range(2):
                            sp.dma_start(carry[r * 64:r * 64 + 64, d, :, 0:AV],
                                         st[d, r::2].rearrange("j d e -> d j e")).then_inc(s["in"], 16)
                            with nc.allow_non_contiguous_dma(reason="256 words"):
                                sp.dma_start(carry[r * 64:r * 64 + 64, d, :, AV:AV + 1],
                                             sn[d, r::2].rearrange("j (d e) -> d j e", e=1)).then_inc(s["in"], 16)
                            n += 2
                    with nc.allow_non_contiguous_dma(reason="8 words"):
                        for d in range(2):
                            sp.dma_start(mp[:, d, ORDER[d][0]:ORDER[d][0] + 1],
                                         A["state_mlstm_m"][0, 0, d].rearrange("(h e) -> h e", e=1)).then_inc(s["in"], 16)
                            n += 1
                    for dst, src in [(tabs, A["rope_b"]), (masks, A["masks"]), (sel[0:4], A["sel"]),
                                     (selpair[0:4], A["selpair"]), (rst, A["rst"]),
                                     (wqk[:, 0, :], A["gqa_q_norm"].to_broadcast([P, BD])),
                                     (wqk[:, 1, :], A["gqa_k_norm"].to_broadcast([P, BD])),
                                     (gb, A["mlstm_gate_b"].to_broadcast([P, 16])),
                                     (vctx, A["cache_gqa_v"][0, 0].rearrange("s h d -> s (h d)")),
                                     (rotb[:, 0, 0:P], A["cache_gqa_k"][0, 0].rearrange("s h d -> s (h d)"))]:
                        sp.dma_start(dst, src).then_inc(s["in"], 16)
                        n += 1
                    sp.in_count = n
                    sp.wait_ge(s["kcache"], 1)
                    sp.dma_start(O[5][0, 0].rearrange("s h d -> s (h d)"), proj[:, PT, C_KB:C_KB + P]).then_inc(s["out"], 16)
                    sp.dma_start(O[6][0, 0].rearrange("s h d -> s (h d)"), proj[:, PT, C_VB:C_VB + P]).then_inc(s["out"], 16)
                    sp.wait_ge(s["out"], 32)
                LOADS = 16 * (8 + 2 + 10)

                @block.gpsimd
                def _(pool):
                    for t in range(TILES):
                        pool.tensor_scalar(proj[:, t, C_KA:C_KA + AH * AQ], proj[:, t, C_KA:C_KA + AH * AQ],
                                           AQ ** -0.5, None, ALU.mult).then_inc(s["pool"], 1)
                    pool.memset(qT, 0.0).then_inc(s["rows"], 1)
                    pool.memset(vaug[:, :, :, AV:AV + 1], 1.0).then_inc(s["rows"], 1)
                    for t in range(TILES):
                        pool.tensor_copy(vaug[:, t, :, 0:AV], proj[:, t, C_VA:C_VA + AH * AV].rearrange("p (h e) -> p h e", h=AH)).then_inc(s["rows"], 1)
                    pool.wait_ge(s["in"], LOADS)
                    pool.wait_ge(s["kcache"], 1)
                    pool.wait_ge(s["m_t"], 2 * TILES + 1)
                    for t in range(ST):
                        x = proj[:, t, 0:640].rearrange("p (h a u i) -> p h a u i", a=2, u=2, i=16)
                        o = rotb[:, t, :].rearrange("p (h a u i) -> p h a u i", a=2, u=2, i=16)
                        sn = tabs[:, t, 1, :].rearrange("p (a u i) -> p a u i", a=2, u=2)
                        for u in range(2):
                            for a in range(2):
                                pool.tensor_tensor(o[:, :, a, u, :], x[:, :, a, 1 - u, :],
                                                   sn[:, a, u, :].unsqueeze(1).to_broadcast([P, 10, 16]), ALU.mult).then_inc(s["rot"], 1)

                @block.vector
                def _(dve):
                    own = Steps(dve, s["own"])
                    dve.wait_ge(s["in"], LOADS)
                    dve.tensor_tensor(proj[:, :, C_GA:C_GA + 16], proj[:, :, C_GA:C_GA + 16],
                                      gb.unsqueeze(1).to_broadcast([P, TILES, 16]), ALU.add).then_inc(s["gates"], 1)
                    dve.memset(mp[:, :, PT:PT + 1], 0.0).then_inc(s["own"], 1)
                    own.n += 1
                    dve.wait_ge(s["sq"], 1)
                    dve.tensor_reduce(ssq.rearrange("p (t h) -> p t h", t=TILES),
                                      sq.rearrange("p t (h d) -> p t h d", d=BD), AX.X, ALU.add).then_inc(s["ssq"], 1)
                    for c in range(5):
                        dve.wait_ge(s["gT"], 20)
                        own(dve.tensor_copy(G.rearrange("p k n -> p (k n)")[:, c * 512:(c + 1) * 512], psum[0:4, c, :]))
                    own.wait()
                    own.link(dve.tensor_scalar(L, G[:, 1::2, :], 0.0, None, ALU.min))
                    dve.wait_ge(s["rs"], 1)
                    own.link(dve.reciprocal(rs, rs))
                    r3 = rs.rearrange("p (t h) -> p t h", t=TILES)
                    for t in range(TILES):
                        own.link(dve.tensor_tensor(proj[:, t, 0:640].rearrange("p (h d) -> p h d", d=BD),
                                              proj[:, t, 0:640].rearrange("p (h d) -> p h d", d=BD),
                                              r3[:, t].unsqueeze(2).to_broadcast([P, 10, BD]), ALU.mult))
                        own(dve.tensor_tensor(proj[:, t, 0:512].rearrange("p (h d) -> p h d", d=BD),
                                              proj[:, t, 0:512].rearrange("p (h d) -> p h d", d=BD),
                                              wqk[:, 0:1, :].to_broadcast([P, BH, BD]), ALU.mult))
                        own.link(dve.tensor_tensor(proj[:, t, 512:640].rearrange("p (h d) -> p h d", d=BD),
                                              proj[:, t, 512:640].rearrange("p (h d) -> p h d", d=BD),
                                              wqk[:, 1:2, :].to_broadcast([P, BKV, BD]), ALU.mult))
                    dve.sem_inc(s["kcache"], 1)
                    for t in range(ST):
                        own(dve.tensor_tensor(sq[:, t, :].rearrange("p (h d) -> p h d", d=BD),
                                              proj[:, t, 0:640].rearrange("p (h d) -> p h d", d=BD),
                                              tabs[:, t, 0:1, :].to_broadcast([P, 10, BD]), ALU.mult))
                    dve.wait_ge(s["own"], own.n)
                    dve.wait_ge(s["rot"], 16)
                    for t in range(ST):
                        own(dve.tensor_tensor(paired(t), by_group(sq[:, t, 0:512]), by_group(rotb[:, t, 0:512]), ALU.add))
                        own.link(dve.tensor_tensor(proj[:, t, 512:640], sq[:, t, 512:640], rotb[:, t, 512:640], ALU.add))
                        dve.sem_inc(s["qk"], 1)
                    own.link(dve.tensor_copy(sq[:, PT, 0:512], proj[:, PT, 0:512]))
                    own.link(dve.tensor_copy(paired(PT), by_group(sq[:, PT, 0:512])))
                    dve.sem_inc(s["qk"], 1)
                    dve.wait_ge(s["act"], 4)
                    own.link(dve.tensor_tensor(L, L, Bc, ALU.subtract))
                    own(dve.tensor_tensor_scan(Bc[:, 0, :], rst, L[:, 0, :], 0.0, ALU.mult, ALU.add))
                    own.link(dve.tensor_tensor_scan(Bc[:, 1, ::-1], rst, L[:, 1, ::-1], 0.0, ALU.mult, ALU.add))
                    own.link(dve.tensor_tensor(a_, G[:, 0::2, :], Bc, ALU.subtract))
                    for step in range(ST + 1):
                        for d in range(2):
                            t = PT if step == ST else ORDER[d][step]
                            lo, hi = t * P, (t + 1) * P
                            if d == 0:
                                src, dst, end = a_[:, 0, lo:hi], M[:, 0, lo:hi], hi - 1
                            else:
                                stop = lo - 1 if lo else None
                                src, dst, end = a_[:, 1, hi - 1:stop:-1], M[:, 1, hi - 1:stop:-1], lo
                            own.link(dve.tensor_tensor_scan(dst, src, src, mp[:, d, t:t + 1], ALU.max, ALU.max))
                            own.link(dve.tensor_tensor(mn[:, d, t:t + 1], Bc[:, d, end:end + 1], M[:, d, end:end + 1], ALU.add))
                            if step < ST - 1:
                                nxt = ORDER[d][step + 1]
                                own.link(dve.tensor_copy(mp[:, d, nxt:nxt + 1], mn[:, d, t:t + 1]))
                    own(dve.tensor_tensor(EN, Bc, M, ALU.add))
                    for d in range(2):
                        Mt = M[:, d, :].rearrange("p (t n) -> p t n", t=TILES)
                        At = a_[:, d, :].rearrange("p (t n) -> p t n", t=TILES)
                        own(dve.tensor_tensor(W1[:, d, :].rearrange("p (t n) -> p t n", t=TILES), Mt,
                                              mp[:, d, :].unsqueeze(2).to_broadcast([4, TILES, P]), ALU.subtract))
                        e = P - 1 if d == 0 else 0
                        own(dve.tensor_tensor(WK[:, d, :].rearrange("p (t n) -> p t n", t=TILES), At,
                                              Mt[:, :, e:e + 1].to_broadcast([4, TILES, P]), ALU.subtract))
                    own.link(dve.tensor_scalar(negM[0:4].rearrange("p d t n -> p (d t n)"), M.rearrange("p d n -> p (d n)"), -1.0, None, ALU.mult))
                    dve.sem_inc(s["ex"], 1)
                    dve.wait_ge(s["exd"], 3)
                    for d in range(2):
                        e = P - 1 if d == 0 else 0
                        own.link(dve.tensor_copy(decr[:, d, :], W1[:, d, e::P]))
                    dve.sem_inc(s["ex"], 1)
                    dve.wait_ge(s["c_t"], 1)
                    own(dve.tensor_copy(cols.rearrange("p k d t h -> p (k d t h)"), bank(6, 160)))
                    own(dve.tensor_copy(dec.rearrange("p j d t -> p (j d t)"), bank(7, 20)))

                @block.scalar
                def _(act):
                    own = Steps(act, s["act"])
                    for t in range(TILES):
                        ins = act.activation(sq[:, t, :], proj[:, t, 0:640], ACT.Square)
                        if t < TILES - 1:
                            act.maybe = ins
                            ins.then_inc(s["cos"], 1)
                        else:
                            ins.then_inc(s["cos"], 1)
                    act.wait_ge(s["cos"], TILES)
                    act.sem_inc(s["sq"], 1)
                    act.wait_ge(s["ssq"], 1)
                    act.activation(rs, ssq, ACT.Sqrt, scale=1.0 / BD, bias=EPS).then_inc(s["rs"], 1)
                    act.wait_ge(s["own"], 6)
                    own.link(act.activation(Bc, G[:, 1::2, :], ACT.Abs))
                    own.link(act.activation(Bc, Bc, ACT.Exp, scale=-1.0))
                    own.link(act.activation(Bc, Bc, ACT.Ln, bias=1.0))
                    act.sem_inc(s["act"], 1)
                    for n in range(2 * TILES):
                        act.wait_ge(s["m_t"], n + 1)
                        dst = (mqT, mkT)[n % 2]
                        act.activation(dst[:, :, (n // 2) * P:(n // 2 + 1) * P],
                                       bank(6 + n % 2, 256).rearrange("p (j c) -> p j c", j=2), ACT.Copy).then_inc(s["m_c"], 1)
                    act.wait_ge(s["m_t"], 2 * TILES + 1)
                    act.activation(kT[:, 0:P], bank(6, P), ACT.Copy).then_inc(s["m_c"], 1)
                    act.wait_ge(s["ex"], 1)
                    act.activation(W1, W1, ACT.Exp, scale=-1.0).then_inc(s["exd"], 1)
                    act.activation(EN, EN, ACT.Exp, scale=-1.0).then_inc(s["exd"], 1)
                    act.activation(WK, WK, ACT.Exp).then_inc(s["exd"], 1)
                    act.wait_ge(s["rows"], 1)
                    for t in range(TILES):
                        act.wait_ge(s["q_t"], t + 1)
                        for g in range(BKV):
                            q = slice(64 * g, 64 * g + 64)
                            act.activation(qT[q, g, :, t * P:(t + 1) * P], psum[q, 2 * (t % 2), :].rearrange("p (j c) -> p j c", j=4), ACT.Copy).then_inc(s["q_c"], 1)
                        act.activation(kT[:, (t + 1) * P:(t + 2) * P], bank(2 * (t % 2) + 1, P), ACT.Copy).then_inc(s["q_c"], 1)

                @block.tensor
                def _(pe):
                    pe.wait_ge(s["gates"], 1)
                    for kind in range(4):
                        for t in range(TILES):
                            at = kind * NT + t * P
                            pe.transpose(psum[0:4, at // 512, at % 512:at % 512 + P], proj[:, t, C_GA + 4 * kind:C_GA + 4 * kind + 4],
                                         ident[:, :]).then_inc(s["gT"], 1)
                    for n in range(2 * TILES):
                        t = n // 2
                        if n % 2:
                            pe.wait_ge(s["pool"], t + 1)
                        if n >= 2:
                            pe.wait_ge(s["m_c"], n - 1)
                        c0 = (C_QA, C_KA)[n % 2]
                        for j in range(2):
                            mm = pe.transpose(bank(6 + n % 2)[:, j * P:(j + 1) * P], proj[:, t, c0 + j * P:c0 + (j + 1) * P], ident[:, :])
                        mm.then_inc(s["m_t"], 1)
                    pe.wait_ge(s["in"], LOADS)
                    pe.wait_ge(s["m_c"], 2 * TILES - 1)
                    pe.transpose(bank(6, P), rotb[:, 0, 0:P], ident[:, :]).then_inc(s["m_t"], 1)
                    pe.wait_ge(s["own"], 6)
                    for t in range(TILES):
                        pe.wait_ge(s["qk"], t + 1)
                        if t >= 2:
                            pe.wait_ge(s["q_c"], 3 * (t - 1))
                        for j in range(4):
                            pe.transpose(bank(2 * (t % 2))[:, j * P:(j + 1) * P],
                                         proj[:, t, j * P:(j + 1) * P], ident[:, :])
                        pe.transpose(bank(2 * (t % 2) + 1, P), proj[:, t, 512:640], ident[:, :]).then_inc(s["q_t"], 1)
                    pe.wait_ge(s["ex"], 2)
                    pe.wait_ge(s["m_c"], 2 * TILES + 1)
                    for kind, src in enumerate((a_, W1, EN, WK)):
                        for d in range(2):
                            for t in range(TILES):
                                at = ((kind * 2 + d) * TILES + t) * AH
                                pe.transpose(bank(6)[:, at:at + 4], src[:, d, t * P:(t + 1) * P], ident[0:4, 0:4])
                    for j in range(2):
                        mm = pe.matmul(bank(7)[:, 10 * j:10 * j + 10], selpair[0:4, j, :], decr.rearrange("p d t -> p (d t)"), start=True, stop=True)
                    mm.then_inc(s["c_t"], 1)
            return mn

        def mlstm(mn):
            s = {n: sem("ml_" + n) for n in ("st", "eb", "E", "W", "mix", "inter", "num", "own", "kw", "upd", "carry", "out", "h")}
            s2 = Carve(holdf)
            E = s2(2, 4, P)
            KW = s2(AH, AQ)
            its = s2(2, 2, AV + 1)
            num = Carve(ringf, EVEN_TOP)(2, 2, AV + 1)
            dn = small[:, 0:4]
            dn2 = small[:, 4:8]
            units = []
            for i in range(ST):
                units += [(0, i), (1, ST - 1 - i)]
            units += [(0, PT), (1, PT)]
            first = {}
            for u, (d, t) in enumerate(units):
                first.setdefault(t, u)
            HA = proj[:, :, C_VA:C_VA + AH * AV]

            def col(kind, d, t, h):
                return cols[:, kind, d, t, h:h + 1]

            with nc.Block("mlstm") as block:
                @block.tensor
                def _(pe):
                    n_inter = 0
                    for u, (d, t) in enumerate(units):
                        tok = slice(t * P, (t + 1) * P)
                        if u >= 1:
                            pe.wait_ge(s["W"], u)
                        for j in range(2):
                            for r in range(2):
                                mm = pe.matmul(psum[:, r, j * P:(j + 1) * P], mkT[r * 64:r * 64 + 64, j, tok],
                                               mqT[r * 64:r * 64 + 64, j, tok], start=True, stop=True)
                        mm.then_inc(s["st"], 1)
                        if u >= 1:
                            pe.wait_ge(s["E"], u)
                        for i in range(4):
                            r, j = i // 2, i % 2
                            pe.matmul(psum[:, 2, i * P:(i + 1) * P], ident[:, :], masks[:, d, :], start=(i == 0), stop=False, skip_group_check=True)
                        for i in range(4):
                            r, j = i // 2, i % 2
                            mm = pe.matmul(psum[:, 2, i * P:(i + 1) * P], sel[0:4, 2 * j + r, :], negM[0:4, d, t, :],
                                           start=False, stop=(i == 3), skip_group_check=True)
                        mm.then_inc(s["eb"], 1)
                        if t != PT:
                            if u >= 2:
                                pe.wait_ge(s["carry"], u - 1)
                            if u >= 1:
                                pe.wait_ge(s["inter"], n_inter)
                            for j in range(2):
                                for r in range(2):
                                    mm = pe.matmul(psum[:, 5 + r, j * 129:(j + 1) * 129], mqT[r * 64:r * 64 + 64, j, tok],
                                                   carry[r * 64:r * 64 + 64, d, j, :], start=True, stop=True)
                            n_inter += 1
                            mm.then_inc(s["mix"], 1)
                        pe.wait_ge(s["kw"], u + 1)
                        if u >= 1:
                            pe.wait_ge(s["carry"], u)
                        for j in range(2):
                            for r in range(2):
                                mm = pe.matmul(psum[r * 64:r * 64 + 64, 7, j * 129:(j + 1) * 129], KW[:, 2 * j + r, :],
                                               vaug[:, t, 2 * j + r, :], start=True, stop=True)
                        mm.then_inc(s["upd"], 1)
                        pe.wait_ge(s["W"], u + 1)
                        if u >= 1:
                            pe.wait_ge(s["num"], u)
                        for j in range(2):
                            for r in range(2):
                                mm = pe.matmul(psum[:, 3 + r, j * 129:(j + 1) * 129], E[:, u % 2, 2 * r + j, :],
                                               vaug[:, t, 2 * j + r, :], start=True, stop=True)
                        mm.then_inc(s["out"], 1)

                @block.scalar
                def _(act):
                    n_inter = 0
                    for u, (d, t) in enumerate(units):
                        act.wait_ge(s["eb"], u + 1)
                        if u >= 2:
                            act.wait_ge(s["out"], u - 1)
                        for i in range(4):
                            r, j = i // 2, i % 2
                            mm = act.activation(E[:, u % 2, i, :], psum[:, 2, i * P:(i + 1) * P], ACT.Exp, bias=col(0, d, t, 2 * j + r))
                        mm.then_inc(s["E"], 1)
                        if t != PT:
                            n_inter += 1
                            act.wait_ge(s["mix"], n_inter)
                            if u >= 1:
                                act.wait_ge(s["num"], u)
                            for r in range(2):
                                for j in range(2):
                                    mm = act.activation(its[:, r, j, :], psum[:, 5 + r, j * 129:(j + 1) * 129], ACT.Copy,
                                                        scale=col(1, d, t, 2 * j + r))
                            mm.then_inc(s["inter"], 1)

                @block.vector
                def _(dve):
                    own = Steps(dve, s["own"])
                    n_inter = 0
                    for u, (d, t) in enumerate(units):
                        if u >= 1:
                            dve.wait_ge(s["upd"], u)
                        dve.tensor_tensor(KW, proj[:, t, C_KA:C_KA + AH * AQ].rearrange("p (h d) -> p h d", d=AQ),
                                          cols[:, 3, d, t, :].unsqueeze(2).to_broadcast([P, AH, AQ]), ALU.mult).then_inc(s["kw"], 1)
                        dve.wait_ge(s["st"], u + 1)
                        dve.wait_ge(s["E"], u + 1)
                        dve.tensor_tensor(E[:, u % 2].rearrange("p (r j) n -> p r (j n)", r=2), E[:, u % 2].rearrange("p (r j) n -> p r (j n)", r=2),
                                          psum[:, 0:2, 0:2 * P], ALU.mult).then_inc(s["W"], 1)
                        dve.wait_ge(s["upd"], u + 1)
                        if t == PT:
                            dve.tensor_copy(carryp[:, d].rearrange("p j e -> p (j e)"), bank(7, 258)).then_inc(s["carry"], 1)
                        else:
                            dve.wait_ge(s["mix"], n_inter + 1)
                            for j in range(2):
                                ins = dve.scalar_tensor_tensor(out=carry[:, d, j, :], in0=carry[:, d, j, :], scalar=dec[:, j, d, t:t + 1],
                                                               in1=bank(7)[:, j * 129:(j + 1) * 129], op0=ALU.mult, op1=ALU.add)
                                if j == 0:
                                    own(ins)
                            ins.then_inc(s["carry"], 1)
                        dve.wait_ge(s["out"], u + 1)
                        o = psum[:, 3:5, 0:258]
                        nv = num.rearrange("p r j e -> p r (j e)")
                        if t == PT:
                            own.link(dve.tensor_copy(nv, o))
                        else:
                            n_inter += 1
                            dve.wait_ge(s["inter"], n_inter)
                            own.link(dve.tensor_tensor(nv, its.rearrange("p r j e -> p r (j e)"), o, ALU.add))
                        dve.sem_inc(s["num"], 1)
                        d4 = num[:, :, :, AV]
                        dn4 = dn.rearrange("p (r j) -> p r j", r=2)
                        dn24 = dn2.rearrange("p (r j) -> p r j", r=2)
                        own.link(dve.tensor_scalar(dn4, d4, -1.0, None, ALU.mult))
                        own.link(dve.tensor_tensor(dn4, dn4, d4, ALU.max))
                        own.link(dve.tensor_tensor(dn24, dn4, cols[:, 2, d, t, :].rearrange("p (j r) -> p r j", r=2), ALU.max))
                        own.link(dve.reciprocal(dn, dn2))
                        for i in range(4):
                            r, j = i // 2, i % 2
                            h = 2 * j + r
                            dst = HA[:, t, h * AV:(h + 1) * AV]
                            if first[t] == u:
                                ins = dve.tensor_scalar(dst, num[:, r, j, 0:AV], dn[:, i:i + 1], None, ALU.mult)
                            else:
                                ins = dve.scalar_tensor_tensor(out=dst, in0=num[:, r, j, 0:AV], scalar=dn[:, i:i + 1], in1=dst,
                                                               op0=ALU.mult, op1=ALU.add)
                            own(ins)
                        dve.wait_ge(s["own"], own.n)

                @block.sync
                def _(sp):
                    sp.wait_ge(s["carry"], len(units))
                    for d in range(2):
                        for r in range(2):
                            sp.dma_start(O[2][0, 0, d, r::2].rearrange("j d e -> d j e"), carryp[r * 64:r * 64 + 64, d, :, 0:AV]).then_inc(s["h"], 16)
                            with nc.allow_non_contiguous_dma(reason="words"):
                                sp.dma_start(O[3][0, 0, d, r::2].rearrange("j (d e) -> d j e", e=1), carryp[r * 64:r * 64 + 64, d, :, AV:AV + 1]).then_inc(s["h"], 16)
                        with nc.allow_non_contiguous_dma(reason="words"):
                            sp.dma_start(O[4][0, 0, d].rearrange("(h e) -> h e", e=1), mn[:, d, PT:PT + 1]).then_inc(s["h"], 16)
                    sp.wait_ge(s["h"], 16 * 10)

        def attention(name, heads, scale, q_of, k_of, v_of, slots, tmp, extra=None):
            s = {n: sem(f"{name}_{n}") for n in ("s", "max", "p", "sum", "n", "na", "t", "c0", "c1", "o", "out", "own")}
            extra = extra or {}
            NB = 4
            Pb = tmp(NB, NT)
            mx, nb, rsum, rr = (small[:, 300 + 8 * i:300 + 8 * i + NB] for i in range(4))
            units = [(h, t) for h in range(heads) for t in range(TILES)]
            wide = [t < ST for _, t in units]
            N = len(units)
            NSL = len(slots)
            HALF = NT // 2
            ctxT = xm[:, 0, 0:4 * P].rearrange("p (h n) -> p h n", h=4)

            def scores(u):
                b = 2 * (u % 2)
                return psum[:, b:b + 2, 0:HALF] if wide[u] else psum[:, b, 0:P]

            def rows(u):
                return Pb[:, u % NB, :].rearrange("p (a n) -> p a n", a=2) if wide[u] else Pb[:, u % NB, 0:P]

            def by_act(u):
                return u % TILES == 3

            def wait_rows(eng, u):
                before = (u + TILES - 4) // TILES
                if by_act(u):
                    eng.wait_ge(s["na"], before + 1)
                else:
                    eng.wait_ge(s["n"], u - before + 1)

            with nc.Block(name) as block:
                @block.sync
                def _(sp):
                    if "sync" in extra:
                        extra["sync"](sp)

                @block.tensor
                def _(pe):
                    def turn(u):
                        h, t = units[u]
                        wait_rows(pe, u)
                        if u >= 1:
                            pe.wait_ge(s["c0"], u)
                            pe.wait_ge(s["c1"], u)
                        for j in range(TILES if wide[u] else 1):
                            mm = pe.transpose(psum[:, 4 + j // 4, (j % 4) * P:(j % 4 + 1) * P], Pb[:, u % NB, j * P:(j + 1) * P], ident[:, :])
                        mm.then_inc(s["t"], 1)

                    def values(pair):
                        done = TILES * (2 * pair + 2)
                        pe.wait_ge(s["c0"], done)
                        pe.wait_ge(s["c1"], done)
                        if pair >= 1:
                            pe.wait_ge(s["out"], 2 * pair)
                        for j in range(TILES):
                            for r in range(2):
                                h = 2 * pair + r
                                pe.matmul(psum[64 * r:64 * r + 64, 6, :], v_of(h, 0, j), slots[h % NSL][:, j, :], start=(j == 0), stop=(j == TILES - 1))
                        for r in range(2):
                            h = 2 * pair + r
                            mm = pe.matmul(psum[64 * r:64 * r + 64, 7, 0:P], v_of(h, PT, 0), ctxT[:, h % 4, :], start=True, stop=True)
                        mm.then_inc(s["o"], 1)

                    for i in range(N + NB - 1):
                        if i < N:
                            h, t = units[i]
                            b = 2 * (i % 2)
                            if i >= 2:
                                pe.wait_ge(s["p"], i - 1)
                            k = k_of(h, t)
                            if wide[i]:
                                for a in range(2):
                                    mm = pe.matmul(psum[:, b + a, 0:HALF], q_of(h, t), k[:, a * HALF:(a + 1) * HALF], start=True, stop=True)
                            else:
                                mm = pe.matmul(psum[:, b, 0:P], q_of(h, t), k, start=True, stop=True)
                            mm.then_inc(s["s"], 1)
                        if i >= NB - 1:
                            u = i - NB + 1
                            turn(u)
                            if u % (2 * TILES) == 1 and u > 1:
                                values(u // (2 * TILES) - 1)
                    values(heads // 2 - 1)

                @block.vector
                def _(dve):
                    if "vector" in extra:
                        extra["vector"](dve)
                    own = Steps(dve, s["own"])

                    def take(pair):
                        dve.wait_ge(s["o"], pair + 1)
                        dve.tensor_copy(xT[:, pair, 0:NS], psum[:, 6, :]).then_inc(s["out"], 1)
                        dve.tensor_copy(xT[:, pair, NS:NT], psum[:, 7, 0:P]).then_inc(s["out"], 1)

                    for i in range(N + NB - 1):
                        if i < N:
                            dve.wait_ge(s["s"], i + 1)
                            own.link(dve.tensor_reduce(mx[:, i % NB:i % NB + 1], scores(i), AX.XY if wide[i] else AX.X, ALU.max))
                            if i >= NB:
                                dve.wait_ge(s["p"], i - NB + 1)
                            dve.tensor_scalar(nb[:, i % NB:i % NB + 1], mx[:, i % NB:i % NB + 1], -scale, None, ALU.mult).then_inc(s["max"], 1)
                        if 1 <= i <= N:
                            u = i - 1
                            dve.wait_ge(s["p"], u + 1)
                            if u >= NB:
                                wait_rows(dve, u - NB)
                            dve.reciprocal(rr[:, u % NB:u % NB + 1], rsum[:, u % NB:u % NB + 1]).then_inc(s["sum"], 1)
                        if i >= NB - 1:
                            u = i - NB + 1
                            h, t = units[u]
                            dve.wait_ge(s["t"], u + 1)
                            if t == 0 and h >= NSL:
                                dve.wait_ge(s["o"], (h - NSL) // 2 + 1)
                            if wide[u]:
                                dve.tensor_copy(slots[h % NSL][:, 0:4, t * P:(t + 1) * P], psum[:, 4, :].rearrange("p (j c) -> p j c", j=4)).then_inc(s["c0"], 1)
                            else:
                                if h >= 4:
                                    dve.wait_ge(s["o"], (h - 4) // 2 + 1)
                                dve.tensor_copy(ctxT[:, h % 4, :], psum[:, 4, 0:P]).then_inc(s["c0"], 1)
                            if u % (2 * TILES) == 4 and u > 4:
                                take(u // (2 * TILES) - 1)
                    take(heads // 2 - 1)

                @block.scalar
                def _(act):
                    if "scalar" in extra:
                        extra["scalar"](act)
                    for i in range(N + NB - 1):
                        if i < N:
                            act.wait_ge(s["max"], i + 1)
                            if i >= NB:
                                act.wait_ge(s["t"], i - NB + 1)
                            act.activation(rows(i), scores(i), ACT.Exp, bias=nb[:, i % NB:i % NB + 1], scale=scale,
                                           accum_out=rsum[:, i % NB:i % NB + 1]).then_inc(s["p"], 1)
                        if 1 <= i <= N and by_act(i - 1):
                            u = i - 1
                            act.wait_ge(s["sum"], u + 1)
                            act.activation(Pb[:, u % NB, :], Pb[:, u % NB, :], ACT.Copy, scale=rr[:, u % NB:u % NB + 1]).then_inc(s["na"], 1)
                        if i >= NB - 1:
                            u = i - NB + 1
                            h, t = units[u]
                            act.wait_ge(s["t"], u + 1)
                            if wide[u]:
                                if t == 0 and h >= NSL:
                                    act.wait_ge(s["o"], (h - NSL) // 2 + 1)
                                act.activation(slots[h % NSL][:, 4, t * P:(t + 1) * P], psum[:, 5, 0:P], ACT.Copy).then_inc(s["c1"], 1)
                            else:
                                act.sem_inc(s["c1"], 1)

                @block.gpsimd
                def _(pool):
                    if "gpsimd" in extra:
                        extra["gpsimd"](pool)
                    for u in range(N):
                        if by_act(u):
                            continue
                        pool.wait_ge(s["sum"], u + 1)
                        w = NT if wide[u] else P
                        pool.tensor_scalar(Pb[:, u % NB, 0:w], Pb[:, u % NB, 0:w], rr[:, u % NB:u % NB + 1], None, ALU.mult).then_inc(s["n"], 1)

        def mix_even():
            s = {n: sem("mx_" + n) for n in ("w", "sq", "ssq", "root", "sig", "own", "ready", "turned", "copied")}
            HA = proj[:, :, C_VA:C_VA + 512]
            w = Carve(ringf, EVEN_TOP)(512)
            sq = Carve(ringf, ML_AT)(TILES, 512)
            ssq, rs = small[:, 0:20], small[:, 32:52]
            with nc.Block("mix_even") as block:
                @block.sync
                def _(sp):
                    sp.dma_start(w, A["mlstm_norm_w"].to_broadcast([P, 512])).then_inc(s["w"], 16)

                @block.scalar
                def _(act):
                    act.activation(sq, HA, ACT.Square).then_inc(s["sq"], 1)
                    act.activation(proj[:, :, C_OA:C_OA + 512], proj[:, :, C_OA:C_OA + 512], ACT.Sigmoid).then_inc(s["sig"], 1)
                    act.wait_ge(s["ssq"], 1)
                    act.activation(rs, ssq, ACT.Sqrt, scale=1.0 / AV, bias=EPS).then_inc(s["root"], 1)
                    for t in range(TILES):
                        act.wait_ge(s["turned"], t + 1)
                        act.activation(xT[:, 4:8, t * P:(t + 1) * P], bank(t % 4).rearrange("p (k c) -> p k c", k=4), ACT.Copy).then_inc(s["copied"], 1)

                @block.vector
                def _(dve):
                    own = Steps(dve, s["own"])
                    dve.wait_ge(s["sq"], 1)
                    dve.tensor_reduce(ssq.rearrange("p (t h) -> p t h", t=TILES), sq.rearrange("p t (h d) -> p t h d", d=AV), AX.X, ALU.add).then_inc(s["ssq"], 1)
                    dve.wait_ge(s["root"], 1)
                    own.link(dve.reciprocal(rs, rs))
                    dve.wait_ge(s["w"], 16)
                    dve.wait_ge(s["sig"], 1)
                    for t in range(TILES):
                        h3 = HA[:, t].rearrange("p (h d) -> p h d", d=AV)
                        own.link(dve.tensor_tensor(h3, h3, rs[:, 4 * t:4 * t + 4].unsqueeze(2).to_broadcast([P, AH, AV]), ALU.mult))
                        own.link(dve.tensor_tensor(HA[:, t], HA[:, t], w, ALU.mult))
                        dve.tensor_tensor(HA[:, t], HA[:, t], proj[:, t, C_OA:C_OA + 512], ALU.mult).then_inc(s["ready"], 1)

                @block.tensor
                def _(pe):
                    for t in range(TILES):
                        pe.wait_ge(s["ready"], t + 1)
                        if t >= 4:
                            pe.wait_ge(s["copied"], t - 3)
                        for k in range(4):
                            mm = pe.transpose(bank(t % 4)[:, k * P:(k + 1) * P], HA[:, t, k * P:(k + 1) * P], ident[:, :])
                        mm.then_inc(s["turned"], 1)

        idx = sb("idx", [CAP, NE], I32)
        gate = sb("gate", [CAP, NE])

        wv = ringf[:, 0:2 * 4096].rearrange("p (k n) -> p k n", k=KD)

        def out_loads(l, w_out, s):
            def issue(sp):
                sp.dma_start(wv, w_out.rearrange("(k p) n -> p k n", p=P)).then_inc(s["w"], 16)
                for cond in range(2):
                    sp.dma_start(hold[:, cond, :], mod_rows[l, cond:cond + 1, 2 * D:3 * D].to_broadcast([P, D])).then_inc(s["gm"], 16)
            return issue

        def out_and_route(l, early, after):
            s = {n: sem(f"o{l}_{n}") for n in ("mods", "mm", "gx", "x", "sq", "root", "own", "xm", "turned", "copied",
                                              "lg", "mx", "ex", "aff", "affT", "top", "it", "st", "row0", "row1")}
            cs = Carve(projf)
            mods, nw = cs(2, 2, D), cs(D)
            junk = cs(D)
            rw = cs(KD, NE)
            g = cs(512)
            affT = cs(NT)
            vals, idxf = cs(CAP), cs(CAP)
            iu = cs(CAP).bitcast(U32)
            soft = cs(TILES, NE)
            ssq, rstd, mxs, sums = small[:, 0:5], small[:, 8:13], small[:, 16:21], small[:, 24:29]
            lg = (bank(7)[:, 0:ST * NE], bank(2)[:, 0:NE])
            affb = (psum[0:NE, 6, :], psum[0:NE, 3, 0:P])
            trunk = (slice(0, ST), slice(PT, TILES))
            with nc.Block(f"out_{l}") as block:
                @block.sync
                def _(sp):
                    for cond in range(2):
                        for j in range(2):
                            sp.dma_start(mods[:, cond, j, :], mod_rows[l, cond:cond + 1, (3 + j) * D:(4 + j) * D].to_broadcast([P, D])).then_inc(s["mods"], 16)
                    sp.dma_start(nw, A["norm2_w"][l:l + 1, :].to_broadcast([P, D])).then_inc(s["mods"], 16)
                    with nc.allow_non_contiguous_dma(reason="64-byte rows"):
                        sp.dma_start(rw, A["router_w"][l].rearrange("(k p) e -> p k e", p=P)).then_inc(s["mods"], 16)
                    after(sp)
                    for t in range(TILES):
                        sp.wait_ge(s["x"], 2 * (t + 1))
                        sp.dma_start(x_rows[t * P:(t + 1) * P, :], xr[:, t, :]).then_inc(s["st"], 16)
                        sp.wait_ge(s["xm"], t + 1)
                        sp.dma_start(xm_rows[t * P:(t + 1) * P, :], xm[:, t % 2, :]).then_inc(s[f"row{t % 2}"], 16)
                    sp.wait_ge(s["st"], 16 * TILES)
                    sp.wait_ge(s["row0"], 16 * 3)
                    sp.wait_ge(s["row1"], 16 * 2)

                @block.tensor
                def _(pe):
                    def product(t, h):
                        u = 2 * t + h
                        if u >= 4:
                            pe.wait_ge(s["gx"], u - 3)
                        for k in range(KD):
                            mm = pe.matmul(bank(u % 4), xT[:, k, t * P:(t + 1) * P], wv[:, k, h * 512:(h + 1) * 512], start=(k == 0), stop=(k == KD - 1))
                        mm.then_inc(s["mm"], 1)

                    def turn(t):
                        pe.wait_ge(s["xm"], t + 1)
                        for h in range(2):
                            if t >= 1:
                                pe.wait_ge(s["copied"], 2 * (t - 1) + h + 1)
                            for k in range(4):
                                mm = pe.transpose(bank(4 + h)[:, k * P:(k + 1) * P], xm[:, t % 2, (4 * h + k) * P:(4 * h + k + 1) * P], ident[:, :])
                            mm.then_inc(s["turned"], 1)

                    def logits(t):
                        pe.wait_ge(s["copied"], 2 * t + 2)
                        dst = lg[0][:, t * NE:(t + 1) * NE] if t < ST else lg[1]
                        for k in range(KD):
                            mm = pe.matmul(dst, xT[:, k, t * P:(t + 1) * P], rw[:, k, :], start=(k == 0), stop=(k == KD - 1))
                        mm.then_inc(s["lg"], 1)

                    def turn_affinities(c):
                        pe.wait_ge(s["aff"], c + 1)
                        for t in range(trunk[c].start, trunk[c].stop):
                            mm = pe.transpose(affb[c][:, (t % ST) * P:(t % ST + 1) * P], soft[:, t, :], ident[:, :])
                        mm.then_inc(s["affT"], 1)

                    pe.wait_ge(early["w"], 16)
                    for t in range(ST):
                        product(t, 0)
                        if t:
                            turn(t - 1)
                        product(t, 1)
                        if t == 1:
                            pe.wait_ge(s["mods"], 16 * 6)
                        if t:
                            logits(t - 1)
                    product(PT, 0)
                    turn(ST - 1)
                    logits(ST - 1)
                    product(PT, 1)
                    turn_affinities(0)
                    turn(PT)
                    logits(PT)
                    turn_affinities(1)
                    pe.wait_ge(s["top"], 1)
                    pe.transpose(bank(4)[0:CAP, 0:NE], idxf[0:NE, :], ident[0:NE, 0:NE])
                    pe.transpose(bank(4)[0:CAP, NE:2 * NE], vals[0:NE, :], ident[0:NE, 0:NE]).then_inc(s["it"], 1)

                @block.vector
                def _(dve):
                    own = Steps(dve, s["own"])

                    def residual(t, h):
                        u = 2 * t + h
                        dve.wait_ge(s["mm"], u + 1)
                        dve.tensor_tensor(g, bank(u % 4), hold[:, t // ST, h * 512:(h + 1) * 512], ALU.mult).then_inc(s["gx"], 1)
                        dve.wait_ge(s["gx"], u + 1)
                        dve.tensor_tensor(xr[:, t, h * 512:(h + 1) * 512], xr[:, t, h * 512:(h + 1) * 512], g, ALU.add).then_inc(s["x"], 1)
                        dve.wait_ge(s["x"], u + 1)

                    def norm(t):
                        dve.wait_ge(s["root"], t + 1)
                        own.link(dve.reciprocal(rstd[:, t:t + 1], rstd[:, t:t + 1]))
                        if t >= 2:
                            dve.wait_ge(s["turned"], 2 * (t - 1))
                            dve.wait_ge(s[f"row{t % 2}"], 16 * (t // 2))
                        own.link(dve.scalar_tensor_tensor(out=xm[:, t % 2, :], in0=xr[:, t, :], scalar=rstd[:, t:t + 1], in1=mods[:, t // ST, 1, :],
                                                          op0=ALU.mult, op1=ALU.mult))
                        dve.tensor_tensor(xm[:, t % 2, :], xm[:, t % 2, :], mods[:, t // ST, 0, :], ALU.add).then_inc(s["xm"], 1)
                        dve.wait_ge(s["xm"], t + 1)

                    def softmax_start(c):
                        q, v = trunk[c], lg[c].rearrange("p (t e) -> p t e", e=NE)
                        dve.wait_ge(s["lg"], q.stop)
                        own.link(dve.tensor_reduce(mxs[:, q], v, AX.X, ALU.max))
                        dve.tensor_tensor(soft[:, q], v, mxs[:, q].unsqueeze(2).to_broadcast([P, q.stop - q.start, NE]), ALU.subtract).then_inc(s["mx"], 1)

                    def softmax_end(c):
                        q = trunk[c]
                        dve.wait_ge(s["ex"], c + 1)
                        own.link(dve.tensor_reduce(sums[:, q], soft[:, q], AX.X, ALU.add))
                        own.link(dve.reciprocal(sums[:, q], sums[:, q]))
                        dve.tensor_tensor(soft[:, q], soft[:, q], sums[:, q].unsqueeze(2).to_broadcast([P, q.stop - q.start, NE]), ALU.mult).then_inc(s["aff"], 1)

                    LO, AT, ROUNDS = (0, NS), (0, CAPS), (CAPS // 8, CAPP // 8)

                    def take_affinities(c):
                        dve.wait_ge(s["affT"], c + 1)
                        own.link(dve.tensor_copy(affT[0:NE, LO[c]:(LO + (NT,))[c + 1]], affb[c]))

                    def choose(c, lo, hi):
                        a = affT[0:NE, LO[c]:(LO + (NT,))[c + 1]]
                        for r in range(lo, hi):
                            at = AT[c] + 8 * r
                            v8 = vals[0:NE, at:at + 8]
                            own.link(dve.max(v8, a))
                            own.link(dve.max_index(iu[0:NE, at:at + 8], v8, a))
                            if r + 1 < ROUNDS[c]:
                                own.link(dve.match_replace(a, v8, a, -1.0))

                    dve.wait_ge(early["gm"], 32)
                    for t in range(TILES):
                        residual(t, 0)
                        if t == PT:
                            softmax_start(0)
                            softmax_end(0)
                        residual(t, 1)
                        if t == 0:
                            dve.wait_ge(s["mods"], 16 * 6)
                            for cond in range(2):
                                own(dve.scalar_tensor_tensor(out=mods[:, cond, 1, :], in0=mods[:, cond, 1, :], scalar=1.0, in1=nw, op0=ALU.add, op1=ALU.mult))
                        if t == PT:
                            take_affinities(0)
                        norm(t)
                    choose(0, 0, 4)
                    softmax_start(1)
                    choose(0, 4, 5)
                    softmax_end(1)
                    choose(0, 5, ROUNDS[0])
                    take_affinities(1)
                    choose(1, 0, ROUNDS[1])
                    own.link(dve.tensor_copy(idxf[0:NE, :], iu[0:NE, :]))
                    own.link(dve.tensor_scalar(idxf[0:NE, CAPS:CAP], idxf[0:NE, CAPS:CAP], float(NS), None, ALU.add))
                    dve.sem_inc(s["top"], 1)
                    dve.wait_ge(s["it"], 1)
                    own(dve.tensor_copy(idx[:, :], bank(4)[0:CAP, 0:NE]))
                    own(dve.tensor_copy(gate[:, :], bank(4)[0:CAP, NE:2 * NE]))

                @block.scalar
                def _(act):
                    def root(t):
                        act.wait_ge(s["x"], 2 * (t + 1))
                        act.activation(junk, xr[:, t, :], ACT.Square, accum_out=ssq[:, t:t + 1]).then_inc(s["sq"], 1)
                        act.wait_ge(s["sq"], t + 1)
                        act.activation(rstd[:, t:t + 1], ssq[:, t:t + 1], ACT.Sqrt, scale=1.0 / D, bias=EPS).then_inc(s["root"], 1)

                    def turn_copy(t):
                        for h in range(2):
                            act.wait_ge(s["turned"], 2 * t + h + 1)
                            if h == 0:
                                act.wait_ge(s["mm"], 2 * t + 2)
                            act.activation(xT[:, 4 * h:4 * h + 4, t * P:(t + 1) * P], bank(4 + h).rearrange("p (k c) -> p k c", k=4), ACT.Copy).then_inc(s["copied"], 1)

                    def exponent(c):
                        act.wait_ge(s["mx"], c + 1)
                        act.activation(soft[:, trunk[c]], soft[:, trunk[c]], ACT.Exp).then_inc(s["ex"], 1)

                    for t in range(TILES):
                        if t:
                            turn_copy(t - 1)
                        if t == PT:
                            exponent(0)
                        root(t)
                    turn_copy(PT)
                    exponent(1)

        wslot = [[ring[:, 3 * (1 - q) + i, :] for i in range(3)] for q in range(2)]
        EXPERT_W = (("wg", "exp_w_gate", "hg", KD), ("wu", "exp_w_up", "hu", KD), ("wd", "exp_w_down", "y", FB))

        def load_expert(sp, l, e, q, n, ready):
            nm, wn, _, k = EXPERT_W[n]
            src = A[wn][l][bass.ds(e, 1)].rearrange("a (p k) n -> p a (k n)", p=P)
            sp.dma_start(wslot[q][n].unsqueeze(1), src).then_inc(ready[f"{nm}{q}"], 16)

        def expert_semaphores(l):
            return {n: sem(f"x{l}_{n}") for n in ("wg0", "wg1", "wu0", "wu1", "wd0", "wd1")}

        def experts(l, ready, after):
            s = {n: sem(f"x{l}_{n}") for n in ("g2", "idx", "sidx", "gcol", "gat0", "gat1", "go", "xT", "xC", "hg", "hu", "hs", "hid", "hT", "hC", "y", "yw", "ye", "sc")}
            s.update(ready)
            cs = Carve(projf)
            g2 = cs(D)
            xg = cs(2, D)
            ye = cs(2, D)
            sg = cs(FF)
            hid = cs(FF)
            hidT = cs(FB, CAP)
            xgT = cs(2, KD, CAP)
            gc = cs(2)
            ic = sb(f"ic{l}", [CAP, 4], I32)

            with nc.Block(f"experts_{l}") as block:
                def pairs(eng, body):
                    body(0)
                    with eng.Fori(1, NE // 2 - 1) as i:
                        body(i)
                    body(NE // 2 - 1)

                @block.sync
                def _(sp):
                    for cond, lo, hi in ((0, 0, CAPS), (1, CAPS, CAP)):
                        sp.dma_start(g2[lo:hi, :], mod_rows[l, cond:cond + 1, 5 * D:6 * D].to_broadcast([hi - lo, D])).then_inc(s["g2"], 16)

                    def body(i):
                        for q in range(2):
                            e = 2 * i + q
                            first = isinstance(i, int) and i == 0
                            for n in range(3):
                                if not first:
                                    sp.wait_ge(s[EXPERT_W[n][2]], 2 * i + q - 1)
                                if not (first and q == 0):
                                    load_expert(sp, l, e, q, n, s)
                    pairs(sp, body)
                    after(sp, s)

                @block.gpsimd
                def _(pool):
                    def gather(e, q, first):
                        if not first:
                            pool.wait_ge(s["xT"], e - 1)
                        pool.tensor_copy(ic[:, q:q + 1], idx[:, bass.ds(e, 1)]).then_inc(s["idx"], 1)
                        pool.wait_ge(s["idx"], e + 1)
                        pool.sem_inc(s["go"], 1)
                        pool.indirect_dma_start(xg[0:CAP, q, :], None, xm_rows, bass.IndirectOffsetOnAxis(ap=ic[:, q:q + 1], axis=0)).then_inc(s[f"gat{q}"], 16)

                    def scatter(e, q, first):
                        if not first:
                            pool.wait_ge(s["sc"], 16 * e)
                        pool.tensor_copy(ic[:, 2 + q:3 + q], idx[:, bass.ds(e, 1)]).then_inc(s["sidx"], 1)
                        pool.wait_ge(s["sidx"], e + 1)
                        pool.wait_ge(s["ye"], e + 1)
                        pool.sem_inc(s["go"], 1)
                        pool.indirect_dma_start(x_rows, bass.IndirectOffsetOnAxis(ap=ic[:, 2 + q:3 + q], axis=0), ye[0:CAP, q, :], None,
                                                compute_op=ALU.add).then_inc(s["sc"], 16)

                    gather(0, 0, True)
                    gather(1, 1, True)

                    def body(i):
                        for q in range(2):
                            e = 2 * i + q
                            if not (isinstance(i, int) and i == NE // 2 - 1):
                                gather(e + 2, q, False)
                            if not (isinstance(i, int) and e == 0):
                                scatter(e - 1, 1 - q, isinstance(i, int) and e == 1)
                    pairs(pool, body)
                    scatter(NE - 1, 1, False)
                    pool.wait_ge(s["sc"], 16 * NE)

                @block.tensor
                def _(pe):
                    def turn(e, q, n, first):
                        pe.wait_ge(s[f"gat{q}"], 16 * n)
                        if not first:
                            pe.wait_ge(s["xC"], 2 * e)
                        for h in range(2):
                            for k in range(4):
                                mm = pe.transpose(bank(h)[:, k * CAP:(k + 1) * CAP], xg[0:CAP, q, 4 * h + k::KD], ident[0:CAP, 0:CAP])
                        mm.then_inc(s["xT"], 1)

                    def into_hidden(e, q, i, n, nm, done, free):
                        pe.wait_ge(s[f"{nm}{q}"], 16 * (i + 1))
                        if free is not None:
                            pe.wait_ge(s[free], e)
                        w = wslot[q][n].rearrange("p (k n) -> p k n", k=KD)
                        for k in range(KD):
                            mm = pe.matmul(bank(2 + n)[0:CAP, :], xgT[:, q, k, :], w[:, k, :], start=(k == 0), stop=(k == KD - 1))
                        mm.then_inc(s[done], 1)

                    def turn_hidden(e, first):
                        pe.wait_ge(s["hid"], e + 1)
                        if not first:
                            pe.wait_ge(s["hC"], e)
                        for f in range(FB):
                            mm = pe.transpose(bank(6)[:, f * CAP:(f + 1) * CAP], hid[0:CAP, f::FB], ident[0:CAP, 0:CAP])
                        mm.then_inc(s["hT"], 1)

                    def down(e, q, loads, first):
                        pe.wait_ge(s["hC"], e + 1)
                        pe.wait_ge(s[f"wd{q}"], 16 * loads)
                        if not first:
                            pe.wait_ge(s["yw"], 2 * e)
                        w = wslot[q][2].rearrange("p (k n) -> p k n", k=FB)
                        for h in range(2):
                            for f in range(FB):
                                mm = pe.matmul(bank(4 + h)[0:CAP, :], hidT[:, f, :], w[:, f, h * 512:(h + 1) * 512], start=(f == 0), stop=(f == FB - 1))
                        mm.then_inc(s["y"], 1)

                    turn(0, 0, 1, True)

                    def body(i):
                        static = isinstance(i, int)
                        for q in range(2):
                            e = 2 * i + q
                            first = static and e == 0
                            second = static and e == 1
                            pe.wait_ge(s["xC"], 2 * e + 2)
                            into_hidden(e, q, i, 0, "wg", "hg", None if first else "hs")
                            if not first:
                                turn_hidden(e - 1, second)
                            into_hidden(e, q, i, 1, "wu", "hu", None if first else "hid")
                            if not first:
                                down(e - 1, 1 - q, i + q, second)
                            if not (static and e == NE - 1):
                                turn(e + 1, 1 - q, i + 1 + q, False)
                    pairs(pe, body)
                    turn_hidden(NE - 1, False)
                    down(NE - 1, 1, NE // 2, False)

                @block.scalar
                def _(act):
                    def turn_copy(e, q, first):
                        act.wait_ge(s["xT"], e + 1)
                        if not first:
                            act.wait_ge(s["hu"], e - 1)
                        for h in range(2):
                            act.activation(xgT[:, q, 4 * h:4 * h + 4, :], bank(h)[:, 0:4 * CAP].rearrange("p (k c) -> p k c", k=4), ACT.Copy).then_inc(s["xC"], 1)

                    def hidden_copy(e, first):
                        act.wait_ge(s["hT"], e + 1)
                        if not first:
                            act.wait_ge(s["y"], e)
                        act.activation(hidT, bank(6)[:, 0:FB * CAP].rearrange("p (k c) -> p k c", k=FB), ACT.Copy).then_inc(s["hC"], 1)

                    turn_copy(0, 0, True)

                    def body(i):
                        static = isinstance(i, int)
                        for q in range(2):
                            e = 2 * i + q
                            first = static and e == 0
                            act.wait_ge(s["hg"], e + 1)
                            if not first:
                                act.wait_ge(s["hid"], e)
                            act.activation(sg[0:CAP, :], bank(2)[0:CAP, :], ACT.Silu).then_inc(s["hs"], 1)
                            if not first:
                                hidden_copy(e - 1, static and e == 1)
                            if not (static and e == NE - 1):
                                turn_copy(e + 1, 1 - q, first)
                    pairs(act, body)
                    hidden_copy(NE - 1, False)

                @block.vector
                def _(dve):
                    dve.wait_ge(s["g2"], 32)

                    def weigh(e, q, first, first2):
                        if not first2:
                            dve.wait_ge(s["ye"], e - 1)
                        dve.tensor_copy(gc[0:CAP, q:q + 1], gate[:, bass.ds(e, 1)]).then_inc(s["gcol"], 1)
                        dve.wait_ge(s["gcol"], e + 1)
                        dve.wait_ge(s["y"], e + 1)
                        if not first2:
                            dve.wait_ge(s["sc"], 16 * (e - 1))
                        for h in range(2):
                            dve.scalar_tensor_tensor(out=ye[0:CAP, q, h * 512:(h + 1) * 512], in0=bank(4 + h)[0:CAP, :], scalar=gc[0:CAP, q:q + 1],
                                                     in1=g2[0:CAP, h * 512:(h + 1) * 512], op0=ALU.mult, op1=ALU.mult).then_inc(s["yw"], 1)
                        dve.wait_ge(s["yw"], 2 * e + 2)
                        dve.sem_inc(s["ye"], 1)

                    def body(i):
                        static = isinstance(i, int)
                        for q in range(2):
                            e = 2 * i + q
                            first = static and e == 0
                            dve.wait_ge(s["hs"], e + 1)
                            dve.wait_ge(s["hu"], e + 1)
                            if not first:
                                dve.wait_ge(s["hT"], e)
                            dve.tensor_tensor(hid[0:CAP, :], sg[0:CAP, :], bank(3)[0:CAP, :], ALU.mult).then_inc(s["hid"], 1)
                            if not first:
                                weigh(e - 1, 1 - q, static and e == 1, static and e <= 2)
                    pairs(dve, body)
                    weigh(NE - 1, 1, False, False)

        pc = Carve(projf)
        po = pc(TILES, ODD_TOK)
        XL = NT + 6
        XS, XPR = 2, NS + 5
        xp = pc(4, XL)
        xg = pc(4, NT)
        rgbd = pc(16, P)
        ODD_CUTS = [(0, 512), (512, ODD_TOK - 512), (ODD_TOK, 512), (ODD_TOK + 512, 512)]
        ODD_SLOTS = [3, 4, 5, 0]
        odd_w = [(ring[:, ODD_SLOTS[i], 0:KD * n].rearrange("p (k n) -> p k n", k=KD),
                  A["od_w_in"][0, :, c:c + n].rearrange("(k p) n -> p k n", p=P)) for i, (c, n) in enumerate(ODD_CUTS)]

        def odd_units():
            units = token_units(ODD_CUTS[:2], odd_w, lambda t, c, n: po[:, t, c:c + n])
            for f in range(8):
                w = odd_w[2 + f // 4][0]
                for lo, n in ((0, NS), (NS, NP)):
                    at = XS if lo == 0 else XPR
                    dst = xp[:, f, at:at + n] if f < 4 else xg[:, f - 4, lo:lo + n]
                    units.append(([w[:, k, (f % 4) * P:(f % 4 + 1) * P] for k in range(KD)], [xT[:, k, lo:lo + n] for k in range(KD)],
                                  n, dst, 2 + f // 4, ST if lo == 0 else TILES))
            return units

        def odd_zeros(pool, done):
            for lo, hi in ((0, XS), (XS + NS, XPR), (XPR + NP, XL)):
                pool.memset(xp[:, :, lo:hi], 0.0).then_inc(done, 1)
            pool.memset(rgbd, 0.0).then_inc(done, 1)

        oc = Carve(ringf)
        kT2 = oc(CH, NT + P)
        v2 = oc(TILES + 1, CH * CV)
        ODD_TOP = oc.at
        qT2 = Carve(ringf, ODD_TOP)(CH, NT)

        def prepare_odd():
            s = {n: sem("od_" + n) for n in ("in", "ckc", "sq", "root", "own", "norm", "rotk", "t", "tc", "mm", "mc", "ck", "krc", "kr", "krd",
                                             "qmm", "qc", "rotq", "q2", "qt", "qtc", "out", "vm")}
            cs = Carve(ringf, ODD_TOP)
            cqT, ckvT = cs(3, NT), cs(2, NT + P)
            wuq = cs(3, CH * CQK)
            Q = cs(TILES, CH * CQK)
            wkn, wv = cs(2, CH * CNOPE), cs(2, CH * CV)
            tabs = cs(ST, 2, CROPE)
            nq, nkv = cs(CQL), cs(CKVL)
            ra, rb = cs(ST, CH * CROPE), cs(ST, CH * CROPE)
            ck_rows = rb[:, 0, :]
            kr_rows = ra[:, 0, 0:CROPE]
            junk = rb[:, 1:3, :].rearrange("p a b -> p (a b)")
            ssq, rs = small[:, 0:10], small[:, 16:26]
            krot = small[:, 32:32 + 2 * ST * CROPE].rearrange("p (a t d) -> p a t d", a=2, t=ST)
            LOADS = 16 * 10
            KR0 = CQL + CKVL

            def quarters(x, lead):
                return x.rearrange(f"p {lead} (a u i) -> p {lead} a u i", a=2, u=2)

            with nc.Block("prepare_odd") as block:
                @block.sync
                def _(sp):
                    sp.dma_start(wuq, A["mla_w_uq"][0].rearrange("(k p) n -> p k n", p=P)).then_inc(s["in"], 16)
                    u4 = A["mla_w_ukv"][0].rearrange("(k p) (h u d) -> k u p h d", p=P, u=2, d=CNOPE)
                    for k in range(2):
                        sp.dma_start(wkn[:, k, :].rearrange("p (h d) -> p h d", d=CNOPE), u4[k, 0]).then_inc(s["in"], 16)
                        sp.dma_start(wv[:, k, :].rearrange("p (h d) -> p h d", d=CV), u4[k, 1]).then_inc(s["in"], 16)
                    for dst, src in [(tabs, A["rope_c"]), (nq, A["mla_q_norm"].to_broadcast([P, CQL])), (nkv, A["mla_kv_norm"].to_broadcast([P, CKVL])),
                                     (ck_rows, A["cache_mla_ckv"][0, 0]), (kr_rows, A["cache_mla_krope"][0, 0])]:
                        sp.dma_start(dst, src).then_inc(s["in"], 16)
                    for d in range(2):
                        for kind, nm in enumerate(("rg_wa", "rg_wx")):
                            for r in range(2):
                                b4 = rgbd.rearrange("p (d w f) n -> p d w f n", d=2, w=2)
                                sp.dma_start(b4[r * 64:r * 64 + 64, d, kind, :, r * 64:r * 64 + 64],
                                             A[nm][0, d].rearrange("(f r) a b -> r a f b", r=2)[r]).then_inc(s["out"], 16)
                    sp.wait_ge(s["norm"], TILES)
                    sp.dma_start(O[7][0, 0], po[:, PT, CQL:CQL + CKVL]).then_inc(s["out"], 16)
                    sp.dma_start(O[8][0, 0], po[:, PT, KR0:KR0 + CROPE]).then_inc(s["out"], 16)
                    sp.wait_ge(s["out"], 16 * 10)

                @block.scalar
                def _(act):
                    own = Steps(act, s["sq"])
                    act.wait_ge(s["t"], 1)
                    for t in range(TILES):
                        own.link(act.activation(junk[:, 0:CQL], po[:, t, 0:CQL], ACT.Square, scale=CQL ** -0.5, accum_out=ssq[:, 2 * t:2 * t + 1]))
                        own.link(act.activation(junk[:, 0:CKVL], po[:, t, CQL:CQL + CKVL], ACT.Square, scale=CKVL ** -0.5, accum_out=ssq[:, 2 * t + 1:2 * t + 2]))
                    act.activation(rs, ssq, ACT.Sqrt, bias=EPS).then_inc(s["root"], 1)
                    act.activation(ckvT[:, :, 0:P], bank(0, 256).rearrange("p (k c) -> p k c", k=2), ACT.Copy).then_inc(s["tc"], 1)
                    act.activation(kT2[64:96, 0, 0:P], psum[0:32, 0, 256:256 + P], ACT.Copy).then_inc(s["krc"], 1)
                    for t in range(TILES):
                        b = 1 + t % 2
                        act.wait_ge(s["t"], t + 2)
                        act.activation(cqT[:, :, t * P:(t + 1) * P], bank(b, 384).rearrange("p (k c) -> p k c", k=3), ACT.Copy).then_inc(s["tc"], 1)
                        act.activation(ckvT[:, :, (t + 1) * P:(t + 2) * P], bank(2 + b, 256).rearrange("p (k c) -> p k c", k=2), ACT.Copy).then_inc(s["tc"], 1)
                        act.activation(kT2[64:96, 0, (t + 1) * P:(t + 2) * P], psum[0:32, 2 + b, 256:256 + P], ACT.Copy).then_inc(s["krc"], 1)
                    for n in range(2 * TILES):
                        act.wait_ge(s["qmm"], n + 1)
                        t, c = n // 2, n % 2
                        act.activation(Q[:, t, c * 384:(c + 1) * 384], bank(5 + n % 2, 384), ACT.Copy).then_inc(s["qc"], 1)
                    for n in range(2 * TILES):
                        act.wait_ge(s["qt"], n + 1)
                        t, c = n // 2, n % 2
                        act.activation(qT2[0:CQK, 4 * c:4 * c + 4, t * P:(t + 1) * P], psum[0:CQK, 5 + n % 2, :].rearrange("p (h c) -> p h c", h=4),
                                       ACT.Copy).then_inc(s["qtc"], 1)

                @block.vector
                def _(dve):
                    own = Steps(dve, s["own"])
                    dve.wait_ge(s["in"], LOADS)
                    dve.wait_ge(s["root"], 1)
                    own.link(dve.reciprocal(rs, rs))
                    kr = po[:, 0:ST, KR0:KR0 + CROPE]
                    own(dve.tensor_tensor(krot[:, 0], kr, tabs[:, :, 0, :], ALU.mult))
                    for u in range(2):
                        own(dve.tensor_tensor(krot[:, 1].rearrange("p t (a u i) -> p t a u i", a=2, u=2)[:, :, :, u, :],
                                              kr.rearrange("p t (a u i) -> p t a u i", a=2, u=2)[:, :, :, 1 - u, :],
                                              tabs[:, :, 1, :].rearrange("p t (a u i) -> p t a u i", a=2, u=2)[:, :, :, u, :], ALU.mult))
                    own.wait()
                    own.link(dve.tensor_tensor(kr, krot[:, 0], krot[:, 1], ALU.add))
                    for t in range(TILES):
                        own(dve.scalar_tensor_tensor(out=po[:, t, 0:CQL], in0=po[:, t, 0:CQL], scalar=rs[:, 2 * t:2 * t + 1], in1=nq, op0=ALU.mult, op1=ALU.mult))
                        own.link(dve.scalar_tensor_tensor(out=po[:, t, CQL:KR0], in0=po[:, t, CQL:KR0], scalar=rs[:, 2 * t + 1:2 * t + 2], in1=nkv, op0=ALU.mult, op1=ALU.mult))
                        dve.sem_inc(s["norm"], 1)
                    for n in range(8):
                        j, c = n // 2, n % 2
                        lo, w = (0, 512) if c == 0 else (512, 256)
                        dve.wait_ge(s["mm"], n + 1)
                        b = 7 if n % 2 else 0
                        own(dve.tensor_copy(kT2[0:64, 2 * j, lo:lo + w], psum[0:64, b, 0:w]))
                        dve.tensor_copy(kT2[0:64, 2 * j + 1, lo:lo + w], psum[64:128, b, 0:w]).then_inc(s["mc"], 1)
                    for n in range(TILES + 1):
                        dve.wait_ge(s["mm"], 8 + n + 1)
                        dve.tensor_copy(v2[:, n, :], bank(7 if n % 2 else 0)).then_inc(s["mc"], 1)
                    for t in range(ST):
                        dve.wait_ge(s["qc"], 2 * t + 2)
                        q3 = Q[:, t, :].rearrange("p (h d) -> p h d", d=CQK)[:, :, CNOPE:CQK]
                        a3 = ra[:, t, :].rearrange("p (h d) -> p h d", d=CROPE)
                        b3 = rb[:, t, :].rearrange("p (h d) -> p h d", d=CROPE)
                        own(dve.tensor_tensor(a3, q3, tabs[:, t, 0:1, :].to_broadcast([P, CH, CROPE]), ALU.mult))
                        sn = tabs[:, t, 1, :].rearrange("p (a u i) -> p a u i", a=2, u=2)
                        for u in range(2):
                            for a in range(2):
                                own(dve.tensor_tensor(quarters(b3, "h")[:, :, a, u, :], quarters(q3, "h")[:, :, a, 1 - u, :],
                                                      sn[:, a, u, :].unsqueeze(1).to_broadcast([P, CH, 8]), ALU.mult))
                        own.wait()
                        dve.tensor_tensor(q3, a3, b3, ALU.add).then_inc(s["q2"], 1)

                @block.gpsimd
                def _(pool):
                    pool.wait_ge(s["krc"], TILES + 1)
                    for h in range(1, CH):
                        pool.tensor_copy(kT2[64:96, h, :], kT2[64:96, 0, :]).then_inc(s["krd"], 1)

                @block.tensor
                def _(pe):
                    pe.wait_ge(s["in"], LOADS)
                    for k in range(2):
                        pe.transpose(bank(0)[:, k * P:(k + 1) * P], ck_rows[:, k * P:(k + 1) * P], ident[:, :])
                    pe.transpose(psum[0:32, 0, 256:256 + P], kr_rows, ident[:, :]).then_inc(s["t"], 1)
                    for t in range(TILES):
                        b = 1 + t % 2
                        pe.wait_ge(s["norm"], t + 1)
                        if t >= 2:
                            pe.wait_ge(s["tc"], 2 * (t - 1) + 1)
                            pe.wait_ge(s["krc"], t)
                        for k in range(3):
                            pe.transpose(bank(b)[:, k * P:(k + 1) * P], po[:, t, k * P:(k + 1) * P], ident[:, :])
                        for k in range(2):
                            pe.transpose(bank(2 + b)[:, k * P:(k + 1) * P], po[:, t, CQL + k * P:CQL + (k + 1) * P], ident[:, :])
                        pe.transpose(psum[0:32, 2 + b, 256:256 + P], po[:, t, KR0:KR0 + CROPE], ident[:, :]).then_inc(s["t"], 1)
                    for n in range(2 * TILES):
                        t, c = n // 2, n % 2
                        pe.wait_ge(s["tc"], 2 * t + 3)
                        if n >= 2:
                            pe.wait_ge(s["qc"], n - 1)
                        for k in range(3):
                            mm = pe.matmul(bank(5 + n % 2, 384), cqT[:, k, t * P:(t + 1) * P], wuq[:, k, c * 384:(c + 1) * 384], start=(k == 0), stop=(k == 2))
                        mm.then_inc(s["qmm"], 1)
                    pe.wait_ge(s["tc"], 2 * TILES + 1)
                    pe.wait_ge(s["krc"], TILES + 1)
                    for n in range(8 + TILES + 1):
                        b = 7 if n % 2 else 0
                        if n >= 2:
                            pe.wait_ge(s["mc"], n - 1)
                        for k in range(2):
                            if n < 8:
                                j, c = n // 2, n % 2
                                lo, w = (0, 512) if c == 0 else (512, 256)
                                mm = pe.matmul(bank(b, w), wkn[:, k, j * P:(j + 1) * P], ckvT[:, k, lo:lo + w], start=(k == 0), stop=(k == 1))
                            else:
                                mm = pe.matmul(bank(b), ckvT[:, k, (n - 8) * P:(n - 7) * P], wv[:, k, :], start=(k == 0), stop=(k == 1))
                        mm.then_inc(s["mm"], 1)
                    for n in range(2 * TILES):
                        t, c = n // 2, n % 2
                        if t < ST:
                            pe.wait_ge(s["q2"], t + 1)
                        pe.wait_ge(s["qc"], 2 * TILES)
                        if n >= 2:
                            pe.wait_ge(s["qtc"], n - 1)
                        for h in range(4):
                            mm = pe.transpose(psum[0:CQK, 5 + n % 2, h * P:(h + 1) * P], Q[:, t, (4 * c + h) * CQK:(4 * c + h + 1) * CQK], ident[:, :])
                        mm.then_inc(s["qt"], 1)

        def recurrence(prefetch):
            s = {n: sem("rg_" + n) for n in ("in", "t", "prm", "ab", "act", "own", "mm", "sg", "ex", "q", "sqrt", "b", "h", "y", "out", "gelu", "conv", "pool")}
            cs = Carve(ringf, 2 * 4096)
            CW = XPR + NP - XS
            CP = XPR - XS
            xc = Carve(projf)(4, CW)
            R, I = cs(2, 4, CW), cs(2, 4, CW)
            th = cs(2, 4, CW)
            tq = Carve(xT[:, 4:6, :].rearrange("p a b -> p (a b)"))(1, CW)
            prow = small[0:52, 0:128]
            prm = small[:, 128:180]
            sp_ = small[:, 192:200]
            e_, z_, z2, p_ = (small[:, 208 + 8 * i:216 + 8 * i] for i in range(4))
            ROWS = [("rg_conv_w", 16), ("rg_conv_b", 4), ("rg_ba", 8), ("rg_bx", 8), ("rg_lambda", 8), ("state_rglru_h", 8)]
            a_of = R
            at = {}
            n = 0
            for nm, c in ROWS:
                at[nm] = n
                n += c

            def prmcol(nm, i):
                return prm[:, at[nm] + i:at[nm] + i + 1]

            spans = ((0, 0, NS), (CP, NS, NP))
            units = [(d, kind, f) for d in range(2) for kind in range(2) for f in range(4)]
            with nc.Block("recurrence") as block:
                @block.sync
                def _(sp):
                    for nm, c in ROWS:
                        a = A[nm]
                        names = {3: "a b (f p) -> (a b f) p", 2: "a (f p) -> (a f) p", 4: "a b c (f p) -> (a b c f) p"}[len(a.shape)]
                        sp.dma_start(prow[at[nm]:at[nm] + c, :], a.rearrange(names, p=P)).then_inc(s["in"], 16)
                    prefetch(sp)
                    sp.wait_ge(s["h"], 16)
                    for d in range(2):
                        e = CP + NP - 1 if d == 0 else CP
                        with nc.allow_non_contiguous_dma(reason="words"):
                            sp.dma_start(O[9][0, 0, d].rearrange("(f p) -> p f", p=P), th[:, d, :, e]).then_inc(s["out"], 16)
                    sp.wait_ge(s["out"], 32)

                @block.tensor
                def _(pe):
                    pe.wait_ge(s["in"], 16 * 6)
                    pe.transpose(bank(0)[:, 0:52], prow, ident[0:52, 0:52]).then_inc(s["t"], 1)
                    pe.wait_ge(s["prm"], 1)
                    for u, (d, kind, f) in enumerate(units):
                        pe.wait_ge(s["conv"], f + 1)
                        if u >= 4:
                            pe.wait_ge(s["sg"], u - 3)
                        b = 2 * (u % 4)
                        for i, (pl, _, w) in enumerate(spans):
                            mm = pe.matmul(bank(b + i, w), rgbd[:, (d * 2 + kind) * 4 + f, :], xc[:, f, pl:pl + w], start=True, stop=True)
                        mm.then_inc(s["mm"], 1)

                @block.scalar
                def _(act):
                    own = Steps(act, s["act"])
                    act.wait_ge(s["prm"], 1)
                    lam = prm[:, at["rg_lambda"]:at["rg_lambda"] + 8]
                    own.link(act.activation(e_, lam, ACT.Abs))
                    act.activation(e_, e_, ACT.Exp, scale=-1.0).then_inc(s["ab"], 1)
                    for u, (d, kind, f) in enumerate(units):
                        act.wait_ge(s["mm"], u + 1)
                        b = 2 * (u % 4)
                        dst = (R, I)[kind]
                        bias = prmcol(("rg_ba", "rg_bx")[kind], 4 * d + f)
                        own(act.activation(dst[:, d, f, 0:NS], bank(b), ACT.Sigmoid, bias=bias))
                        act.activation(dst[:, d, f, CP:CW], bank(b + 1, NP), ACT.Sigmoid, bias=bias).then_inc(s["sg"], 1)
                    act.wait_ge(s["q"], 1)
                    act.wait_ge(s["sg"], 16)
                    act.wait_ge(s["pool"], 2)
                    own.wait()
                    for d in range(2):
                        for f in range(4):
                            sc = sp_[:, 4 * d + f:4 * d + f + 1]
                            own.link(act.activation(th[:, d, f, :], R[:, d, f, :], ACT.Tanh, scale=sc))
                            act.activation(R[:, d, f, :], R[:, d, f, :], ACT.Exp, scale=sc).then_inc(s["ex"], 1)
                    for n in range(8):
                        act.wait_ge(s["b"], n + 1)
                        act.activation(th[:, n // 4, n % 4, :], th[:, n // 4, n % 4, :], ACT.Sqrt, scale=-1.0).then_inc(s["sqrt"], 1)
                    act.activation(xg, xg, ACT.Gelu_apprx_tanh).then_inc(s["gelu"], 1)

                @block.gpsimd
                def _(pool):
                    pool.memset(R[:, :, :, NS:CP], 0.0).then_inc(s["pool"], 1)
                    pool.memset(I[:, :, :, NS:CP], 0.0).then_inc(s["pool"], 1)
                    pool.wait_ge(s["pool"], 2)
                    for n in range(8):
                        d, f = n // 4, n % 4
                        pool.wait_ge(s["sg"], 8 * d + 4 + f + 1)
                        pool.tensor_tensor(I[:, d, f, :], I[:, d, f, :], xc[:, f, :], ALU.mult).then_inc(s["y"], 1)

                @block.vector
                def _(dve):
                    own = Steps(dve, s["own"])
                    dve.wait_ge(s["t"], 1)
                    dve.tensor_copy(prm, bank(0)[:, 0:52]).then_inc(s["prm"], 1)
                    dve.wait_ge(s["prm"], 1)
                    for f in range(4):
                        own.link(dve.tensor_scalar(xc[:, f, :], xp[:, f, 0:CW], prmcol("rg_conv_w", f), prmcol("rg_conv_b", f), ALU.mult, ALU.add))
                        for w in range(1, 4):
                            own.link(dve.scalar_tensor_tensor(out=xc[:, f, :], in0=xp[:, f, w:w + CW], scalar=prmcol("rg_conv_w", 4 * w + f),
                                                              in1=xc[:, f, :], op0=ALU.mult, op1=ALU.add))
                        dve.sem_inc(s["conv"], 1)
                    dve.wait_ge(s["ab"], 1)
                    own.link(dve.tensor_scalar(z_, e_, 2.0, None, ALU.add))
                    own.link(dve.reciprocal(z_, z_))
                    own.link(dve.tensor_tensor(z_, z_, e_, ALU.mult))
                    own.link(dve.tensor_tensor(z2, z_, z_, ALU.mult))
                    own.link(dve.tensor_scalar(p_, z2, 1.0 / 17, None, ALU.mult))
                    for k in range(15, 1, -2):
                        own.link(dve.scalar_tensor_tensor(out=p_, in0=p_, scalar=1.0 / k, in1=z2, op0=ALU.add, op1=ALU.mult))
                    own.link(dve.scalar_tensor_tensor(out=p_, in0=p_, scalar=1.0, in1=z_, op0=ALU.add, op1=ALU.mult))
                    own.link(dve.tensor_scalar(z2, prm[:, at["rg_lambda"]:at["rg_lambda"] + 8], -1.0, 0.0, ALU.mult, ALU.max))
                    own.link(dve.scalar_tensor_tensor(out=p_, in0=p_, scalar=2.0, in1=z2, op0=ALU.mult, op1=ALU.add))
                    dve.tensor_scalar(sp_, p_, -8.0, None, ALU.mult).then_inc(s["q"], 1)
                    for n in range(8):
                        d, f = n // 4, n % 4
                        dve.wait_ge(s["ex"], n + 1)
                        if n:
                            dve.wait_ge(s["b"], n)
                        own.link(dve.tensor_tensor(tq[:, 0, :], R[:, d, f, :], R[:, d, f, :], ALU.mult))
                        dve.scalar_tensor_tensor(out=th[:, d, f, :], in0=tq[:, 0, :], scalar=1.0, in1=th[:, d, f, :], op0=ALU.add, op1=ALU.mult).then_inc(s["b"], 1)
                    for n in range(8):
                        d, f = n // 4, n % 4
                        dve.wait_ge(s["sqrt"], n + 1)
                        dve.wait_ge(s["y"], n + 1)
                        own.link(dve.tensor_tensor(I[:, d, f, :], I[:, d, f, :], th[:, d, f, :], ALU.mult))
                        for i, (pl, _, w) in enumerate(spans):
                            def run(x):
                                v = x[:, d, f, pl:pl + w]
                                return v if d == 0 else v[:, ::-1]
                            init = prmcol("state_rglru_h", 4 * d + f) if i == 0 else 0.0
                            dve.tensor_tensor_scan(run(th), run(R), run(I), init, ALU.mult, ALU.add).then_inc(s["h"], 1)
                    dve.wait_ge(s["h"], 16)
                    dve.wait_ge(s["gelu"], 1)
                    for f in range(4):
                        for pl, lo, w in spans:
                            own.link(dve.tensor_tensor(xc[:, f, pl:pl + w], th[:, 0, f, pl:pl + w], th[:, 1, f, pl:pl + w], ALU.add))
                            own(dve.tensor_tensor(xT[:, 4 + f, lo:lo + w], xg[:, f, lo:lo + w], xc[:, f, pl:pl + w], ALU.mult))

        def final_norm():
            s = {n: sem("f_" + n) for n in ("w", "sq", "root", "own", "y", "out")}
            s_x = [sem(f"f_x{t}") for t in range(TILES)]
            cs = Carve(projf)
            nw, junk = cs(D), cs(D)
            ssq, rstd = small[:, 0:TILES], small[:, 8:8 + TILES]
            with nc.Block("final_norm") as block:
                @block.sync
                def _(sp):
                    for t in range(TILES):
                        sp.dma_start(xr[:, t, :], x_rows[t * P:(t + 1) * P, :]).then_inc(s_x[t], 16)
                    sp.dma_start(nw, A["final_norm_w"].rearrange("(a n) -> a n", a=1).to_broadcast([P, D])).then_inc(s["w"], 16)
                    for t in range(TILES):
                        sp.wait_ge(s["y"], t + 1)
                        dst = O[1][0, t * P:(t + 1) * P, :] if t < ST else O[0][0]
                        sp.dma_start(dst, xr[:, t, :]).then_inc(s["out"], 16)
                    sp.wait_ge(s["out"], 16 * TILES)

                @block.scalar
                def _(act):
                    for t in range(TILES):
                        act.wait_ge(s_x[t], 16)
                        act.activation(junk, xr[:, t, :], ACT.Square, accum_out=ssq[:, t:t + 1]).then_inc(s["sq"], 1)
                        act.wait_ge(s["sq"], t + 1)
                    act.activation(rstd, ssq, ACT.Sqrt, scale=1.0 / D, bias=EPS).then_inc(s["root"], 1)

                @block.vector
                def _(dve):
                    own = Steps(dve, s["own"])
                    dve.wait_ge(s["root"], 1)
                    own.link(dve.reciprocal(rstd, rstd))
                    dve.wait_ge(s["w"], 16)
                    for t in range(TILES):
                        dve.scalar_tensor_tensor(out=xr[:, t, :], in0=xr[:, t, :], scalar=rstd[:, t:t + 1], in1=nw, op0=ALU.mult, op1=ALU.mult).then_inc(s["y"], 1)

        x_in = [sem(f"x_in{t}") for t in range(TILES)]
        start()
        project(0, x_in, even_w, [sem(f"w_in{i}") for i in range(len(even_w))],
                token_units(W_IN_CUTS, even_w, lambda t, c, n: proj[:, t, c:c + n]),
                [(c, k) for c in range(1, len(CHUNKS)) for k in range(KD)], lambda pool, done: None)
        mn = prepare_even()
        mlstm(mn)
        mix_even()

        def even_keys(h, t):
            return kT[:, 0:NT] if t < ST else kT[:, NT:NT + P]

        def even_values(h, t, j):
            g = h // 4
            if t < ST and j == 0:
                return vctx[:, g * 64:g * 64 + 64]
            return proj[:, (j - 1) if t < ST else PT, C_VB + g * 64:C_VB + g * 64 + 64]

        early = {n: sem("e0_" + n) for n in ("w", "gm")}
        tmp = Carve(ringf, ML_AT)
        slots = [proj[:, :, 0:512], proj[:, :, C_QA:C_QA + 512], tmp(TILES, NS), tmp(TILES, NS)]
        attention("gqa", BH, BD ** -0.5, lambda h, t: qT[:, h // 4, h % 4, t * P:(t + 1) * P],
                  even_keys, even_values, slots, tmp, extra={"sync": out_loads(0, A["ev_w_out"][0], early)})
        ready = expert_semaphores(0)
        out_and_route(0, early, lambda sp: [load_expert(sp, 0, 0, 0, n, ready) for n in range(3)])
        experts(0, ready, lambda sp, s: None)
        clear_semaphores()
        x_in = [sem(f"x1_in{t}") for t in range(TILES)]
        project(1, x_in, odd_w, [sem(f"w_odd{i}") for i in range(len(odd_w))], odd_units(), [], odd_zeros)
        prepare_odd()
        tmp = Carve(ringf, ODD_TOP + CH * NT)
        slots = [projf[:, 0:TILES * NS].rearrange("p (j n) -> p j n", j=TILES), tmp(TILES, NS), tmp(TILES, NS), tmp(TILES, NS)]
        attention("mla", CH, CQK ** -0.5, lambda h, t: qT2[0:CQK, h, t * P:(t + 1) * P],
                  lambda h, t: kT2[0:CQK, h, 0:NT] if t < ST else kT2[0:CQK, h, NT:NT + P],
                  lambda h, t, j: v2[:, j if t < ST else TILES, h * CV:(h + 1) * CV], slots, tmp)
        early = {n: sem("e1_" + n) for n in ("w", "gm")}
        recurrence(out_loads(1, A["od_w_out"][0], early))
        ready = expert_semaphores(1)
        out_and_route(1, early, lambda sp: [load_expert(sp, 1, 0, 0, n, ready) for n in range(3)])
        experts(1, ready, lambda sp, s: None)
        final_norm()


def tables():
    import numpy as np
    def rope(half):
        inv = (np.float32(10000.0) ** (-np.arange(half, dtype=np.float32) / np.float32(half))).astype(np.float32)
        t = np.arange(NS)
        pos = [(t // 64).astype(np.float32), (t % 64).astype(np.float32)]
        out = np.zeros((NS, 2, 2, 2, half), np.float32)
        for a in range(2):
            ang = pos[a][:, None] * inv[None, :]
            out[:, 0, a, :, :] = np.cos(ang)[:, None, :]
            out[:, 1, a, 0, :] = -np.sin(ang)
            out[:, 1, a, 1, :] = np.sin(ang)
        return np.ascontiguousarray(out.reshape(ST, P, 2, 4 * half).transpose(1, 0, 2, 3))
    s_, t_ = np.arange(P)[:, None], np.arange(P)[None, :]
    masks = np.stack([np.where(s_ <= t_, 0.0, -1e30), np.where(s_ >= t_, 0.0, -1e30)], axis=1).astype(np.float32)
    sel = np.zeros((4, 4, P), np.float32)
    selpair = np.zeros((4, 2, P), np.float32)
    for h in range(4):
        sel[h, h] = 1
        selpair[h, h // 2, (h % 2) * 64:(h % 2) * 64 + 64] = 1
    rst = np.tile((np.arange(NT) % P != 0).astype(np.float32), (4, 1))
    return {"ident": np.eye(P, dtype=np.float32), "rope_b": rope(16), "rope_c": rope(8), "masks": masks, "sel": sel,
            "selpair": selpair, "rst": rst}


OUTS = [(1, NP, D), (1, NS, D), (1, 1, 2, AH, AQ, AV), (1, 1, 2, AH, AQ), (1, 1, 2, AH), (1, 1, NP, BKV, BD), (1, 1, NP, BKV, BD),
        (1, 1, NP, CKVL), (1, 1, NP, CROPE), (1, 1, 2, DR)]


def kernel(**inputs):
    import numpy as np
    import concourse.bacc as bacc
    from concourse.bass_utils import run_bass_kernel_spmd

    nc = bacc.Bacc("TRN2", target_bir_lowering=False, num_devices=1)
    arrays, A = {}, {}
    for name, a in [*inputs.items(), *tables().items()]:
        a = np.ascontiguousarray(a)
        arrays[f"in_{name}_dram"] = a
        A[name] = nc.dram_tensor(f"in_{name}_dram", a.shape, mybir.dt.from_np(a.dtype), kind="ExternalInput").ap()
    O = [nc.dram_tensor(f"out_{i}_dram", shape, F32, kind="ExternalOutput").ap() for i, shape in enumerate(OUTS)]
    build(nc, A, O)
    r = run_bass_kernel_spmd(nc, [arrays], core_ids=[0])
    return tuple(r.results[0][f"out_{i}_dram"] for i in range(len(OUTS)))
```
